# Optimizing a Trainium2 kernel written in Bass

```python
import math
import jax, jax.numpy as jnp
from jax import lax
import numpy as np

D_MODEL = 1024
BATCH = 1
SEQ = 512
DEPTH = 2

MEM_LEN = 256
EPS = 1e-6
POS_OFFSET_MAX = 1024

N_GROUPS_MIX = 4
GROUP_W = 256
D_MIX = N_GROUPS_MIX * GROUP_W

MLA_HEADS = 4
MLA_Q_RANK = 256
MLA_KV_RANK = 128
MLA_NOPE = 64
MLA_ROPE = 32
MLA_QK_DIM = MLA_NOPE + MLA_ROPE
MLA_V = GROUP_W // MLA_HEADS
ROPE_THETA = 10000.0
Q_BLOCK = 128

POOL_WINDOWS = (2, 4, 8, 16)
POOL_GROUP = GROUP_W // len(POOL_WINDOWS)

SWA_HEADS = 4
SWA_KV_HEADS = 2
SWA_HEAD_DIM = GROUP_W // SWA_HEADS
SWA_WINDOW = 128

CONV_W = 3
CONV_CH = GROUP_W

A_COLS = MLA_Q_RANK + MLA_KV_RANK + MLA_ROPE
B_COLS = GROUP_W
C_COLS = (SWA_HEADS + 2 * SWA_KV_HEADS) * SWA_HEAD_DIM
D_COLS = 3 * CONV_CH
IN_COLS = A_COLS + B_COLS + C_COLS + D_COLS

XA_HEADS = 4
XA_HEAD_DIM = 64

N_EXPERT_GROUPS = 4
EXPERTS_PER_GROUP = 8
N_EXPERTS = N_EXPERT_GROUPS * EXPERTS_PER_GROUP
TOP_K = 2
D_EXPERT = 256
MOE_BLOCK = 256

kernel_name = "hybrid_parallel_heads_mla_pool_swa_conv_hmoe"

def rms_norm(x, gain):
    xf = x.astype(jnp.float32)
    y = xf * lax.rsqrt(jnp.mean(xf * xf, axis=-1, keepdims=True) + EPS)
    return (y * gain.astype(jnp.float32)).astype(x.dtype)

def rotary(x, positions):
    half = x.shape[-1] // 2
    inv_freq = ROPE_THETA ** (-jnp.arange(half, dtype=jnp.float32) / half)
    ang = positions.astype(jnp.float32)[..., None] * inv_freq
    cos = jnp.cos(ang)[:, :, None, :]
    sin = jnp.sin(ang)[:, :, None, :]
    xf = x.astype(jnp.float32)
    x1, x2 = xf[..., :half], xf[..., half:]
    return jnp.concatenate([x1 * cos - x2 * sin, x2 * cos + x1 * sin], axis=-1).astype(x.dtype)

def causal_attention_qblocks(q, k, v, scale):
    B, S, H, dq = q.shape
    nb = S // Q_BLOCK
    qb = q.reshape(B, nb, Q_BLOCK, H, dq).transpose(1, 0, 2, 3, 4)
    key_pos = jnp.arange(S)

    def one_block(args):
        qi, bi = args
        s = jnp.einsum('bqhd,bkhd->bhqk', qi, k, preferred_element_type=jnp.float32) * scale
        q_pos = bi * Q_BLOCK + jnp.arange(Q_BLOCK)
        mask = key_pos[None, :] <= q_pos[:, None]
        s = jnp.where(mask[None, None], s, -jnp.inf)
        p = jax.nn.softmax(s, axis=-1)
        return jnp.einsum('bhqk,bkhd->bqhd', p.astype(v.dtype), v)

    out = lax.map(one_block, (qb, jnp.arange(nb)))
    return out.transpose(1, 0, 2, 3, 4).reshape(B, S, H, v.shape[-1])

def mla_mixer(u, positions, g_cq, w_uq, g_ckv, w_ukv, g_q, g_k):
    B, S, _ = u.shape
    c_q = u[..., :MLA_Q_RANK]
    c_kv = u[..., MLA_Q_RANK:MLA_Q_RANK + MLA_KV_RANK]
    k_rope = u[..., MLA_Q_RANK + MLA_KV_RANK:]
    q = (rms_norm(c_q, g_cq) @ w_uq).reshape(B, S, MLA_HEADS, MLA_QK_DIM)
    kv = (rms_norm(c_kv, g_ckv) @ w_ukv).reshape(B, S, MLA_HEADS, MLA_NOPE + MLA_V)
    k = jnp.concatenate(
        [kv[..., :MLA_NOPE], jnp.broadcast_to(k_rope[:, :, None, :], (B, S, MLA_HEADS, MLA_ROPE))], axis=-1)
    v = kv[..., MLA_NOPE:]
    q = rms_norm(q, g_q)
    k = rms_norm(k, g_k)
    q = jnp.concatenate([q[..., :MLA_NOPE], rotary(q[..., MLA_NOPE:], positions)], axis=-1)
    k = jnp.concatenate([k[..., :MLA_NOPE], rotary(k[..., MLA_NOPE:], positions)], axis=-1)
    o = causal_attention_qblocks(q, k, v, MLA_QK_DIM ** -0.5)
    return o.reshape(B, S, MLA_HEADS * MLA_V)

def pool_mixer(u, w_pool, pool_scale):
    B, S, C = u.shape
    uf = u.astype(jnp.float32)
    cs = jnp.pad(jnp.cumsum(uf, axis=1), ((0, 0), (1, 0), (0, 0)))
    t = jnp.arange(S)
    outs = []
    for gi, w in enumerate(POOL_WINDOWS):
        lo, hi = gi * POOL_GROUP, (gi + 1) * POOL_GROUP
        csg = cs[..., lo:hi]
        start = jnp.maximum(t + 1 - w, 0)
        win_sum = csg[:, 1:] - csg[:, start]
        count = jnp.minimum(t + 1, w).astype(jnp.float32)
        outs.append(win_sum / count[None, :, None] - uf[..., lo:hi])
    pooled = jnp.concatenate(outs, axis=-1).astype(u.dtype).reshape(B, S, len(POOL_WINDOWS), POOL_GROUP)
    y = jnp.einsum('bsgc,gcd->bsgd', pooled, w_pool).reshape(B, S, C)
    return y * pool_scale

def swa_mixer(u, g_q, g_k, sinks):
    B, S, _ = u.shape
    H, KV, dh, W = SWA_HEADS, SWA_KV_HEADS, SWA_HEAD_DIM, SWA_WINDOW
    G = H // KV
    nb = S // W
    q = rms_norm(u[..., :H * dh].reshape(B, S, KV, G, dh), g_q)
    k = rms_norm(u[..., H * dh:(H + KV) * dh].reshape(B, S, KV, dh), g_k)
    v = u[..., (H + KV) * dh:].reshape(B, S, KV, dh)
    qb = q.reshape(B, nb, W, KV, G, dh)

    def band(z):
        zb = z.reshape(B, nb, W, KV, dh)
        prev = jnp.pad(zb, ((0, 0), (1, 0), (0, 0), (0, 0), (0, 0)))[:, :-1]
        return jnp.concatenate([prev, zb], axis=2)

    kb, vb = band(k), band(v)
    s = jnp.einsum('bnqkgd,bnjkd->bnkgqj', qb, kb, preferred_element_type=jnp.float32) * (dh ** -0.5)
    qi = jnp.arange(W)[:, None]
    kj = jnp.arange(2 * W)[None, :]
    diff = W + qi - kj
    in_win = (diff >= 0) & (diff < W)
    key_ok = (jnp.arange(nb)[:, None] * W + kj - W) >= 0
    mask = in_win[None] & key_ok[:, None, :]
    s = jnp.where(mask[None, :, None, None], s, -jnp.inf)
    sink = jnp.broadcast_to(sinks.reshape(KV, G).astype(jnp.float32)[None, None, :, :, None, None],
                            s.shape[:-1] + (1,))
    p = jax.nn.softmax(jnp.concatenate([s, sink], axis=-1), axis=-1)[..., :2 * W]
    o = jnp.einsum('bnkgqj,bnjkd->bnqkgd', p.astype(vb.dtype), vb)
    return o.reshape(B, S, H * dh)

def conv_mixer(u, conv_w, conv_b):
    b_gate = u[..., :CONV_CH]
    c_gate = u[..., CONV_CH:2 * CONV_CH]
    h = u[..., 2 * CONV_CH:]
    z = c_gate * h
    conv = lax.conv_general_dilated(
        z, conv_w.reshape(CONV_W, 1, CONV_CH), window_strides=(1,), padding=[(CONV_W - 1, 0)],
        dimension_numbers=('NWC', 'WIO', 'NWC'), feature_group_count=CONV_CH)
    return b_gate * (conv + conv_b)

def cross_attention(h, m, w_q, w_kv, g_q, g_k, w_o):
    B, S, _ = h.shape
    M = m.shape[1]
    q = rms_norm((h @ w_q).reshape(B, S, XA_HEADS, XA_HEAD_DIM), g_q)
    kv = (m @ w_kv).reshape(B, M, 2, XA_HEADS, XA_HEAD_DIM)
    k = rms_norm(kv[:, :, 0], g_k)
    v = kv[:, :, 1]
    s = jnp.einsum('bshd,bmhd->bhsm', q, k, preferred_element_type=jnp.float32) * (XA_HEAD_DIM ** -0.5)
    p = jax.nn.softmax(s, axis=-1)
    o = jnp.einsum('bhsm,bmhd->bshd', p.astype(v.dtype), v).reshape(B, S, XA_HEADS * XA_HEAD_DIM)
    return o @ w_o

def hier_moe(h, w_group, b_group, w_expert, b_expert, w_gate, w_up, w_down):
    B, S, D = h.shape
    N = B * S
    t = h.reshape(N, D)
    rows = jnp.arange(N)
    g_logits = (t @ w_group).astype(jnp.float32) + b_group.astype(jnp.float32)
    g_prob = jax.nn.softmax(g_logits, axis=-1)
    g_idx = jnp.argmax(g_logits, axis=-1)
    g_w = g_prob[rows, g_idx]
    e_logits = ((t @ w_expert).astype(jnp.float32) + b_expert.astype(jnp.float32)).reshape(
        N, N_EXPERT_GROUPS, EXPERTS_PER_GROUP)
    e_prob = jax.nn.softmax(e_logits[rows, g_idx], axis=-1)
    top_p, top_i = lax.top_k(e_prob, TOP_K)
    top_p = top_p / jnp.sum(top_p, axis=-1, keepdims=True)
    weights = g_w[:, None] * top_p
    expert_id = g_idx[:, None] * EXPERTS_PER_GROUP + top_i
    A = N * TOP_K
    flat_e = expert_id.reshape(A)
    flat_w = weights.reshape(A)
    flat_tok = jnp.repeat(rows, TOP_K)
    order = jnp.argsort(flat_e)
    se, stok, sw = flat_e[order], flat_tok[order], flat_w[order]
    counts = jnp.bincount(flat_e, length=N_EXPERTS)
    starts = jnp.cumsum(counts) - counts
    padded = ((counts + MOE_BLOCK - 1) // MOE_BLOCK) * MOE_BLOCK
    pends = jnp.cumsum(padded)
    pstarts = pends - padded
    dest = pstarts[se] + (jnp.arange(A) - starts[se])
    P = ((A + N_EXPERTS * (MOE_BLOCK - 1) + MOE_BLOCK - 1) // MOE_BLOCK) * MOE_BLOCK
    n_blocks = P // MOE_BLOCK
    tok_buf = jnp.zeros((P,), jnp.int32).at[dest].set(stok.astype(jnp.int32))
    w_buf = jnp.zeros((P,), jnp.float32).at[dest].set(sw)
    blk_expert = jnp.minimum(
        jnp.searchsorted(pends, jnp.arange(n_blocks) * MOE_BLOCK, side='right'), N_EXPERTS - 1)

    def expert_block(args):
        tok, wt, e = args
        xb = t[tok]
        y = (jax.nn.silu(xb @ w_gate[e]) * (xb @ w_up[e])) @ w_down[e]
        return y * wt[:, None].astype(y.dtype)

    ys = lax.map(expert_block, (tok_buf.reshape(n_blocks, MOE_BLOCK),
                                w_buf.reshape(n_blocks, MOE_BLOCK), blk_expert))
    out = jax.ops.segment_sum(ys.reshape(P, D), tok_buf, num_segments=N)
    return out.reshape(B, S, D)

def setup_inputs(seed: int = 0) -> dict:
    key = jax.random.key(seed)
    ks = iter(jax.random.split(key, 64))
    f32 = jnp.float32
    L = DEPTH

    def nrm(shape, scale):
        return jax.random.normal(next(ks), shape, f32) * scale

    def gain(shape):
        return 1.0 + 0.05 * jax.random.normal(next(ks), shape, f32)

    x = nrm((BATCH, SEQ, D_MODEL), 1.0)
    mem = nrm((BATCH, MEM_LEN, D_MODEL), 1.0)
    positions = jnp.arange(SEQ, dtype=jnp.int32)[None, :] + jax.random.randint(
        next(ks), (BATCH, 1), 0, POS_OFFSET_MAX, dtype=jnp.int32)
    return {
        "x": x,
        "mem": mem,
        "positions": positions,
        "norm_mix": gain((L, D_MODEL)),
        "w_in": nrm((L, D_MODEL, IN_COLS), D_MODEL ** -0.5),
        "mla_g_cq": gain((L, MLA_Q_RANK)),
        "mla_w_uq": nrm((L, MLA_Q_RANK, MLA_HEADS * MLA_QK_DIM), MLA_Q_RANK ** -0.5),
        "mla_g_ckv": gain((L, MLA_KV_RANK)),
        "mla_w_ukv": nrm((L, MLA_KV_RANK, MLA_HEADS * (MLA_NOPE + MLA_V)), MLA_KV_RANK ** -0.5),
        "mla_g_q": gain((L, MLA_QK_DIM)),
        "mla_g_k": gain((L, MLA_QK_DIM)),
        "pool_w": nrm((L, len(POOL_WINDOWS), POOL_GROUP, POOL_GROUP), POOL_GROUP ** -0.5),
        "pool_scale": gain((L, GROUP_W)),
        "swa_g_q": gain((L, SWA_HEAD_DIM)),
        "swa_g_k": gain((L, SWA_HEAD_DIM)),
        "swa_sinks": nrm((L, SWA_HEADS), 0.5),
        "conv_w": nrm((L, CONV_W, CONV_CH), CONV_W ** -0.5),
        "conv_b": nrm((L, CONV_CH), 0.02),
        "mix_out_norm": gain((L, D_MIX)),
        "w_mix_out": nrm((L, D_MIX, D_MODEL), D_MIX ** -0.5),
        "norm_xa": gain((L, D_MODEL)),
        "norm_mem": gain((L, D_MODEL)),
        "xa_w_q": nrm((L, D_MODEL, XA_HEADS * XA_HEAD_DIM), D_MODEL ** -0.5),
        "xa_w_kv": nrm((L, D_MODEL, 2 * XA_HEADS * XA_HEAD_DIM), D_MODEL ** -0.5),
        "xa_g_q": gain((L, XA_HEAD_DIM)),
        "xa_g_k": gain((L, XA_HEAD_DIM)),
        "xa_w_o": nrm((L, XA_HEADS * XA_HEAD_DIM, D_MODEL), (XA_HEADS * XA_HEAD_DIM) ** -0.5),
        "norm_ffn": gain((L, D_MODEL)),
        "w_group": nrm((L, D_MODEL, N_EXPERT_GROUPS), D_MODEL ** -0.5),
        "b_group": nrm((L, N_EXPERT_GROUPS), 0.01),
        "w_expert": nrm((L, D_MODEL, N_EXPERTS), D_MODEL ** -0.5),
        "b_expert": nrm((L, N_EXPERTS), 0.01),
        "w_gate": nrm((L, N_EXPERTS, D_MODEL, D_EXPERT), D_MODEL ** -0.5),
        "w_up": nrm((L, N_EXPERTS, D_MODEL, D_EXPERT), D_MODEL ** -0.5),
        "w_down": nrm((L, N_EXPERTS, D_EXPERT, D_MODEL), D_EXPERT ** -0.5),
    }

def reference(x, mem, positions, norm_mix, w_in, mla_g_cq, mla_w_uq, mla_g_ckv, mla_w_ukv,
              mla_g_q, mla_g_k, pool_w, pool_scale, swa_g_q, swa_g_k, swa_sinks, conv_w, conv_b,
              mix_out_norm, w_mix_out, norm_xa, norm_mem, xa_w_q, xa_w_kv, xa_g_q, xa_g_k, xa_w_o,
              norm_ffn, w_group, b_group, w_expert, b_expert, w_gate, w_up, w_down):
    B, S, _ = x.shape
    for l in range(DEPTH):
        h = rms_norm(x, norm_mix[l])
        u = h @ w_in[l]
        c0 = A_COLS
        c1 = c0 + B_COLS
        c2 = c1 + C_COLS
        y_a = mla_mixer(u[..., :c0], positions, mla_g_cq[l], mla_w_uq[l], mla_g_ckv[l],
                        mla_w_ukv[l], mla_g_q[l], mla_g_k[l])
        y_b = pool_mixer(u[..., c0:c1], pool_w[l], pool_scale[l])
        y_c = swa_mixer(u[..., c1:c2], swa_g_q[l], swa_g_k[l], swa_sinks[l])
        y_d = conv_mixer(u[..., c2:], conv_w[l], conv_b[l])
        y = jnp.stack([y_a, y_b, y_c, y_d], axis=2)
        y = rms_norm(y, mix_out_norm[l].reshape(N_GROUPS_MIX, GROUP_W)).reshape(B, S, D_MIX)
        x = x + y @ w_mix_out[l]
        h = rms_norm(x, norm_xa[l])
        m = rms_norm(mem, norm_mem[l])
        x = x + cross_attention(h, m, xa_w_q[l], xa_w_kv[l], xa_g_q[l], xa_g_k[l], xa_w_o[l])
        h = rms_norm(x, norm_ffn[l])
        x = x + hier_moe(h, w_group[l], b_group[l], w_expert[l], b_expert[l],
                         w_gate[l], w_up[l], w_down[l])
    return x


_drawn_inputs = setup_inputs


def setup_inputs(seed=0):
    import zlib

    import numpy as np

    out = dict(_drawn_inputs(seed))
    spreads = {}
    factors = {'swa_sinks': 4.884,
     'conv_b': 3.258,
     'norm_xa': 3.853,
     'norm_mem': 3.053,
     'xa_g_q': 3.64,
     'xa_g_k': 3.477,
     'b_group': 5.298,
     'b_expert': 4.828}
    for name, (base, spread) in spreads.items():
        noise = np.random.default_rng([zlib.crc32(name.encode()), seed]).standard_normal(out[name].shape)
        drawn = base * np.exp(spread * noise) if base else spread * noise
        out[name] = __import__('jax').numpy.asarray(drawn.astype(out[name].dtype))
    for name, factor in factors.items():
        out[name] = (out[name] * factor).astype(out[name].dtype)
    return out
```

```python
from contextlib import ExitStack

import concourse.bass as bass
from concourse import mybir
import math
import numpy as np

ALU = mybir.AluOpType
ACT = mybir.ActivationFunctionType
F32 = mybir.dt.float32
F32R = mybir.dt.float32r
BF16 = mybir.dt.bfloat16
I32 = mybir.dt.int32
AX_X = mybir.AxisListType.X

P = 128
SEQ = 512
D = 1024
DEPTH = 2
KD = D // P
NT = SEQ // P
MEM = 256
NM = MEM // P
EPS = 1e-6
GW = 256
HD = 64
QK = 96
ROPE = 32
NOPE = 64
QR = 256
KVR = 128
THETA = 10000.0
WINDOWS = (2, 4, 8, 16)
C_B = QR + KVR + ROPE
C_C = C_B + GW
C_D = C_C + 2 * GW
NG = 4
NE = 32
EPG = NE // NG
FF = 256
SLOTS = 64
PAIRS = NE // 2
BATCHES = 4
PPB = PAIRS // BATCHES
BS = 8 * SLOTS
OVF = 16
NEG = -1e30
BIG = 1e30

HALF = P // 2
TWO_PI = 2.0 * math.pi
PI_A = 6.28125
PI_B = float(np.float32(np.round((TWO_PI - PI_A) * 2 ** 21) / 2 ** 21))
PI_C = TWO_PI - PI_A - PI_B
PI_MAX = float(np.nextafter(np.float32(math.pi), np.float32(0)))
ROUND = 12582912.0
RSQRT_MAGIC = float(0x5F3759DF)


class Banks:

    def __init__(self):
        self.full = [0] * 8
        self.free = [0] * 8
        self.job = {}
        self.order = []

    def use(self, name, bank, frees=1):
        self.full[bank] += 1
        self.job[name] = (bank, self.full[bank], self.free[bank])
        self.free[bank] += frees
        self.order.append(name)


def attention_units():
    units = []
    for pair in range(2):
        for t in range(NT):
            units.append(("swa", pair, t, 1 if t == 0 else 2))
    for pair in range(2):
        for t in range(NT):
            units.append(("mla", pair, t, t + 1))
    return units


def cross_units():
    return [("xa", pair, t, NM) for pair in range(2) for t in range(NT)]


def dense_plan(units, cross):
    b = Banks()
    for i in range(NM):
        for h in range(2):
            b.use(("memT", i, h), 2 * i + h)
    for i in range(NM):
        b.use(("kvx", i), 4 + i, frees=2)
    for t in range(NT):
        for h in range(2):
            b.use(("xT", 0, t, h), 2 * (t % 2) + h)
    for t in range(NT):
        b.use(("uC", t, 0), 2 * (t % 2))
        b.use(("uC", t, 1), 2 * (t % 2) + 1)
    for i in range(NM):
        b.use(("kxT", i), 4 + i)
    for m in range(3):
        b.use(("A", m), 6 - m % 2, frees=2)
    b.use(("stA",), 7)
    for m in range(2):
        b.use(("B", m), m)
    for t in range(NT):
        b.use(("qA", t), 4 + 2 * (t % 2))
        b.use(("kvA", t), 5 + 2 * (t % 2))
    for t in range(NT):
        b.use(("cT", t), t, frees=2)
    b.use(("D", 0), 4)
    b.use(("pool", 0), 5, frees=2)
    b.use(("D", 1), 6)
    b.use(("pool", 1), 7, frees=2)
    b.use(("stY", 0), 0)
    b.use(("D", 2), 4)
    b.use(("stY", 1), 1)
    for t in range(2):
        b.use(("qAT", t), 2)
        b.use(("kAT", t), 3)
    b.use(("D", 3), 5)
    b.use(("D", 4), 6)
    for t in range(2, NT):
        b.use(("qAT", t), 2)
        b.use(("kAT", t), 3)
    b.use(("stY", 2), 0)
    b.use(("D", 5), 4)
    b.use(("stY", 3), 1)
    plan_units(b, units)
    for t in range(NT):
        for g in range(NG):
            for h in range(2):
                b.use(("mix", t, g, h), (2 * g + h) % 6)
        if t > 0:
            for h in range(2):
                b.use(("xT", 1, t - 1, h), 6 + h)
    for h in range(2):
        b.use(("xT", 1, NT - 1, h), 6 + h)
    for t in range(NT):
        b.use(("qx", t), t)
    for t in range(NT):
        b.use(("qxT", t), 4 + t % 2)
    plan_units(b, cross)
    for t in range(NT):
        for h in range(2):
            b.use(("wo", t, h), 2 * (t % 2) + h)
        if t > 0:
            for h in range(2):
                b.use(("xT", 2, t - 1, h), 6 + h)
    for h in range(2):
        b.use(("xT", 2, NT - 1, h), 6 + h)
    b.use(("route",), 0)
    b.use(("rank",), 1)
    return b


def plan_units(b, units):
    for n in range(len(units) + 3):
        if n < len(units):
            for a in range(2):
                b.use(("S", units[n], a), 2 * (n % 2) + a)
        if 1 <= n <= len(units):
            for a in range(2):
                b.use(("T", units[n - 1], a), 4 + a)
        if 2 <= n <= len(units) + 1 and units[n - 2][2] == 0:
            kind, pair = units[n - 2][:2]
            b.use(("O", kind, pair), 6 + pair, frees=1 if kind == "xa" else 2)
        if n >= 3 and units[n - 3][2] == NT - 1 and units[n - 3][0] != "xa":
            b.use(("stY", stat_of(units[n - 3])), 4)


def stat_of(unit):
    return {"mla": 4, "swa": 6}[unit[0]] + unit[1]


def moe_plan():
    b = Banks()
    for c in range(KD):
        b.use(("gather", c), c % 4)
    b.use(("wslot",), 5)
    for p in range(PPB):
        b.use(("GT", p), 5)
        b.use(("gu", p), 4, frees=2)
        if p > 0:
            for n in range(4):
                b.use(("comb", p - 1, n), n % 4)
        b.use(("hhT", p), 5)
        if p > 0:
            for n in range(4, 8):
                b.use(("comb", p - 1, n), n % 4)
        for h in range(2):
            b.use(("down", p, h), 6 + h, frees=2)
    for n in range(8):
        b.use(("comb", PPB - 1, n), n % 4)
    return b


LAYER_COUNTS = dict(
    mem_ssq=1, mem_rstd=1, memx_ready=NM, hmT_ready=2 * NM, kx_squared=NM, kx_ready=NM,
    xa_kv_ready=2 * NM, x_ssq=1 + 2 * NT, x_rstd=1 + 2 * NT, xn_ready=3 * NT, hT_ready=6 * NT,
    uC_copied=NT, uC_reduced=NT, qC_ready=NT, cT_ready=2 * NT, sqA_ready=3, cqT_ready=3,
    sA_ready=1, u_ready=2, u_free=2, pooled_ready=2, qkA_copied=NT, qkA_reduced=NT,
    qkA_ready=NT, qkAT_ready=2 * NT, c_ready=2, z_done=2, yD_ready=2, sqY_ready=8, yT_ready=8,
    max_ready=24, p_ready=24, pn_ready=24, x_updated=2 * NT, qx_copied=NT,
    qx_reduced=NT, qx_ready=NT, qxT_ready=NT, oTx_ready=2, xhi_ready=NT, xlo_ready=1,
    M_ready=1, exp_arg=1, exp_done=1, route_ready=1, layer_done=1,
)
MOE_COUNTS = dict(
    G_ready=1, xg_ready=KD, ws_ready=1, Wt_ready=PPB, silu_ready=PPB, hh_ready=PPB,
    hhT_ready=PPB, yhi_ready=2 * PPB, ylo_ready=2 * PPB, gathered=1,
)


def build(nc, a, out):
    units = attention_units()
    cross = cross_units()
    dense = dense_plan(units, cross)
    moe = moe_plan()
    ctx = ExitStack()
    with ctx:
        base = 16512

        def at(name, shape, dt, offset):
            return nc.alloc_sbuf_tensor_at(name, shape, dt, offset=base + offset)

        E_BYTES = 3 * 8192
        wgu = [at(f"wgu{s}", [P, 2, KD, FF], F32, s * E_BYTES) for s in range(4)]
        wdn = [at(f"wdn{s}", [P, 2, D], F32, s * E_BYTES + 16384) for s in range(4)]

        o = 2 * E_BYTES
        qTA = at("qTA", [P, 4, SEQ], F32, o)
        kTA = at("kTA", [P, 4, SEQ], F32, o + 8192)
        qkA = at("qkA", [P, NT, 8, QK], F32, o + 16384)
        sqO = at("sqO", [P, 2, SEQ], F32, o + 16384)
        o += 16384 + 10240
        vA = at("vA", [P, NT, GW], F32, o + 2048)
        qTC = at("qTC", [P, 2, SEQ], F32, o + 6144)
        kTC = at("kTC", [P, SEQ], F32, o + 10240)
        vC = at("vC", [P, NT, P], F32, o + 12288)
        w_uq = at("w_uq", [P, 2, 4 * QK], F32, o + 14336)
        w_ukv = at("w_ukv", [P, 512], F32, o + 17408)
        rope_q = at("rope_q", [P, NT, 2, ROPE], F32, o + 19456)
        rope_k = at("rope_k", [P, NT, 2, ROPE], F32, o + 20480)
        kr = at("kr", [P, NT, ROPE], F32, o + 21504)
        krot = at("krot", [P, NT, ROPE], F32, o + 22016)
        assert o + 22528 <= 4 * E_BYTES

        o = 4 * E_BYTES
        X = at("X", [P, NT, D], F32, o)
        o += 16384
        hT = at("hT", [P, KD, SEQ], F32, o)
        xgT = at("xgT", [P, KD, BS], F32, o)
        o += 16384
        ring0 = at("ring0", [P, KD, 512], F32, o)
        xhi = at("xhi", [P, NT, D], F32R, o)
        o += 16384
        ring1 = at("ring1", [P, KD, 544], F32, o)
        xlo = at("xlo", [P, NT, D], F32R, o)
        M16 = at("M16", [P, NT, NE], BF16, o + 16384)
        o += 17408
        yT = at("yT", [P, 8, SEQ], F32, o)
        memx = at("memx", [P, NM, D], F32, o)
        hmT = at("hmT", [P, KD, MEM], F32, o + 8192)
        qkC = at("qkC", [P, NT, 384], F32, o + 8192)
        qx = at("qx", [P, NT, GW], F32, o)
        sqx = at("sqx", [P, 2, GW], F32, o + 4096)
        qTx = at("qTx", [P, 2, SEQ], F32, o + 6144)
        oTx = at("oTx", [P, 2, SEQ], F32, o + 10240)
        yhi = at("yhi", [P, 2, D], F32R, o)
        ylo = at("ylo", [P, 2, D], F32R, o + 8192)
        Gx = at("Gx", [P, BS], F32, o + 8192)
        o += 16384
        xn = at("xn", [P, 2, D], F32, o)
        cqT = at("cqT", [P, 3, SEQ], F32, o)
        sqC = at("sqC", [P, 2, 384], F32, o + 8192)
        knx = at("knx", [P, NM, GW], F32, o + 11264)
        sqA = at("sqA", [P, 3, SEQ], F32, o + 6144)
        U0 = at("U0", [P, 528], F32, o + 6144)
        U1 = at("U1", [P, 528], F32, o + 8256)
        U2 = at("U2", [P, 528], F32, o + 10368)
        sqY = at("sqY", [P, 640], F32, o + 12480)
        Pr = at("Pr", [P, 2, 2, SEQ], F32, o)
        PT = at("PT", [P, 2, 2, SEQ], F32, o + 8192)
        rope0 = at("rope0", [P, 6, NT, 16], F32, o + 8192)
        pos_i = at("pos_i", [P, NT], I32, o + 10240)
        freqs = at("freqs", [P, 16], F32, o + 10304)
        rt = at("rt", [P, 16, NT * NE], F32, o + 8192)
        G = at("G", [P, NT, BS], F32R, o)
        Wt = at("Wt", [P, 2, SEQ], F32R, o + 8192)
        silu = at("silu", [P, FF], F32, o + 12288)
        hh = at("hh", [P, FF], F32, o + 13312)
        hhT = at("hhT", [P, 2, P], F32, o + 14336)
        Gq = at("Gq", [P, NT, SLOTS], F32R, o)
        Gw = at("Gw", [P, NT, SLOTS], F32, o + 1024)
        xgq = at("xgq", [P, KD, SLOTS], F32, o + 2048)
        Wq = at("Wq", [P, SEQ], F32R, o + 8192)
        o += 16384

        def small(name, shape, dt=F32):
            nonlocal o
            n = int(np.prod(shape[1:])) * (2 if dt == BF16 else 4)
            got = at(name, shape, dt, o)
            o += -(-n // 32) * 32
            return got

        ident = small("ident", [P, P])
        ident16 = small("ident16", [P, P], BF16)
        causal16 = small("causal16", [P, P], BF16)
        before16 = small("before16", [P, P], BF16)
        earlier16 = small("earlier16", [P, P], BF16)
        ones16 = small("ones16", [P, P], BF16)
        iota = small("iota", [P, SEQ])
        ones = small("ones", [P, 2])
        cossin = small("cossin", [P, 2, NT, 16])
        inv_n = small("inv_n", [P, 2, 16])
        inv_w = small("inv_w", [P, 2])
        past = small("past", [P, 8])
        kTx = small("kTx", [P, 2, MEM])
        vX = small("vX", [P, NM, GW])
        gains = small("gains", [P, 4, KD])
        g_out = small("g_out", [P, KD])
        g_cq = small("g_cq", [P, 3])
        g_rope = small("g_rope", [P, 2, ROPE])
        g_qk = small("g_qk", [P, 6])
        pool_s = small("pool_s", [P, 4])
        pool_w = small("pool_w", [P, 2, P])
        conv_w = small("conv_w", [P, 3, 2])
        conv_b = small("conv_b", [P, 2])
        sinks = small("sinks", [P, 4])
        w_rt = small("w_rt", [P, KD, 36])
        b_rt = small("b_rt", [P, 36])
        stat = small("stat", [P, 32])
        rsq_h = small("rsq_h", [P, 32])
        rsq_t = small("rsq_t", [P, 32])
        ssq_x = small("ssq_x", [P, NT])
        rstd_x = small("rstd_x", [P, NT])
        ssq_kr = small("ssq_kr", [P, NT])
        sA = small("sA", [P, NT, 2])
        rC = small("rC", [P, NT, 8])
        ssqA = small("ssqA", [P, NT, 8])
        rope_t = small("rope_t", [P, 4, ROPE])
        stat6 = small("stat6", [P, 24])
        mem_s = small("mem_s", [P, 2, NM])
        ssqY = small("ssqY", [P, 8, NT])
        rstdY = small("rstdY", [P, NG, NT])
        neg_max = small("neg_max", [P, 2, 2])
        den = small("den", [P, 2, 2])
        sink_e = small("sink_e", [P, 2, 2])
        slot = small("slot", [P, 2, NT])
        srel = small("srel", [P, 2, NT])
        wk = small("wk", [P, 2, NT])
        W_te = small("W_te", [P, NT, NE])
        ws = small("ws", [P, PPB])
        wsq = small("wsq", [P, 1])
        ovf = small("ovf", [P, 2 + OVF], I32)
        ovf_f = small("ovf_f", [P, 2 + OVF])
        assert base + o <= 229368, base + o

        ps = ctx.enter_context(nc.psum_tensor("ps", [P, 8, 512], F32))

        S = {n: ctx.enter_context(nc.semaphore(n)) for n in (*LAYER_COUNTS, *MOE_COUNTS)}
        bank_full = [ctx.enter_context(nc.semaphore(f"bank_full{i}")) for i in range(8)]
        bank_free = [ctx.enter_context(nc.semaphore(f"bank_free{i}")) for i in range(8)]
        moe_full = [ctx.enter_context(nc.semaphore(f"moe_full{i}")) for i in range(8)]
        moe_free = [ctx.enter_context(nc.semaphore(f"moe_free{i}")) for i in range(8)]
        ring_in = [ctx.enter_context(nc.semaphore(f"ring_in{i}")) for i in range(2)]
        slot_in = [ctx.enter_context(nc.semaphore(f"slot_in{i}")) for i in range(4)]
        slots_read = [ctx.enter_context(nc.semaphore(f"slots_read{i}")) for i in range(2)]
        sem = lambda n: ctx.enter_context(nc.semaphore(n))
        x_in, mem_in, pos_in, params_in, x_out = map(sem, ("x_in", "mem_in", "pos_in", "params_in", "x_out"))
        consts, init_pool, init_dve, sin_ready = map(sem, ("consts", "init_pool", "init_dve", "sin_ready"))
        rope_arg, waited = map(sem, ("rope_arg", "waited"))
        ovf_w, ovf_pe, ovf_act, ovf_dve = map(sem, ("ovf_w", "ovf_pe", "ovf_act", "ovf_dve"))

        OVF_PE, OVF_ACT, OVF_DVE = 7, 2, 8

        def done(l, name, n):
            return l * LAYER_COUNTS[name] + n

        def mdone(lb, name, n):
            return lb * MOE_COUNTS[name] + n

        def full(eng, l, name):
            bank, n, _ = dense.job[name]
            eng.wait_ge(bank_full[bank], l * dense.full[bank] + n)
            return ps[:, bank, :]

        def emptied(eng, l, name):
            bank, _, before = dense.job[name]
            eng.wait_ge(bank_free[bank], l * dense.free[bank] + before + 2)
            return ps[:, bank, :]

        def mfull(eng, lb, name):
            bank, n, _ = moe.job[name]
            eng.wait_ge(moe_full[bank], lb * moe.full[bank] + n)
            return ps[:, bank, :]

        def freed(name):
            return bank_free[dense.job[name][0]]

        def mfreed(name):
            return moe_free[moe.job[name][0]]

        def wait_apart(eng, semaphore, value):
            eng.wait_ge(semaphore, value)
            eng.sem_inc(waited, 1)

        x_d = a["x"].rearrange("b (t p) d -> p (b t) d", p=P)
        out_d = out.rearrange("b (t p) d -> p (b t) d", p=P)
        mem_d = a["mem"].rearrange("b (t p) d -> p (b t) d", p=P)
        pos_d = a["positions"].rearrange("b (t p) -> p (b t)", p=P)

        def lay(name, l):
            return a[name][bass.ds(l, 1)]

        def cols(name, l, c0, c1):
            return lay(name, l).rearrange("l (p c) n -> p (l c) n", c=KD)[:, :, c0:c1]

        wg_d = a["w_gate"].rearrange("l e (p c) n -> (l e) p (c n)", c=KD)
        wu_d = a["w_up"].rearrange("l e (p c) n -> (l e) p (c n)", c=KD)
        wd_d = a["w_down"].rearrange("l e (p c) n -> (l e) p (c n)", c=2)

        def expert(w, e):
            return w[bass.ds(e, 1)].rearrange("e p n -> p (e n)")

        RING0_DMAS = 9
        RING1_DMAS = 12
        PARAM_DMAS = 37

        def ring0_wait(eng, l, n):
            eng.wait_ge(ring_in[0], (l * RING0_DMAS + n) * 16)

        def ring1_wait(eng, l, n):
            eng.wait_ge(ring_in[1], (l * RING1_DMAS + n) * 16)

        block = ctx.enter_context(nc.Block())

        @block.sync
        def _(sp):
            sp.dma_start(memx[:], mem_d).then_inc(mem_in, 16)
            sp.dma_start(X[:], x_d).then_inc(x_in, 16)

            def read(l, name):
                bank, n, _ = dense.job[name]
                wait_apart(sp, bank_full[bank], l * dense.full[bank] + n)

            def load_mix(ring, q, l, n):
                w = lay("w_mix_out", l)[:, :, n * 512:(n + 1) * 512]

                def rows(r0, k):
                    return w[:, r0:r0 + k * P, :].rearrange("l (c p) n -> p (l c) n", p=P)
                sp.dma_start(ring[:, 0:2, 0:512], rows(GW, 2)).then_inc(ring_in[q], 16)
                sp.dma_start(ring[:, 2:4, 0:512], rows(3 * GW, 2)).then_inc(ring_in[q], 16)
                sp.dma_start(ring[:, 4:6, 0:512], rows(0, 2)).then_inc(ring_in[q], 16)
                for half in range(2):
                    src = w[:, 2 * GW + half * P:2 * GW + (half + 1) * P, :]
                    sp.dma_start(ring[half * HALF:(half + 1) * HALF, 6:8, 0:512],
                                 src.rearrange("l (c p) n -> p (l c) n", p=HALF)).then_inc(ring_in[q], 16)

            def load_pair(l, pair_of_layer, ps_):
                for j in range(2):
                    s = 2 * ps_ + j
                    e = l * NE + pair_of_layer * 2 + j
                    flat = wgu[s][:].rearrange("p u c n -> p u (c n)")
                    sp.dma_start(flat[:, 0, :], expert(wg_d, e)).then_inc(slot_in[s], 16)
                    sp.dma_start(flat[:, 1, :], expert(wu_d, e)).then_inc(slot_in[s], 16)
                    sp.dma_start(wdn[s][:].rearrange("p c n -> p (c n)"), expert(wd_d, e)).then_inc(slot_in[s], 16)

            with sp.Fori(0, DEPTH) as l:
                sp.wait_ge(S["gathered"], l * BATCHES + 1)
                sp.dma_start(ring0[:], cols("xa_w_kv", l, 0, 512)).then_inc(ring_in[0], 16)
                sp.dma_start(ring1[:, :, 0:ROPE], cols("w_in", l, C_B - ROPE, C_B)).then_inc(ring_in[1], 16)
                sp.dma_start(ring1[:, :, ROPE:544], cols("w_in", l, C_C, C_D)).then_inc(ring_in[1], 16)
                with sp.If(l > 0):
                    sp.wait_ge(S["layer_done"], l + 1)
                    sp.dma_start(memx[:], mem_d).then_inc(mem_in, 16)
                sp.wait_ge(slots_read[0], l * 8 + 1)
                load_pair(l, 0, 0)
                read(l, ("kvx", NM - 1))
                sp.dma_start(ring0[:, :, 0:384], cols("w_in", l, 0, 384)).then_inc(ring_in[0], 16)
                read(l, ("uC", NT - 1, 1))
                sp.dma_start(ring1[:, :, 0:256], cols("w_in", l, C_B, C_C)).then_inc(ring_in[1], 16)
                sp.dma_start(ring1[:, :, 256:512], cols("w_in", l, C_D + 256, C_D + 512)).then_inc(ring_in[1], 16)
                read(l, ("A", 2))
                sp.dma_start(ring0[:, :, 0:256], cols("w_in", l, C_D + 512, C_D + 768)).then_inc(ring_in[0], 16)
                sp.dma_start(ring0[:, :, 256:512], cols("w_in", l, C_D, C_D + 256)).then_inc(ring_in[0], 16)
                read(l, ("D", 3))
                load_mix(ring1, 1, l, 0)
                read(l, ("D", 5))
                load_mix(ring0, 0, l, 1)
                read(l, ("stY", 5))
                load_pair(l, 1, 1)
                read(l, ("mix", NT - 1, NG - 1, 0))
                sp.dma_start(ring1[:, :, 0:256], cols("xa_w_q", l, 0, 256)).then_inc(ring_in[1], 16)
                for c in range(2):
                    src = lay("xa_w_o", l)[:, c * P:(c + 1) * P, :]
                    sp.dma_start(ring1[:, 4 * c:4 * c + 4, 272:528],
                                 src.rearrange("l p (q n) -> p (l q) n", n=256)).then_inc(ring_in[1], 16)
                for p in range(2, PPB):
                    sp.wait_ge(slots_read[p % 2], l * 8 + 1 + p // 2)
                    load_pair(l, p, p % 2)
                with sp.Fori(1, BATCHES) as b:
                    for p in range(PPB):
                        sp.wait_ge(slots_read[p % 2], l * 8 + b * 2 + 1 + p // 2)
                        load_pair(l, b * PPB + p, p % 2)
                wait_apart(sp, S["route_ready"], l + 1)
                n_ovf = sp.value_load(ovf[0:1, 0:1], min_val=0, max_val=OVF - 1)
                before = sp.value_load(ovf[0:1, 1:2], min_val=0, max_val=DEPTH * OVF)
                with sp.If(n_ovf > 0):
                    wait_apart(sp, slots_read[0], l * 8 + 8 + 1)
                    with sp.Fori(0, n_ovf) as q:
                        e = sp.value_load(ovf[0:1, bass.ds(q + 2, 1)], min_val=0, max_val=NE - 1)
                        with sp.If(q > 0):
                            wait_apart(sp, ovf_pe, (before + q) * OVF_PE)
                        row = l * NE + e
                        flat = wgu[0][:].rearrange("p u c n -> p u (c n)")
                        sp.dma_start(flat[:, 0, :], expert(wg_d, row)).then_inc(ovf_w, 16)
                        sp.dma_start(flat[:, 1, :], expert(wu_d, row)).then_inc(ovf_w, 16)
                        sp.dma_start(wdn[0][:].rearrange("p c n -> p (c n)"), expert(wd_d, row)).then_inc(ovf_w, 16)
                    wait_apart(sp, ovf_pe, (before + n_ovf) * OVF_PE)
            sp.wait_ge(S["layer_done"], DEPTH + 1)
            sp.dma_start(out_d, X[:]).then_inc(x_out, 16)
            sp.wait_ge(x_out, 16)

        @block.gpsimd
        def _(pool):
            pool.dma_start(pos_i[:], pos_d, allow_slow_non_contiguous=True).then_inc(pos_in, 16)
            pool.memset(ident[:], 0.0)
            pool.memset(causal16[:], 0.0)
            pool.memset(before16[:], 0.0)
            pool.memset(earlier16[:], 1.0)
            pool.memset(ones16[:], 1.0)
            pool.memset(ones[:], 1.0)
            pool.memset(pool_w[:], 0.0)
            for j in range(16):
                freq = float(np.float32(THETA) ** (-np.float32(j) / np.float32(16)))
                pool.memset(freqs[:, j:j + 1], freq)
            pool.drain()
            for w in range(4):
                rows = slice((w % 2) * HALF, (w % 2 + 1) * HALF)
                pool.memset(inv_w[rows, w // 2:w // 2 + 1], 1.0 / WINDOWS[w])
                pool.memset(inv_n[rows, w // 2, :], float(WINDOWS[w]))
                pool.drain()
            pool.iota(iota[:], pattern=[[1, SEQ]], base=0, channel_multiplier=0, allow_small_or_imprecise_dtypes=True)
            pool.drain()
            pool.affine_select(out=ident[:], in_=ident[:], compare_op=ALU.not_equal, fill=1.0,
                               base=0, pattern=[[-1, P]], channel_multiplier=1)
            pool.affine_select(out=causal16[:], in_=causal16[:], compare_op=ALU.is_ge, fill=NEG,
                               base=0, pattern=[[-1, P]], channel_multiplier=1)
            pool.affine_select(out=before16[:], in_=before16[:], compare_op=ALU.is_gt, fill=NEG,
                               base=0, pattern=[[1, P]], channel_multiplier=-1)
            pool.affine_select(out=earlier16[:], in_=earlier16[:], compare_op=ALU.is_gt, fill=0.0,
                               base=0, pattern=[[1, P]], channel_multiplier=-1)
            pool.drain()
            pool.tensor_copy(ident16[:], ident[:])
            pool.drain()
            pool.nop().then_inc(init_pool, 1)

            n_dma = 0

            def load(dst, src):
                nonlocal n_dma
                n_dma += 1
                pool.dma_start(dst, src, allow_slow_non_contiguous=True).then_inc(params_in, 16)

            def across(src, n):
                return src.partition_broadcast(n)

            with pool.Fori(0, DEPTH) as l:
                n_dma = 0
                pool.wait_ge(S["layer_done"], l + 1)
                for i, name in enumerate(("norm_mix", "norm_xa", "norm_ffn", "norm_mem")):
                    load(gains[:, i, :], lay(name, l).rearrange("l (p c) -> p (l c)", c=KD))
                load(g_cq[:, 0:2], lay("mla_g_cq", l).rearrange("l (c p) -> p (l c)", p=P))
                load(g_cq[:, 2:3], lay("mla_g_ckv", l).rearrange("l (c p) -> p (l c)", p=P))
                load(w_uq[:], lay("mla_w_uq", l).rearrange("l (c p) n -> p (l c) n", p=P))
                load(w_ukv[:], lay("mla_w_ukv", l).rearrange("l p n -> p (l n)"))
                for i, name in enumerate(("mla_g_q", "mla_g_k")):
                    g = lay(name, l)
                    load(g_rope[:, i, :], g[0, NOPE:QK].partition_broadcast(P))
                    load(g_qk[0:NOPE, i:i + 1], g[:, 0:NOPE].rearrange("l p -> p l"))
                for i, name in enumerate(("swa_g_q", "swa_g_k", "xa_g_q", "xa_g_k")):
                    for half in range(2):
                        load(g_qk[half * HD:(half + 1) * HD, 2 + i:3 + i], lay(name, l).rearrange("l p -> p l"))
                load(pool_s[:, 0:2], lay("pool_scale", l).rearrange("l (c p) -> p (l c)", p=P))
                for g in range(4):
                    h = (g % 2) * HD
                    load(pool_w[h:h + HD, g // 2, h:h + HD], lay("pool_w", l)[:, g].rearrange("l c d -> c (l d)"))
                load(conv_w[:].rearrange("p k c -> p (k c)"), lay("conv_w", l).rearrange("l k (c p) -> p (l k c)", p=P))
                load(conv_b[:], lay("conv_b", l).rearrange("l (c p) -> p (l c)", p=P))
                load(sinks[:], lay("swa_sinks", l)[0].partition_broadcast(P))
                g = lay("mix_out_norm", l)
                load(g_out[:, 0:2], g[:, GW:2 * GW].rearrange("l (c p) -> p (l c)", p=P))
                load(g_out[:, 2:4], g[:, 3 * GW:].rearrange("l (c p) -> p (l c)", p=P))
                load(g_out[:, 4:6], g[:, 0:GW].rearrange("l (c p) -> p (l c)", p=P))
                for half in range(2):
                    load(g_out[half * HALF:(half + 1) * HALF, 6:8],
                         g[:, 2 * GW + half * P:2 * GW + (half + 1) * P].rearrange("l (c p) -> p (l c)", p=HALF))
                load(w_rt[:, :, 0:NG], cols("w_group", l, 0, NG))
                load(w_rt[:, :, NG:NG + NE], cols("w_expert", l, 0, NE))
                load(b_rt[:, 0:NG], lay("b_group", l)[0].partition_broadcast(P))
                load(b_rt[:, NG:NG + NE], lay("b_expert", l)[0].partition_broadcast(P))
            assert n_dma == PARAM_DMAS, n_dma

        @block.scalar
        def _(act):
            def copy(dst, src, scale=1.0):
                return nc.scalar.activation(dst, src, ACT.Copy, scale=scale)

            def square(dst, src, **kw):
                return nc.scalar.activation(dst, src, ACT.Square, **kw)

            act.wait_ge(rope_arg, 1)
            nc.scalar.activation(cossin[:], rope0[:, 4:6], ACT.Sin).then_inc(sin_ready, 1)

            def normalise(l, s, t):
                act.wait_ge(S["x_rstd"], done(l, "x_rstd", 1 if s == 0 else 2 + NT * (s - 1) + t))
                if t >= 2:
                    full(act, l, ("xT", s, t - 2, 1))
                copy(xn[:, t % 2], X[:, t], scale=rstd_x[:, t:t + 1]).then_inc(S["xn_ready"], 1)

            def sum_squares(l, s, t):
                act.wait_ge(S["x_updated"], done(l, "x_updated", NT * (s - 1) + t + 1))
                square(xn[:, t % 2], X[:, t], accum_out=ssq_x[:, t:t + 1])
                act.drain()
                act.nop().then_inc(S["x_ssq"], 1)

            def attend(l, list_, first):
                for n in range(len(list_) + 3):
                    if n < len(list_):
                        kind, pair, t, nk = list_[n]
                        u = first + n
                        L = nk * P
                        act.wait_ge(S["max_ready"], done(l, "max_ready", u + 1))
                        if n >= 2:
                            full(act, l, ("T", list_[n - 2], 1))
                        for h in range(2):
                            bank = full(act, l, ("S", list_[n], h))
                            nc.scalar.activation(Pr[:, n % 2, h, 0:L], bank[:, 0:L], ACT.Exp,
                                                 bias=neg_max[:, n % 2, h:h + 1],
                                                 accum_out=den[:, n % 2, h:h + 1]
                                                 ).then_inc(freed(("S", list_[n], h)), 1)
                        if kind == "swa":
                            nc.scalar.activation(sink_e[:, n % 2], sink_e[:, n % 2], ACT.Exp)
                        act.drain()
                        act.nop().then_inc(S["p_ready"], 1)
                    if 1 <= n <= len(list_):
                        nk = list_[n - 1][3]
                        bank = full(act, l, ("T", list_[n - 1], 0))
                        copy(PT[:, (n - 1) % 2, 0, 0:nk * P], bank[:, 0:nk * P]
                             ).then_inc(freed(("T", list_[n - 1], 0)), 1)
                    if 2 <= n <= len(list_) + 1 and list_[n - 2][2] == NT - 1:
                        kind, pair = list_[n - 2][:2]
                        bank = full(act, l, ("O", kind, pair))
                        if kind == "xa":
                            copy(oTx[:, pair], bank).then_inc(freed(("O", kind, pair)), 1)
                            act.drain()
                            act.nop().then_inc(S["oTx_ready"], 1)
                        else:
                            if kind == "mla":
                                full(act, l, ("stY", stat_of(("swa", pair))))
                            square(sqO[:, pair], bank).then_inc(freed(("O", kind, pair)), 1)
                            act.drain()
                            act.nop().then_inc(S["sqY_ready"], 1)

            with act.Fori(0, DEPTH) as l:
                act.wait_ge(S["layer_done"], l + 1)
                act.wait_ge(mem_in, (l + 1) * 16)
                for i in range(NM):
                    square(xn[:, i], memx[:, i], accum_out=mem_s[:, 0, i:i + 1])
                act.drain()
                act.nop().then_inc(S["mem_ssq"], 1)
                act.wait_ge(x_in, 16)
                for t in range(NT):
                    square(xn[:, t % 2], X[:, t], accum_out=ssq_x[:, t:t + 1])
                    act.drain()
                act.nop().then_inc(S["x_ssq"], 1)
                act.wait_ge(S["mem_rstd"], done(l, "mem_rstd", 1))
                for i in range(NM):
                    copy(memx[:, i], memx[:, i], scale=mem_s[:, 1, i:i + 1]).then_inc(S["memx_ready"], 1)
                normalise(l, 0, 0)
                normalise(l, 0, 1)
                for i in range(NM):
                    bank = full(act, l, ("kvx", i))
                    copy(vX[:, i], bank[:, GW:]).then_inc(S["xa_kv_ready"], 1)
                    square(sqC[:, i, 0:GW], bank[:, 0:GW]).then_inc(freed(("kvx", i)), 1)
                    act.drain()
                    act.nop().then_inc(S["kx_squared"], 1)
                normalise(l, 0, 2)
                normalise(l, 0, 3)
                act.wait_ge(S["kx_ready"], done(l, "kx_ready", NM))
                for t in range(NT):
                    if t >= 2:
                        act.wait_ge(S["uC_reduced"], done(l, "uC_reduced", t - 1))
                    bank = full(act, l, ("uC", t, 0))
                    copy(kr[:, t], bank[:, 0:ROPE])
                    square(sqC[:, t % 2, 0:ROPE], bank[:, 0:ROPE], accum_out=ssq_kr[:, t:t + 1])
                    act.drain()
                    copy(qkC[:, t, 0:GW].rearrange("p (g k d) -> p k g d", g=2, k=2),
                         bank[:, ROPE:ROPE + GW].rearrange("p (k g d) -> p k g d", g=2, k=2)
                         ).then_inc(freed(("uC", t, 0)), 1)
                    bank = full(act, l, ("uC", t, 1))
                    copy(vC[:, t], bank[:, P:2 * P])
                    copy(qkC[:, t, GW:], bank[:, 0:P]).then_inc(freed(("uC", t, 1)), 1)
                    act.drain()
                    square(sqC[:, t % 2], qkC[:, t])
                    act.drain()
                    act.nop().then_inc(S["uC_copied"], 1)
                for i in range(NM):
                    bank = full(act, l, ("kxT", i))
                    copy(kTx[:, :, i * P:(i + 1) * P], bank[:, 0:2 * P].rearrange("p (c m) -> p c m", c=2),
                         scale=g_qk[:, 5:6]).then_inc(freed(("kxT", i)), 1)
                    act.drain()
                    act.nop().then_inc(S["xa_kv_ready"], 1)
                act.wait_ge(S["uC_reduced"], done(l, "uC_reduced", NT))
                for m in range(3):
                    bank = full(act, l, ("A", m))
                    square(sqA[:, m], bank).then_inc(freed(("A", m)), 1)
                    act.drain()
                    act.nop().then_inc(S["sqA_ready"], 1)
                full(act, l, ("stA",))
                for m in range(2):
                    bank = full(act, l, ("B", m))
                    if m > 0:
                        act.wait_ge(S["u_free"], done(l, "u_free", m))
                    nc.scalar.activation(U0[:, 0:16], bank[:, 0:16], ACT.Copy, scale=0.0)
                    copy(U0[:, 16:528], bank).then_inc(freed(("B", m)), 1)
                    act.drain()
                    act.nop().then_inc(S["u_ready"], 1)
                act.wait_ge(S["sA_ready"], done(l, "sA_ready", 1))
                for t in range(NT):
                    bank = full(act, l, ("qA", t))
                    if t > 0:
                        act.wait_ge(S["qkA_reduced"], done(l, "qkA_reduced", t))
                    copy(qkA[:, t, 0:4], bank[:, 0:384].rearrange("p (h d) -> p h d", h=4), scale=sA[:, t, 0:1]).then_inc(freed(("qA", t)), 1)
                    bank = full(act, l, ("kvA", t))
                    kv = bank.rearrange("p (h u d) -> p h u d", h=4, u=2)
                    copy(qkA[:, t, 4:8, 0:NOPE], kv[:, :, 0, :], scale=sA[:, t, 1:2])
                    copy(vA[:, t].rearrange("p (h d) -> p h d", h=4), kv[:, :, 1, :],
                         scale=sA[:, t, 1:2]).then_inc(freed(("kvA", t)), 1)
                    act.drain()
                    square(sqY[:, 0:384].rearrange("p (h d) -> p h d", h=4), qkA[:, t, 0:4])
                    square(sqY[:, 384:640].rearrange("p (h d) -> p h d", h=4), qkA[:, t, 4:8, 0:NOPE])
                    act.drain()
                    act.nop().then_inc(S["qkA_copied"], 1)
                for t in range(NT):
                    bank = full(act, l, ("cT", t))
                    copy(qTC[:, :, t * P:(t + 1) * P], bank[:, 0:2 * P].rearrange("p (c m) -> p c m", c=2),
                         scale=g_qk[:, 2:3]).then_inc(freed(("cT", t)), 1)
                    act.drain()
                    act.nop().then_inc(S["cT_ready"], 1)

                def gate_copy(i, name):
                    bank = full(act, l, name)
                    if i > 0:
                        act.wait_ge(S["z_done"], done(l, "z_done", i))
                    copy(U0[:, 0:SEQ], bank).then_inc(freed(name), 1)
                    act.drain()
                    act.nop().then_inc(S["c_ready"], 1)

                def pool_square(m):
                    bank = full(act, l, ("pool", m))
                    if m > 0:
                        full(act, l, ("stY", m - 1))
                    square(sqY[:, 0:SEQ], bank, scale=pool_s[:, m:m + 1]).then_inc(freed(("pool", m)), 1)
                    act.drain()
                    act.nop().then_inc(S["sqY_ready"], 1)

                def conv_square(m):
                    full(act, l, ("stY", 1 + m))
                    act.wait_ge(S["yD_ready"], done(l, "yD_ready", m + 1))
                    square(sqY[:, 0:SEQ], U2[:, 0:SEQ])
                    act.drain()
                    act.nop().then_inc(S["sqY_ready"], 1)

                def query_transposed(t):
                    bank = full(act, l, ("qAT", t))
                    copy(qTA[0:QK, :, t * P:(t + 1) * P], bank[0:QK].rearrange("p (h m) -> p h m", h=4),
                         scale=g_qk[0:QK, 0:1]).then_inc(freed(("qAT", t)), 1)
                    act.drain()
                    act.nop().then_inc(S["qkAT_ready"], 1)

                act.wait_ge(S["u_free"], done(l, "u_free", 2))
                gate_copy(0, ("D", 0))
                act.wait_ge(S["qkA_reduced"], done(l, "qkA_reduced", NT))
                pool_square(0)
                pool_square(1)
                query_transposed(0)
                query_transposed(1)
                gate_copy(1, ("D", 3))
                query_transposed(2)
                query_transposed(3)
                conv_square(0)
                conv_square(1)
                attend(l, units, 0)
                for t in range(NT):
                    if t >= 2:
                        full(act, l, ("xT", 1, t - 2, 1))
                    sum_squares(l, 1, t)
                    normalise(l, 1, t)
                for t in range(NT):
                    bank = full(act, l, ("qx", t))
                    if t >= 2:
                        act.wait_ge(S["qx_reduced"], done(l, "qx_reduced", t - 1))
                    copy(qx[:, t], bank[:, 0:GW])
                    square(sqx[:, t % 2], bank[:, 0:GW]).then_inc(freed(("qx", t)), 1)
                    act.drain()
                    act.nop().then_inc(S["qx_copied"], 1)
                for t in range(NT):
                    bank = full(act, l, ("qxT", t))
                    copy(qTx[:, :, t * P:(t + 1) * P], bank[:, 0:2 * P].rearrange("p (c m) -> p c m", c=2),
                         scale=g_qk[:, 4:5]).then_inc(freed(("qxT", t)), 1)
                    act.drain()
                    act.nop().then_inc(S["qxT_ready"], 1)
                attend(l, cross, len(units))
                for t in range(NT):
                    if t >= 2:
                        full(act, l, ("xT", 2, t - 2, 1))
                    sum_squares(l, 2, t)
                    normalise(l, 2, t)
                    copy(xhi[:, t], X[:, t], scale=rstd_x[:, t:t + 1]).then_inc(S["xhi_ready"], 1)

                act.wait_ge(S["exp_arg"], done(l, "exp_arg", 1))
                nc.scalar.activation(rt[:, 4, 0:NT * NG], rt[:, 4, 0:NT * NG], ACT.Exp)
                nc.scalar.activation(rt[:, 11, 0:NT], rt[:, 11, 0:NT], ACT.Exp)
                act.drain()
                act.nop().then_inc(S["exp_done"], 1)

                with act.Fori(0, BATCHES) as b:
                    lb = l * BATCHES + b
                    for c in range(0, KD, 2):
                        bank = mfull(act, lb, ("gather", c))
                        copy(xgT[:, c], bank, scale=gains[:, 2, c:c + 1]).then_inc(mfreed(("gather", c)), 1)
                        act.drain()
                        act.nop().then_inc(S["xg_ready"], 1)
                    for p in range(PPB):
                        bank = mfull(act, lb, ("GT", p))
                        copy(Wt[:, p % 2], bank).then_inc(mfreed(("GT", p)), 1)
                        act.drain()
                        act.nop().then_inc(S["Wt_ready"], 1)
                        bank = mfull(act, lb, ("gu", p))
                        if p > 0:
                            act.wait_ge(S["hh_ready"], mdone(lb, "hh_ready", p))
                        nc.scalar.activation(silu[:], bank[:, 0:FF], ACT.Silu).then_inc(mfreed(("gu", p)), 1)
                        act.drain()
                        act.nop().then_inc(S["silu_ready"], 1)
                        bank = mfull(act, lb, ("hhT", p))
                        copy(hhT[:], bank[:, 0:2 * P].rearrange("p (c m) -> p c m", c=2)
                             ).then_inc(mfreed(("hhT", p)), 1)
                        act.drain()
                        act.nop().then_inc(S["hhT_ready"], 1)
                        for h in range(2):
                            bank = mfull(act, lb, ("down", p, h))
                            if p == 0 and h == 0:
                                act.wait_ge(S["ws_ready"], mdone(lb, "ws_ready", 1))
                            copy(yhi[:, p % 2, h * 512:(h + 1) * 512], bank, scale=ws[:, p:p + 1]
                                 ).then_inc(mfreed(("down", p, h)), 1)
                            act.drain()
                            act.nop().then_inc(S["yhi_ready"], 1)
                wait_apart(act, S["route_ready"], l + 1)
                n_ovf = act.value_load(ovf[0:1, 0:1], min_val=0, max_val=OVF - 1)
                before = act.value_load(ovf[0:1, 1:2], min_val=0, max_val=DEPTH * OVF)
                with act.If(n_ovf > 0):
                    with act.Fori(0, n_ovf) as q:
                        tile = before + q
                        act.wait_ge(ovf_pe, tile * OVF_PE + 3)
                        nc.scalar.activation(silu[0:SLOTS], ps[0:SLOTS, 4, 0:FF], ACT.Silu).then_inc(ovf_act, 1)
                        act.wait_ge(ovf_pe, tile * OVF_PE + 5)
                        act.wait_ge(ovf_dve, tile * OVF_DVE + 3)
                        copy(yhi[0:SLOTS, 0].rearrange("p (h n) -> p h n", h=2), ps[0:SLOTS, 6:8, :],
                             scale=wsq[0:SLOTS]).then_inc(ovf_act, 1)

        @block.vector
        def _(dve):
            tt, ts, stt = nc.vector.tensor_tensor, nc.vector.tensor_scalar, nc.vector.scalar_tensor_tensor

            def signal(name):
                dve.drain()
                dve.nop().then_inc(S[name], 1)

            def mean_eps(dst, src, n):
                ts(dst, src, 1.0 / n, EPS, ALU.mult, ALU.add)

            def rsqrt(dst, v, n):
                h, w = rsq_h[:, 0:n], rsq_t[:, 0:n]
                dve.drain()
                ts(h, v, -0.5, None, ALU.mult)
                ts(dst.bitcast(I32), v.bitcast(I32), 1, None, ALU.logical_shift_right)
                dve.drain()
                ts(dst.bitcast(I32), dst.bitcast(I32), -1.0, RSQRT_MAGIC, ALU.mult, ALU.add)
                for _ in range(3):
                    dve.drain()
                    tt(w, dst, dst, ALU.mult)
                    dve.drain()
                    tt(w, w, h, ALU.mult)
                    dve.drain()
                    stt(dst, w, 1.5, dst, ALU.add, ALU.mult)
                dve.drain()

            def flat(tile):
                pattern = {2: "p a -> p a", 3: "p a b -> p (a b)", 4: "p a b c -> p (a b c)"}[len(tile.shape)]
                return tile[:].rearrange(pattern)

            def transposed(l, s, t, gain):
                for h in range(2):
                    bank = full(dve, l, ("xT", s, t, h))
                    g = gains[:, gain, 4 * h:4 * h + 4].unsqueeze(2).to_broadcast([P, 4, P])
                    tt(hT[:, 4 * h:4 * h + 4, t * P:(t + 1) * P], bank.rearrange("p (c m) -> p c m", c=4), g,
                       ALU.mult).then_inc(freed(("xT", s, t, h)), 1)
                    signal("hT_ready")

            def tile_rstd(l, s, t):
                dve.wait_ge(S["x_ssq"], done(l, "x_ssq", 2 + NT * (s - 1) + t))
                mean_eps(stat[:, 0:1], ssq_x[:, t:t + 1], D)
                rsqrt(rstd_x[:, t:t + 1], stat[:, 0:1], 1)
                signal("x_rstd")

            def attend(l, list_, first):
                for n in range(len(list_) + 3):
                    if n < len(list_):
                        kind, pair, t, nk = list_[n]
                        L = nk * P
                        full(dve, l, ("S", list_[n], 0))
                        full(dve, l, ("S", list_[n], 1))
                        u = n % 2
                        m = neg_max[:, u]
                        nc.vector.tensor_reduce(m, ps[:, 2 * u:2 * u + 2, 0:L], AX_X, ALU.max)
                        dve.drain()
                        if kind == "swa":
                            s = sinks[:, pair::2]
                            tt(m, m, s, ALU.max)
                            dve.drain()
                            tt(sink_e[:, u], s, m, ALU.subtract)
                        ts(m, m, -1.0, None, ALU.mult)
                        signal("max_ready")
                    if 1 <= n <= len(list_):
                        nk = list_[n - 1][3]
                        bank = full(dve, l, ("T", list_[n - 1], 1))
                        nc.vector.tensor_copy(PT[:, (n - 1) % 2, 1, 0:nk * P], bank[:, 0:nk * P]
                                              ).then_inc(freed(("T", list_[n - 1], 1)), 1)
                    if n < len(list_):
                        dve.wait_ge(S["p_ready"], done(l, "p_ready", first + n + 1))
                        if kind == "swa":
                            tt(den[:, u], den[:, u], sink_e[:, u], ALU.add)
                            dve.drain()
                        nc.vector.reciprocal(den[:, u], den[:, u])
                        dve.drain()
                        for h in range(2):
                            ts(Pr[:, u, h, 0:L], Pr[:, u, h, 0:L], den[:, u, h:h + 1], None, ALU.mult)
                        signal("pn_ready")
                    if 2 <= n <= len(list_) + 1 and list_[n - 2][2] == NT - 1 and list_[n - 2][0] != "xa":
                        kind2, pair2 = list_[n - 2][:2]
                        bank = emptied(dve, l, ("O", kind2, pair2))
                        c = stat_of(list_[n - 2])
                        ts(yT[:, c], bank, g_out[:, c:c + 1], None, ALU.mult).then_inc(freed(("O", kind2, pair2)), 1)
                        signal("yT_ready")
                    if n >= 3 and list_[n - 3][2] == NT - 1 and list_[n - 3][0] != "xa":
                        evacuate_stat(l, stat_of(list_[n - 3]))

            def evacuate_stat(l, c):
                bank = full(dve, l, ("stY", c))
                nc.vector.tensor_copy(ssqY[:, c], bank[:, 0:NT]).then_inc(freed(("stY", c)), 1)

            def argmax_first(vals, n, m, oh, tmp):
                mb = m.to_broadcast([P, NT, n])
                tt(tmp, vals, mb, ALU.is_lt)
                dve.drain()
                io = iota[:, 0:n].unsqueeze(1).to_broadcast([P, NT, n])
                stt(tmp, tmp, float(SEQ), io, ALU.mult, ALU.add)
                dve.drain()
                nc.vector.tensor_reduce(rt[:, 15, 0:NT].unsqueeze(2), tmp, AX_X, ALU.min)
                dve.drain()
                tt(oh, io, rt[:, 15, 0:NT].unsqueeze(2).to_broadcast([P, NT, n]), ALU.is_equal)
                dve.drain()

            for bank in range(8):
                dve.sem_inc(bank_free[bank], 1)
                dve.sem_inc(moe_free[bank], 1)
            for s_ in (*slots_read, S["layer_done"], S["gathered"]):
                dve.sem_inc(s_, 1)
            dve.wait_ge(init_pool, 1)
            dve.wait_ge(pos_in, 16)
            posf = rope0[:, 3, 0, 0:NT]
            nc.vector.tensor_copy(posf, pos_i[:])
            dve.drain()
            tt(rope0[:, 0], posf.unsqueeze(2).to_broadcast([P, NT, 16]),
               freqs[:].unsqueeze(1).to_broadcast([P, NT, 16]), ALU.mult)
            dve.drain()
            ts(rope0[:, 1], rope0[:, 0], 1.0 / TWO_PI, ROUND, ALU.mult, ALU.add)
            dve.drain()
            ts(rope0[:, 1], rope0[:, 1], -ROUND, None, ALU.add)
            dve.drain()
            stt(rope0[:, 2], rope0[:, 1], -PI_A, rope0[:, 0], ALU.mult, ALU.add)
            dve.drain()
            stt(rope0[:, 0], rope0[:, 1], -PI_B, rope0[:, 2], ALU.mult, ALU.add)
            dve.drain()
            stt(rope0[:, 2], rope0[:, 1], -PI_C, rope0[:, 0], ALU.mult, ALU.add)
            dve.drain()
            ts(rope0[:, 0], rope0[:, 2], math.pi / 2, None, ALU.add)
            ts(rope0[:, 5], rope0[:, 2], PI_MAX, -PI_MAX, ALU.min, ALU.max)
            dve.drain()
            ts(rope0[:, 1], rope0[:, 0], math.pi, -TWO_PI, ALU.is_gt, ALU.mult)
            dve.drain()
            tt(rope0[:, 0], rope0[:, 0], rope0[:, 1], ALU.add)
            dve.drain()
            ts(rope0[:, 4], rope0[:, 0], PI_MAX, -PI_MAX, ALU.min, ALU.max)
            dve.drain()
            dve.nop().then_inc(rope_arg, 1)
            for c in range(2):
                stt(inv_n[:, c], iota[:, 0:16], 1.0, inv_n[:, c], ALU.add, ALU.min)
            dve.drain()
            nc.vector.reciprocal(inv_n[:], inv_n[:])
            ts(past[:, 0:7], iota[:, 1:8], float(SLOTS), None, ALU.mult)
            nc.vector.memset(ovf_f[:], 0.0)
            dve.drain()
            dve.nop().then_inc(init_dve, 1)
            dve.wait_ge(sin_ready, 1)

            with dve.Fori(0, DEPTH) as l:
                dve.wait_ge(S["mem_ssq"], done(l, "mem_ssq", 1))
                mean_eps(stat[:, 0:NM], mem_s[:, 0], D)
                rsqrt(mem_s[:, 1], stat[:, 0:NM], NM)
                signal("mem_rstd")
                dve.wait_ge(S["x_ssq"], done(l, "x_ssq", 1))
                mean_eps(stat[:, 0:NT], ssq_x[:], D)
                rsqrt(rstd_x[:], stat[:, 0:NT], NT)
                signal("x_rstd")
                dve.wait_ge(params_in, (l + 1) * PARAM_DMAS * 16)
                for i in range(NM):
                    for h in range(2):
                        bank = full(dve, l, ("memT", i, h))
                        g = gains[:, 3, 4 * h:4 * h + 4].unsqueeze(2).to_broadcast([P, 4, P])
                        tt(hmT[:, 4 * h:4 * h + 4, i * P:(i + 1) * P], bank.rearrange("p (c m) -> p c m", c=4), g,
                           ALU.mult).then_inc(freed(("memT", i, h)), 1)
                        signal("hmT_ready")
                tt(pool_s[:, 2:4], pool_s[:, 0:2], g_out[:, 0:2], ALU.mult)
                nc.vector.memset(g_qk[HD:QK, 0:2], 1.0)
                for table, i in ((rope_q, 0), (rope_k, 1)):
                    g1 = g_rope[:, i, 0:16].unsqueeze(1).to_broadcast([P, NT, 16])
                    g2 = g_rope[:, i, 16:32].unsqueeze(1).to_broadcast([P, NT, 16])
                    tt(table[:, :, 0, 0:16], cossin[:, 0], g1, ALU.mult)
                    tt(table[:, :, 0, 16:32], cossin[:, 0], g2, ALU.mult)
                    stt(table[:, :, 1, 0:16], cossin[:, 1], -1.0, g2, ALU.mult, ALU.mult)
                    tt(table[:, :, 1, 16:32], cossin[:, 1], g1, ALU.mult)
                for t in range(NT):
                    transposed(l, 0, t, 0)
                dve.wait_ge(S["kx_squared"], done(l, "kx_squared", NM))
                for i in range(NM):
                    nc.vector.tensor_reduce(stat[:, 8 + 4 * i:12 + 4 * i].unsqueeze(2),
                                            sqC[:, i, 0:GW].rearrange("p (h d) -> p h d", h=4), AX_X, ALU.add)
                dve.drain()
                mean_eps(stat[:, 0:8], stat[:, 8:16], HD)
                rsqrt(stat[:, 16:24], stat[:, 0:8], 8)
                for i in range(NM):
                    bank = full(dve, l, ("kvx", i))
                    r = stat[:, 16 + 4 * i:20 + 4 * i].unsqueeze(2).to_broadcast([P, 4, HD])
                    tt(knx[:, i].rearrange("p (h d) -> p h d", h=4), bank[:, 0:GW].rearrange("p (h d) -> p h d", h=4),
                       r, ALU.mult).then_inc(freed(("kvx", i)), 1)
                    signal("kx_ready")
                for t in range(NT):
                    dve.wait_ge(S["uC_copied"], done(l, "uC_copied", t + 1))
                    nc.vector.tensor_reduce(rC[:, t, 0:6].unsqueeze(2),
                                            sqC[:, t % 2].rearrange("p (h d) -> p h d", h=6), AX_X, ALU.add)
                    signal("uC_reduced")
                mean_eps(stat[:, 0:24].rearrange("p (t h) -> p t h", t=NT), rC[:, :, 0:6], HD)
                rsqrt(stat6[:], stat[:, 0:24], 24)
                s6 = stat6[:].rearrange("p (t h) -> p t h", t=NT)
                ts(s6[:, :, 0:4], s6[:, :, 0:4], HD ** -0.5, None, ALU.mult)
                dve.drain()
                for t in range(NT):
                    r = s6[:, t].unsqueeze(2).to_broadcast([P, 6, HD])
                    v = qkC[:, t].rearrange("p (h d) -> p h d", h=6)
                    tt(v, v, r, ALU.mult)
                    signal("qC_ready")
                def rotate(dst, src, table, heads, tmp):
                    shape = [P, heads, ROPE]
                    c = table[:, 0].unsqueeze(1).to_broadcast(shape)
                    s1 = table[:, 1, 0:16].unsqueeze(1).to_broadcast([P, heads, 16])
                    s2 = table[:, 1, 16:32].unsqueeze(1).to_broadcast([P, heads, 16])
                    tt(tmp[:, :, 0:16], src[:, :, 16:32], s1, ALU.mult)
                    tt(tmp[:, :, 16:32], src[:, :, 0:16], s2, ALU.mult)
                    dve.drain()
                    tt(dst, src, c, ALU.mult)
                    dve.drain()
                    tt(dst, dst, tmp, ALU.add)
                tt(krot[:, :, 0:16], kr[:, :, 16:32], rope_k[:, :, 1, 0:16], ALU.mult)
                tt(krot[:, :, 16:32], kr[:, :, 0:16], rope_k[:, :, 1, 16:32], ALU.mult)
                dve.drain()
                tt(kr[:], kr[:], rope_k[:, :, 0], ALU.mult)
                dve.drain()
                tt(krot[:], krot[:], kr[:], ALU.add)
                for m in range(3):
                    bank = emptied(dve, l, ("A", m))
                    ts(cqT[:, m], bank, g_cq[:, m:m + 1], None, ALU.mult).then_inc(freed(("A", m)), 1)
                    signal("cqT_ready")
                bank = full(dve, l, ("stA",))
                v = bank[:, 0:2 * NT].rearrange("p (t j) -> p t j", j=2)
                st = stat[:, 0:8].rearrange("p (t j) -> p t j", j=2)
                mean_eps(st[:, :, 0], v[:, :, 0], QR)
                ts(st[:, :, 1], v[:, :, 1], 1.0 / KVR, EPS, ALU.mult, ALU.add).then_inc(freed(("stA",)), 1)
                rsqrt(flat(sA), stat[:, 0:8], 8)
                signal("sA_ready")
                for m in range(2):
                    dve.wait_ge(S["u_ready"], done(l, "u_ready", m + 1))
                    src, spare, width = U0, [U1, U2], 1
                    wins = []
                    for k in range(2 * m + 2):
                        dst = spare[k % 2]
                        rows = slice(0, P) if k < 2 * m + 1 else slice(HALF, P)
                        lo = 2 * width - 1
                        tt(dst[rows, lo:528], src[rows, lo:528], src[rows, lo - width:528 - width], ALU.add)
                        dve.drain()
                        wins.append(dst)
                        src, width = dst, 2 * width
                    for rows, win in ((slice(0, HALF), wins[-2]), (slice(HALF, P), wins[-1])):
                        stt(yT[rows, 2 + m, 16:SEQ], win[rows, 32:528], inv_w[rows, m:m + 1], U0[rows, 32:528],
                            ALU.mult, ALU.subtract)
                        tt(yT[rows, 2 + m, 0:16], win[rows, 16:32], inv_n[rows, m], ALU.mult)
                    dve.drain()
                    tt(yT[:, 2 + m, 0:16], yT[:, 2 + m, 0:16], U0[:, 16:32], ALU.subtract)
                    dve.drain()
                    dve.nop().then_inc(S["u_free"], 1)
                    dve.nop().then_inc(S["pooled_ready"], 1)
                for t in range(NT):
                    dve.wait_ge(S["qkA_copied"], done(l, "qkA_copied", t + 1))
                    nc.vector.tensor_reduce(ssqA[:, t, 0:4].unsqueeze(2),
                                            sqY[:, 0:384].rearrange("p (h d) -> p h d", h=4), AX_X, ALU.add)
                    nc.vector.tensor_reduce(ssqA[:, t, 4:8].unsqueeze(2),
                                            sqY[:, 384:640].rearrange("p (h d) -> p h d", h=4), AX_X, ALU.add)
                    signal("qkA_reduced")
                for t in range(NT):
                    bank = emptied(dve, l, ("cT", t))
                    ts(kTC[:, t * P:(t + 1) * P], bank[:, 2 * P:3 * P], g_qk[:, 3:4], None,
                       ALU.mult).then_inc(freed(("cT", t)), 1)
                    signal("cT_ready")
                for t in range(NT):
                    ts(ssqA[:, t, 4:8], ssqA[:, t, 4:8], ssq_kr[:, t:t + 1], None, ALU.add)
                dve.drain()
                mean_eps(stat[:, 0:32], flat(ssqA), QK)
                rsqrt(flat(ssqA), stat[:, 0:32], 32)
                ts(ssqA[:, :, 0:4], ssqA[:, :, 0:4], QK ** -0.5, None, ALU.mult)
                dve.drain()
                for t in range(NT):
                    q, k, kr_ = qkA[:, t, 0:4], qkA[:, t, 4:8, 0:NOPE], qkA[:, t, 4:8, NOPE:QK]
                    tt(q, q, ssqA[:, t, 0:4].unsqueeze(2).to_broadcast([P, 4, QK]), ALU.mult)
                    tt(k, k, ssqA[:, t, 4:8].unsqueeze(2).to_broadcast([P, 4, NOPE]), ALU.mult)
                    tt(kr_, krot[:, t].unsqueeze(1).to_broadcast([P, 4, ROPE]),
                       ssqA[:, t, 4:8].unsqueeze(2).to_broadcast([P, 4, ROPE]), ALU.mult)
                    dve.drain()
                    rotate(q[:, :, NOPE:QK], q[:, :, NOPE:QK], rope_q[:, t], 4, rope_t[:])
                    signal("qkA_ready")

                def conv_in(i, name):
                    dve.wait_ge(S["c_ready"], done(l, "c_ready", i + 1))
                    bank = full(dve, l, name)
                    nc.vector.memset(U1[:, 0:2], 0.0)
                    tt(U1[:, 2:514], bank, U0[:, 0:SEQ], ALU.mult).then_inc(freed(name), 1)
                    signal("z_done")
                    if i > 0:
                        dve.wait_ge(S["sqY_ready"], done(l, "sqY_ready", 2 + i))
                    ts(U2[:, 0:SEQ], U1[:, 0:SEQ], conv_w[:, 0, i:i + 1], conv_b[:, i:i + 1], ALU.mult, ALU.add)
                    for k in (1, 2):
                        dve.drain()
                        stt(U2[:, 0:SEQ], U1[:, k:k + SEQ], conv_w[:, k, i:i + 1], U2[:, 0:SEQ], ALU.mult, ALU.add)
                    dve.drain()

                def conv_gate(i, name):
                    bank = full(dve, l, name)
                    tt(U2[:, 0:SEQ], bank, U2[:, 0:SEQ], ALU.mult).then_inc(freed(name), 1)
                    signal("yD_ready")
                    ts(yT[:, 2 + i], U2[:, 0:SEQ], g_out[:, 2 + i:3 + i], None, ALU.mult)
                    signal("yT_ready")

                def pool_out(m):
                    bank = emptied(dve, l, ("pool", m))
                    ts(yT[:, m], bank, pool_s[:, 2 + m:3 + m], None, ALU.mult).then_inc(freed(("pool", m)), 1)
                    signal("yT_ready")

                def key_transposed(t):
                    bank = full(dve, l, ("kAT", t))
                    ts(kTA[0:QK, :, t * P:(t + 1) * P], bank[0:QK].rearrange("p (h m) -> p h m", h=4),
                       g_qk[0:QK, 1:2], None, ALU.mult).then_inc(freed(("kAT", t)), 1)
                    signal("qkAT_ready")

                conv_in(0, ("D", 1))
                pool_out(0)
                pool_out(1)
                evacuate_stat(l, 0)
                evacuate_stat(l, 1)
                conv_gate(0, ("D", 2))
                key_transposed(0)
                key_transposed(1)
                key_transposed(2)
                key_transposed(3)
                conv_in(1, ("D", 4))
                evacuate_stat(l, 2)
                conv_gate(1, ("D", 5))
                evacuate_stat(l, 3)
                attend(l, units, 0)

                dve.drain()
                v = ssqY[:].rearrange("p (g m) t -> p g m t", m=2)
                tt(v[:, :, 0], v[:, :, 0], v[:, :, 1], ALU.add)
                dve.drain()
                mean_eps(stat[:, 0:16].rearrange("p (g t) -> p g t", g=NG), v[:, :, 0], GW)
                rsqrt(flat(rstdY), stat[:, 0:16], 16)
                for t in range(NT):
                    for g in range(NG):
                        for h in range(2):
                            bank = full(dve, l, ("mix", t, g, h))
                            xh = X[:, t, h * 512:(h + 1) * 512]
                            stt(xh, bank, rstdY[:, g, t:t + 1], xh, ALU.mult, ALU.add
                                ).then_inc(freed(("mix", t, g, h)), 1)
                        dve.drain()
                    dve.nop().then_inc(S["x_updated"], 1)
                    if t > 0:
                        tile_rstd(l, 1, t - 1)
                        transposed(l, 1, t - 1, 1)
                tile_rstd(l, 1, NT - 1)
                transposed(l, 1, NT - 1, 1)

                for t in range(NT):
                    dve.wait_ge(S["qx_copied"], done(l, "qx_copied", t + 1))
                    nc.vector.tensor_reduce(rC[:, t, 0:4].unsqueeze(2),
                                            sqx[:, t % 2].rearrange("p (h d) -> p h d", h=4), AX_X, ALU.add)
                    signal("qx_reduced")
                mean_eps(stat[:, 0:16].rearrange("p (t h) -> p t h", t=NT), rC[:, :, 0:4], HD)
                rsqrt(stat[:, 16:32], stat[:, 0:16], 16)
                ts(stat[:, 16:32], stat[:, 16:32], HD ** -0.5, None, ALU.mult)
                dve.drain()
                for t in range(NT):
                    v = qx[:, t].rearrange("p (h d) -> p h d", h=4)
                    tt(v, v, stat[:, 16 + 4 * t:20 + 4 * t].unsqueeze(2).to_broadcast([P, 4, HD]), ALU.mult)
                    signal("qx_ready")
                attend(l, cross, len(units))
                for t in range(NT):
                    for h in range(2):
                        bank = full(dve, l, ("wo", t, h))
                        xh = X[:, t, h * 512:(h + 1) * 512]
                        tt(xh, bank, xh, ALU.add).then_inc(freed(("wo", t, h)), 1)
                    signal("x_updated")
                    if t > 0:
                        tile_rstd(l, 2, t - 1)
                        transposed(l, 2, t - 1, 2)
                tile_rstd(l, 2, NT - 1)
                transposed(l, 2, NT - 1, 2)
                dve.wait_ge(S["xhi_ready"], done(l, "xhi_ready", NT))
                for t in range(NT):
                    stt(xlo[:, t], X[:, t], rstd_x[:, t:t + 1], xhi[:, t].bitcast(F32), ALU.mult, ALU.subtract)
                signal("xlo_ready")

                def r32(i):
                    return rt[:, i].rearrange("p (t e) -> p t e", t=NT)

                def r4(i):
                    return rt[:, i, 0:16].rearrange("p (t e) -> p t e", t=NT)

                def r1(i):
                    return rt[:, i, 0:NT].unsqueeze(2)
                bank = full(dve, l, ("route",))
                lg = bank[:, 0:36 * NT].rearrange("p (t e) -> p t e", t=NT)
                tt(r4(0), lg[:, :, 0:NG], b_rt[:, 0:NG].unsqueeze(1).to_broadcast([P, NT, NG]), ALU.add)
                tt(r32(1), lg[:, :, NG:36], b_rt[:, NG:36].unsqueeze(1).to_broadcast([P, NT, NE]), ALU.add
                   ).then_inc(freed(("route",)), 1)
                dve.drain()
                nc.vector.tensor_reduce(r1(2), r4(0), AX_X, ALU.max)
                dve.drain()
                argmax_first(r4(0), NG, r1(2), r4(3), r4(4))
                tt(r4(4), r4(0), r1(2).to_broadcast([P, NT, NG]), ALU.subtract)
                ts(r4(5), r4(3), -1.0, BIG, ALU.add, ALU.mult)
                dve.drain()
                tt(r32(1).rearrange("p t (g e) -> p t g e", g=NG), r32(1).rearrange("p t (g e) -> p t g e", g=NG),
                   r4(5).unsqueeze(3).to_broadcast([P, NT, NG, EPG]), ALU.add)
                dve.drain()
                nc.vector.tensor_reduce(r1(6), r32(1), AX_X, ALU.max)
                dve.drain()
                argmax_first(r32(1), NE, r1(6), r32(7), r32(8))
                stt(r32(1), r32(7), -2.0 * BIG, r32(1), ALU.mult, ALU.add)
                dve.drain()
                nc.vector.tensor_reduce(r1(9), r32(1), AX_X, ALU.max)
                dve.drain()
                argmax_first(r32(1), NE, r1(9), r32(10), r32(8))
                tt(M16[:], r32(7), r32(10), ALU.add)
                signal("M_ready")
                tt(rt[:, 11, 0:NT], rt[:, 9, 0:NT], rt[:, 6, 0:NT], ALU.subtract)
                signal("exp_arg")
                dve.wait_ge(S["exp_done"], done(l, "exp_done", 1))
                nc.vector.tensor_reduce(r1(12), r4(4), AX_X, ALU.add)
                ts(rt[:, 13, 0:NT], rt[:, 11, 0:NT], 1.0, None, ALU.add)
                dve.drain()
                tt(rt[:, 12, 0:NT], rt[:, 12, 0:NT], rt[:, 13, 0:NT], ALU.mult)
                dve.drain()
                nc.vector.reciprocal(wk[:, 0], rt[:, 12, 0:NT])
                dve.drain()
                tt(wk[:, 1], wk[:, 0], rt[:, 11, 0:NT], ALU.mult)
                dve.drain()
                tt(W_te[:], r32(7), wk[:, 0].unsqueeze(2).to_broadcast([P, NT, NE]), ALU.mult)
                tt(r32(8), r32(10), wk[:, 1].unsqueeze(2).to_broadcast([P, NT, NE]), ALU.mult)
                dve.drain()
                tt(W_te[:], W_te[:], r32(8), ALU.add)
                bank = full(dve, l, ("rank",))
                counts = bank[:, NT * NE:NT * NE + NE]
                over = Gx[:, 0:NE * 7].rearrange("p (e k) -> p e k", k=7)
                tt(over, counts.unsqueeze(2).to_broadcast([P, NE, 7]),
                   past[:, 0:7].unsqueeze(1).to_broadcast([P, NE, 7]), ALU.is_gt)
                dve.drain()
                nc.vector.tensor_reduce(rt[:, 0, 0:NE].unsqueeze(2), over, AX_X, ALU.add)
                nc.vector.memset(rt[:, 2, 0:NE], 0.0)
                dve.drain()
                nc.vector.tensor_tensor_scan(rt[:, 3, 0:NE], rt[:, 0, 0:NE], rt[:, 2, 0:NE], 0.0, ALU.add, ALU.add)
                dve.drain()
                tt(rt[:, 2, 0:NE], rt[:, 3, 0:NE], rt[:, 0, 0:NE], ALU.subtract)
                tt(ovf_f[:, 1:2], ovf_f[:, 1:2], ovf_f[:, 0:1], ALU.add)
                over = Gx[:, 0:NE * OVF].rearrange("p (q e) -> p q e", q=OVF)
                dve.drain()
                tt(over, rt[:, 3, 0:NE].unsqueeze(1).to_broadcast([P, OVF, NE]),
                   iota[:, 0:OVF].unsqueeze(2).to_broadcast([P, OVF, NE]), ALU.is_le)
                nc.vector.tensor_copy(ovf_f[:, 0:1], rt[:, 3, NE - 1:NE])
                dve.drain()
                nc.vector.tensor_reduce(ovf_f[:, 2:2 + OVF].unsqueeze(2), over, AX_X, ALU.add)
                dve.drain()
                ts(ovf_f[:, 2:2 + OVF], ovf_f[:, 2:2 + OVF], float(NE - 1), None, ALU.min)
                dve.drain()
                nc.vector.tensor_copy(ovf[:], ovf_f[:])
                signal("route_ready")
                rank = bank[:, 0:NT * NE].rearrange("p (t e) -> p t e", t=NT)
                e32 = iota[:, 0:NE].unsqueeze(1).to_broadcast([P, NT, NE])
                o32 = rt[:, 2, 0:NE].unsqueeze(1).to_broadcast([P, NT, NE])
                for k, oh in ((0, 7), (1, 10)):
                    tt(r32(8), r32(oh), rank, ALU.mult)
                    dve.drain()
                    nc.vector.tensor_reduce(r1(4), r32(8), AX_X, ALU.add)
                    dve.drain()
                    tt(r32(8), r32(oh), e32, ALU.mult)
                    dve.drain()
                    nc.vector.tensor_reduce(r1(5), r32(8), AX_X, ALU.add)
                    dve.drain()
                    tt(r32(8), r32(oh), o32, ALU.mult)
                    dve.drain()
                    nc.vector.tensor_reduce(r1(6), r32(8), AX_X, ALU.add)
                    ts(rt[:, 12, 0:NT], rt[:, 4, 0:NT], float(SLOTS), None, ALU.is_ge)
                    dve.drain()
                    tt(rt[:, 13, 0:NT], rt[:, 6, 0:NT], rt[:, 5, 0:NT], ALU.subtract)
                    dve.drain()
                    ts(rt[:, 13, 0:NT], rt[:, 13, 0:NT], float(NE - 1), float(SLOTS), ALU.add, ALU.mult)
                    dve.drain()
                    tt(rt[:, 13, 0:NT], rt[:, 13, 0:NT], rt[:, 12, 0:NT], ALU.mult)
                    dve.drain()
                    stt(rt[:, 13, 0:NT], rt[:, 5, 0:NT], float(SLOTS), rt[:, 13, 0:NT], ALU.mult, ALU.add)
                    dve.drain()
                    tt(slot[:, k], rt[:, 4, 0:NT], rt[:, 13, 0:NT], ALU.add)
                dve.drain()
                nc.vector.tensor_copy(srel[:], slot[:])
                dve.drain()
                dve.nop().then_inc(freed(("rank",)), 1)

                with dve.Fori(0, BATCHES) as b:
                    lb = l * BATCHES + b
                    for t in range(NT):
                        ts(Gx[:], iota[:], srel[:, 0, t:t + 1], None, ALU.is_equal)
                        dve.drain()
                        stt(G[:, t], iota[:], srel[:, 1, t:t + 1], Gx[:], ALU.is_equal, ALU.add)
                        dve.drain()
                    ts(srel[:], srel[:], -float(BS), None, ALU.add)
                    signal("G_ready")
                    for c in range(1, KD, 2):
                        bank = mfull(dve, lb, ("gather", c))
                        ts(xgT[:, c], bank, gains[:, 2, c:c + 1], None, ALU.mult).then_inc(mfreed(("gather", c)), 1)
                        signal("xg_ready")
                    bank = mfull(dve, lb, ("wslot",))
                    w = bank[:, 0:2 * PPB].rearrange("p (c e) -> p c e", c=PPB)
                    nc.vector.tensor_copy(ws[0:HALF], w[0:HALF, :, 0])
                    nc.vector.tensor_copy(ws[HALF:P], w[HALF:P, :, 1]).then_inc(mfreed(("wslot",)), 1)
                    signal("ws_ready")

                    def bring_back(p):
                        dve.drain()
                        for n in range(8):
                            bank = mfull(dve, lb, ("comb", p, n))
                            xh = X[:, n // 2, (n % 2) * 512:(n % 2 + 1) * 512]
                            tt(xh, bank, xh, ALU.add).then_inc(mfreed(("comb", p, n)), 1)

                    for p in range(PPB):
                        dve.wait_ge(S["silu_ready"], mdone(lb, "silu_ready", p + 1))
                        bank = mfull(dve, lb, ("gu", p))
                        tt(hh[:], bank[:, FF:2 * FF], silu[:], ALU.mult).then_inc(mfreed(("gu", p)), 1)
                        signal("hh_ready")
                        if p > 0:
                            bring_back(p - 1)
                        for h in range(2):
                            dve.wait_ge(S["yhi_ready"], mdone(lb, "yhi_ready", 2 * p + h + 1))
                            bank = mfull(dve, lb, ("down", p, h))
                            c = slice(h * 512, (h + 1) * 512)
                            stt(ylo[:, p % 2, c], bank, ws[:, p:p + 1], yhi[:, p % 2, c].bitcast(F32),
                                ALU.mult, ALU.subtract).then_inc(mfreed(("down", p, h)), 1)
                            signal("ylo_ready")
                    bring_back(PPB - 1)

                n_ovf = dve.value_load(ovf[0:1, 0:1], min_val=0, max_val=OVF - 1)
                before = dve.value_load(ovf[0:1, 1:2], min_val=0, max_val=DEPTH * OVF)
                with dve.If(n_ovf > 0):
                    with dve.Fori(0, n_ovf) as q:
                        tile = before + q

                        def step():
                            dve.drain()
                            dve.nop().then_inc(ovf_dve, 1)
                        dve.drain()
                        for t in range(NT):
                            io = iota[:, 0:SLOTS]
                            ts(Gx[:, 0:SLOTS], io, srel[:, 0, t:t + 1], None, ALU.is_equal)
                            ts(Gx[:, SLOTS:2 * SLOTS], io, srel[:, 1, t:t + 1], None, ALU.is_equal)
                            dve.drain()
                            tt(Gq[:, t], Gx[:, 0:SLOTS], Gx[:, SLOTS:2 * SLOTS], ALU.add)
                            ts(Gx[:, 2 * SLOTS:3 * SLOTS], Gx[:, 0:SLOTS], wk[:, 0, t:t + 1], None, ALU.mult)
                            dve.drain()
                            stt(Gw[:, t], Gx[:, SLOTS:2 * SLOTS], wk[:, 1, t:t + 1], Gx[:, 2 * SLOTS:3 * SLOTS],
                                ALU.mult, ALU.add)
                            dve.drain()
                        ts(srel[:], srel[:], -float(SLOTS), None, ALU.add)
                        step()
                        dve.wait_ge(ovf_pe, tile * OVF_PE + 1)
                        g = gains[:, 2].unsqueeze(2).to_broadcast([P, KD, SLOTS])
                        tt(xgq[:], ps[:, 0, :].rearrange("p (c s) -> p c s", c=KD), g, ALU.mult)
                        dve.wait_ge(ovf_pe, tile * OVF_PE + 2)
                        nc.vector.tensor_copy(Wq[0:SLOTS], ps[0:SLOTS, 1, :])
                        step()
                        nc.vector.tensor_copy(wsq[0:SLOTS], ps[0:SLOTS, 2, 0:1])
                        step()
                        dve.wait_ge(ovf_act, tile * OVF_ACT + 1)
                        tt(hh[0:SLOTS], ps[0:SLOTS, 4, FF:2 * FF], silu[0:SLOTS], ALU.mult)
                        step()
                        dve.wait_ge(ovf_pe, tile * OVF_PE + 4)
                        nc.vector.tensor_copy(hhT[:, :, 0:SLOTS], ps[:, 5, 0:2 * SLOTS].rearrange("p (c s) -> p c s", c=2))
                        step()
                        dve.wait_ge(ovf_act, tile * OVF_ACT + 2)
                        for h in range(2):
                            c = slice(h * 512, (h + 1) * 512)
                            stt(ylo[0:SLOTS, 1, c], ps[0:SLOTS, 6 + h, :], wsq[0:SLOTS], yhi[0:SLOTS, 0, c].bitcast(F32),
                                ALU.mult, ALU.subtract)
                        step()
                        for part in range(2):
                            dve.wait_ge(ovf_pe, tile * OVF_PE + 6 + part)
                            for n in range(4 * part, 4 * part + 4):
                                xh = X[:, n // 2, (n % 2) * 512:(n % 2 + 1) * 512]
                                tt(xh, ps[:, n % 4, :], xh, ALU.add)
                            step()
                signal("layer_done")

        @block.tensor
        def _(pe):
            mm = nc.tensor.matmul
            opened = []

            def bank_of(l, name):
                opened.append(name)
                bank, _, before = dense.job[name]
                pe.wait_ge(bank_free[bank], l * dense.free[bank] + before + 1)
                return ps[:, bank, :]

            def filled(name):
                return bank_full[dense.job[name][0]]

            def mbank_of(lb, name):
                bank, _, before = moe.job[name]
                pe.wait_ge(moe_free[bank], lb * moe.free[bank] + before + 1)
                return ps[:, bank, :]

            def mfilled(name):
                return moe_full[moe.job[name][0]]

            def flip(out_, in_):
                k = in_.shape[0]
                return nc.tensor.transpose(out_, in_, ident[0:k, 0:k])

            def transpose_tile(l, s, t):
                pe.wait_ge(S["xn_ready"], done(l, "xn_ready", NT * s + t + 1))
                for h in range(2):
                    bank = bank_of(l, ("xT", s, t, h))
                    for c in range(4):
                        last = flip(bank[:, c * P:(c + 1) * P], xn[:, t % 2, 4 * h + c::KD])
                    last.then_inc(filled(("xT", s, t, h)), 1)

            def tokens(l, name, lhs, t, w, c0, c1, n=0):
                bank = bank_of(l, name)
                for c in range(KD):
                    last = mm(bank[:, n:n + c1 - c0], lhs[:, c, t * P:(t + 1) * P], w[:, c, c0:c1],
                              start=c == 0, stop=c == KD - 1)
                last.then_inc(filled(name), 1)

            def channels(l, name, w, c0):
                bank = bank_of(l, name)
                for c in range(KD):
                    last = mm(bank, w[:, c, c0:c0 + P], hT[:, c, :], start=c == 0, stop=c == KD - 1)
                last.then_inc(filled(name), 1)

            def attend(l, list_, first):
                obank = {}
                for n in range(len(list_) + 3):
                    if n < len(list_):
                        kind, pair, t, nk = list_[n]
                        L = nk * P
                        q = slice(t * P, (t + 1) * P)
                        for h in range(2):
                            bank = bank_of(l, ("S", list_[n], h))
                            if kind == "mla":
                                head = 2 * pair + h
                                lhs, rhs = qTA[0:QK, head, q], kTA[0:QK, head, 0:L]
                            elif kind == "swa":
                                rows = slice(h * HD, (h + 1) * HD)
                                lhs, rhs = qTC[rows, pair, q], kTC[rows, (t + 1) * P - L:(t + 1) * P]
                            else:
                                rows = slice(h * HD, (h + 1) * HD)
                                lhs, rhs = qTx[rows, pair, q], kTx[rows, pair, 0:L]
                            last = mm(bank[:, 0:L], lhs, rhs, start=True, stop=kind == "xa")
                            if kind == "swa" and nk == 2:
                                mm(bank[:, 0:P], ident16[:], before16[:], start=False, stop=False)
                            if kind != "xa":
                                last = mm(bank[:, L - P:L], ident16[:], causal16[:], start=False, stop=True)
                            last.then_inc(filled(("S", list_[n], h)), 1)
                    if 1 <= n <= len(list_):
                        nk = list_[n - 1][3]
                        pe.wait_ge(S["pn_ready"], done(l, "pn_ready", first + n))
                        for h in range(2):
                            bank = bank_of(l, ("T", list_[n - 1], h))
                            for j in range(nk):
                                last = flip(bank[:, j * P:(j + 1) * P], Pr[:, (n - 1) % 2, h, j * P:(j + 1) * P])
                            last.then_inc(filled(("T", list_[n - 1], h)), 1)
                    if 2 <= n <= len(list_) + 1:
                        kind, pair, t, nk = list_[n - 2]
                        for h in range(2):
                            emptied(pe, l, ("T", list_[n - 2], h))
                        if t == 0:
                            obank = bank_of(l, ("O", kind, pair))
                        for h in range(2):
                            for j in range(nk):
                                if kind == "mla":
                                    head = 2 * pair + h
                                    v = vA[:, j, head * HD:(head + 1) * HD]
                                elif kind == "swa":
                                    v = vC[:, t + 1 - nk + j, h * HD:(h + 1) * HD]
                                else:
                                    head = 2 * pair + h
                                    v = vX[:, j, head * HD:(head + 1) * HD]
                                last = mm(obank[h * HD:(h + 1) * HD, t * P:(t + 1) * P], v,
                                          PT[:, n % 2, h, j * P:(j + 1) * P], start=j == 0, stop=j == nk - 1)
                        if t == NT - 1:
                            last.then_inc(filled(("O", kind, pair)), 1)
                    if n >= 3 and list_[n - 3][2] == NT - 1 and list_[n - 3][0] != "xa":
                        summed = {6: 5, 7: 6, 4: 7, 5: 8}[stat_of(list_[n - 3])]
                        sum_channels(l, stat_of(list_[n - 3]), summed, sqO[:, list_[n - 3][1]])

            def sum_channels(l, c, n, sq):
                pe.wait_ge(S["sqY_ready"], done(l, "sqY_ready", n))
                bank = bank_of(l, ("stY", c))
                for t in range(NT):
                    last = mm(bank[:, t:t + 1], sq[:, t * P:(t + 1) * P], ones[:, 0:1], start=True, stop=True)
                last.then_inc(filled(("stY", c)), 1)

            pe.wait_ge(init_pool, 1)
            with pe.Fori(0, DEPTH) as l:
                for i in range(NM):
                    pe.wait_ge(S["memx_ready"], done(l, "memx_ready", i + 1))
                    for h in range(2):
                        bank = bank_of(l, ("memT", i, h))
                        for c in range(4):
                            last = flip(bank[:, c * P:(c + 1) * P], memx[:, i, 4 * h + c::KD])
                        last.then_inc(filled(("memT", i, h)), 1)
                ring0_wait(pe, l, 1)
                for i in range(NM):
                    pe.wait_ge(S["hmT_ready"], done(l, "hmT_ready", 2 * i + 2))
                    tokens(l, ("kvx", i), hmT, i, ring0, 0, 512)
                for t in range(NT):
                    transpose_tile(l, 0, t)
                ring1_wait(pe, l, 2)
                for t in range(NT):
                    pe.wait_ge(S["hT_ready"], done(l, "hT_ready", 2 * t + 2))
                    tokens(l, ("uC", t, 0), hT, t, ring1, 0, ROPE + GW)
                    tokens(l, ("uC", t, 1), hT, t, ring1, ROPE + GW, 544)
                for i in range(NM):
                    pe.wait_ge(S["kx_ready"], done(l, "kx_ready", i + 1))
                    bank = bank_of(l, ("kxT", i))
                    for c in range(2):
                        last = flip(bank[:, c * P:(c + 1) * P], knx[:, i, c * P:(c + 1) * P])
                    last.then_inc(filled(("kxT", i)), 1)
                ring0_wait(pe, l, 2)
                for m in range(3):
                    channels(l, ("A", m), ring0, m * P)
                pe.wait_ge(S["sqA_ready"], done(l, "sqA_ready", 3))
                bank = bank_of(l, ("stA",))
                for t in range(NT):
                    q = slice(t * P, (t + 1) * P)
                    mm(bank[:, 2 * t:2 * t + 1], sqA[:, 0, q], ones[:, 0:1], start=True, stop=False)
                    mm(bank[:, 2 * t:2 * t + 1], sqA[:, 1, q], ones[:, 0:1], start=False, stop=True)
                    last = mm(bank[:, 2 * t + 1:2 * t + 2], sqA[:, 2, q], ones[:, 0:1], start=True, stop=True)
                last.then_inc(filled(("stA",)), 1)
                ring1_wait(pe, l, 4)
                for m in range(2):
                    channels(l, ("B", m), ring1, m * P)
                pe.wait_ge(S["cqT_ready"], done(l, "cqT_ready", 3))
                pe.wait_ge(params_in, (l + 1) * PARAM_DMAS * 16)
                for t in range(NT):
                    q = slice(t * P, (t + 1) * P)
                    bank = bank_of(l, ("qA", t))
                    mm(bank[:, 0:384], cqT[:, 0, q], w_uq[:, 0, :], start=True, stop=False)
                    mm(bank[:, 0:384], cqT[:, 1, q], w_uq[:, 1, :], start=False, stop=True
                       ).then_inc(filled(("qA", t)), 1)
                    bank = bank_of(l, ("kvA", t))
                    mm(bank, cqT[:, 2, q], w_ukv[:], start=True, stop=True).then_inc(filled(("kvA", t)), 1)
                for t in range(NT):
                    pe.wait_ge(S["qC_ready"], done(l, "qC_ready", t + 1))
                    bank = bank_of(l, ("cT", t))
                    for c in range(3):
                        last = flip(bank[:, c * P:(c + 1) * P], qkC[:, t, c * P:(c + 1) * P])
                    last.then_inc(filled(("cT", t)), 1)

                def pool_map(m):
                    pe.wait_ge(S["pooled_ready"], done(l, "pooled_ready", m + 1))
                    bank = bank_of(l, ("pool", m))
                    mm(bank, pool_w[:, m, :], yT[:, 2 + m, :], start=True, stop=True
                       ).then_inc(filled(("pool", m)), 1)

                def heads_transposed(t):
                    pe.wait_ge(S["qkA_ready"], done(l, "qkA_ready", t + 1))
                    bank = bank_of(l, ("qAT", t))
                    for h in range(4):
                        last = flip(bank[0:QK, h * P:(h + 1) * P], qkA[:, t, h])
                    last.then_inc(filled(("qAT", t)), 1)
                    bank = bank_of(l, ("kAT", t))
                    for h in range(4):
                        last = flip(bank[0:QK, h * P:(h + 1) * P], qkA[:, t, 4 + h])
                    last.then_inc(filled(("kAT", t)), 1)

                channels(l, ("D", 0), ring1, GW)
                pool_map(0)
                ring0_wait(pe, l, 4)
                channels(l, ("D", 1), ring0, 0)
                pool_map(1)
                sum_channels(l, 0, 1, sqY)
                channels(l, ("D", 2), ring0, GW)
                sum_channels(l, 1, 2, sqY)
                heads_transposed(0)
                heads_transposed(1)
                channels(l, ("D", 3), ring1, GW + P)
                channels(l, ("D", 4), ring0, P)
                heads_transposed(2)
                heads_transposed(3)
                sum_channels(l, 2, 3, sqY)
                channels(l, ("D", 5), ring0, GW + P)
                sum_channels(l, 3, 4, sqY)
                pe.wait_ge(S["cT_ready"], done(l, "cT_ready", 2 * NT))
                pe.wait_ge(S["qkAT_ready"], done(l, "qkAT_ready", 2 * NT))
                attend(l, units, 0)

                pe.wait_ge(S["yT_ready"], done(l, "yT_ready", 8))
                ring0_wait(pe, l, 9)
                ring1_wait(pe, l, 9)
                block_of = {0: 4, 1: 0, 2: 6, 3: 2}
                for t in range(NT):
                    for g in range(NG):
                        for h in range(2):
                            bank = bank_of(l, ("mix", t, g, h))
                            w = (ring1, ring0)[h]
                            for j in range(2):
                                c = 2 * g + j
                                last = mm(bank, yT[:, c, t * P:(t + 1) * P], w[:, c, 0:512], start=j == 0, stop=j == 1)
                            last.then_inc(filled(("mix", t, g, h)), 1)
                    if t > 0:
                        transpose_tile(l, 1, t - 1)
                transpose_tile(l, 1, NT - 1)
                ring1_wait(pe, l, 12)
                for t in range(NT):
                    pe.wait_ge(S["hT_ready"], done(l, "hT_ready", 2 * NT + 2 * t + 2))
                    tokens(l, ("qx", t), hT, t, ring1, 0, GW)
                for t in range(NT):
                    pe.wait_ge(S["qx_ready"], done(l, "qx_ready", t + 1))
                    bank = bank_of(l, ("qxT", t))
                    for c in range(2):
                        last = flip(bank[:, c * P:(c + 1) * P], qx[:, t, c * P:(c + 1) * P])
                    last.then_inc(filled(("qxT", t)), 1)
                pe.wait_ge(S["xa_kv_ready"], done(l, "xa_kv_ready", 2 * NM))
                pe.wait_ge(S["qxT_ready"], done(l, "qxT_ready", NT))
                attend(l, cross, len(units))
                pe.wait_ge(S["oTx_ready"], done(l, "oTx_ready", 2))
                for t in range(NT):
                    for h in range(2):
                        bank = bank_of(l, ("wo", t, h))
                        for c in range(2):
                            r = 4 * c + 2 * h
                            last = mm(bank, oTx[:, c, t * P:(t + 1) * P], ring1[:, r:r + 2, 272:528],
                                      start=c == 0, stop=c == 1)
                        last.then_inc(filled(("wo", t, h)), 1)
                    if t > 0:
                        transpose_tile(l, 2, t - 1)
                transpose_tile(l, 2, NT - 1)

                bank = bank_of(l, ("route",))
                for t in range(NT):
                    pe.wait_ge(S["hT_ready"], done(l, "hT_ready", 4 * NT + 2 * t + 2))
                    for c in range(KD):
                        last = mm(bank[:, 36 * t:36 * (t + 1)], hT[:, c, t * P:(t + 1) * P], w_rt[:, c, :],
                                  start=c == 0, stop=c == KD - 1)
                last.then_inc(filled(("route",)), 1)
                pe.wait_ge(S["M_ready"], done(l, "M_ready", 1))
                bank = bank_of(l, ("rank",))
                for t in range(NT):
                    for j in range(t + 1):
                        mm(bank[:, t * NE:(t + 1) * NE], (earlier16 if j == t else ones16)[:], M16[:, j, :],
                           start=j == 0, stop=j == t)
                for j in range(NT):
                    last = mm(bank[:, NT * NE:(NT + 1) * NE], ones16[:], M16[:, j, :], start=j == 0, stop=j == NT - 1)
                last.then_inc(filled(("rank",)), 1)
                wait_apart(pe, S["xhi_ready"], done(l, "xhi_ready", NT))
                wait_apart(pe, S["xlo_ready"], done(l, "xlo_ready", 1))
                wait_apart(pe, S["route_ready"], l + 1)

                with pe.Fori(0, BATCHES) as b:
                    lb = l * BATCHES + b
                    pe.wait_ge(S["G_ready"], mdone(lb, "G_ready", 1))
                    for c in range(KD):
                        bank = mbank_of(lb, ("gather", c))
                        for t in range(NT):
                            mm(bank, xhi[:, t, c::KD], G[:, t], start=t == 0, stop=False)
                            last = mm(bank, xlo[:, t, c::KD], G[:, t], start=False, stop=t == NT - 1)
                        last.then_inc(mfilled(("gather", c)), 1)
                    pe.drain()
                    pe.nop().then_inc(S["gathered"], 1)
                    bank = mbank_of(lb, ("wslot",))
                    for p in range(PPB):
                        for t in range(NT):
                            last = mm(bank[:, 2 * p:2 * p + 2], G[:, t, p * P:(p + 1) * P].bitcast(F32),
                                      W_te[:, t, bass.ds(b * 2 * PPB + 2 * p, 2)], start=t == 0, stop=t == NT - 1)
                    last.then_inc(mfilled(("wslot",)), 1)
                    pe.wait_ge(S["xg_ready"], mdone(lb, "xg_ready", KD))

                    def bring_back(p, part):
                        for n in range(4 * part, 4 * part + 4):
                            bank = mbank_of(lb, ("comb", p, n))
                            w = Wt[:, p % 2, (n // 2) * P:(n // 2 + 1) * P]
                            c = slice((n % 2) * 512, (n % 2 + 1) * 512)
                            mm(bank, w, yhi[:, p % 2, c], start=True, stop=False)
                            mm(bank, w, ylo[:, p % 2, c], start=False, stop=True).then_inc(mfilled(("comb", p, n)), 1)

                    for p in range(PPB):
                        bank = mbank_of(lb, ("GT", p))
                        for t in range(NT):
                            last = flip(bank[:, t * P:(t + 1) * P], G[:, t, p * P:(p + 1) * P].bitcast(F32))
                        last.then_inc(mfilled(("GT", p)), 1)
                        bank = mbank_of(lb, ("gu", p))
                        for s in (2 * (p % 2), 2 * (p % 2) + 1):
                            pe.wait_ge(slot_in[s], (lb * (PPB // 2) + p // 2 + 1) * 48)
                        for c in range(KD):
                            for j in range(2):
                                r = slice(j * SLOTS, (j + 1) * SLOTS)
                                last = mm(bank[r], xgT[:, c, p * P + j * SLOTS:p * P + (j + 1) * SLOTS],
                                          wgu[2 * (p % 2) + j][:, :, c, :], start=c == 0, stop=c == KD - 1)
                        last.then_inc(mfilled(("gu", p)), 1)
                        if p > 0:
                            pe.wait_ge(S["ylo_ready"], mdone(lb, "ylo_ready", 2 * p))
                            bring_back(p - 1, 0)
                        pe.wait_ge(S["hh_ready"], mdone(lb, "hh_ready", p + 1))
                        bank = mbank_of(lb, ("hhT", p))
                        for c in range(2):
                            last = flip(bank[:, c * P:(c + 1) * P], hh[:, c::2])
                        last.then_inc(mfilled(("hhT", p)), 1)
                        if p > 0:
                            bring_back(p - 1, 1)
                        pe.wait_ge(S["hhT_ready"], mdone(lb, "hhT_ready", p + 1))
                        for h in range(2):
                            bank = mbank_of(lb, ("down", p, h))
                            for c in range(2):
                                for j in range(2):
                                    r = slice(j * SLOTS, (j + 1) * SLOTS)
                                    last = mm(bank[r], hhT[:, c, r], wdn[2 * (p % 2) + j][:, c, h * 512:(h + 1) * 512],
                                              start=c == 0, stop=c == 1)
                            last.then_inc(mfilled(("down", p, h)), 1)
                        pe.drain()
                        pe.nop().then_inc(slots_read[p % 2], 1)
                    pe.wait_ge(S["Wt_ready"], mdone(lb, "Wt_ready", PPB))
                    pe.wait_ge(S["ylo_ready"], mdone(lb, "ylo_ready", 2 * PPB))
                    bring_back(PPB - 1, 0)
                    bring_back(PPB - 1, 1)

                n_ovf = pe.value_load(ovf[0:1, 0:1], min_val=0, max_val=OVF - 1)
                before = pe.value_load(ovf[0:1, 1:2], min_val=0, max_val=DEPTH * OVF)
                with pe.If(n_ovf > 0):
                    with pe.Fori(0, n_ovf) as q:
                        tile = before + q
                        pe.wait_ge(ovf_dve, tile * OVF_DVE + 1)
                        for c in range(KD):
                            for t in range(NT):
                                o_ = ps[:, 0, c * SLOTS:(c + 1) * SLOTS]
                                mm(o_, xhi[:, t, c::KD], Gq[:, t], start=t == 0, stop=False)
                                last = mm(o_, xlo[:, t, c::KD], Gq[:, t], start=False, stop=t == NT - 1)
                        last.then_inc(ovf_pe, 1)
                        for t in range(NT):
                            flip(ps[0:SLOTS, 1, t * P:(t + 1) * P], Gq[:, t].bitcast(F32))
                        for t in range(NT):
                            last = mm(ps[0:SLOTS, 2, 0:1], Gw[:, t], ones[:, 0:1], start=t == 0, stop=t == NT - 1)
                        last.then_inc(ovf_pe, 1)
                        pe.wait_ge(ovf_dve, tile * OVF_DVE + 2)
                        pe.wait_ge(ovf_w, (tile + 1) * 48)
                        for c in range(KD):
                            last = mm(ps[0:SLOTS, 4, :], xgq[:, c, :], wgu[0][:, :, c, :], start=c == 0, stop=c == KD - 1)
                        last.then_inc(ovf_pe, 1)
                        wait_apart(pe, ovf_dve, tile * OVF_DVE + 4)
                        for c in range(2):
                            last = flip(ps[:, 5, c * SLOTS:(c + 1) * SLOTS], hh[0:SLOTS, c::2])
                        last.then_inc(ovf_pe, 1)
                        pe.wait_ge(ovf_dve, tile * OVF_DVE + 5)
                        for h in range(2):
                            for c in range(2):
                                last = mm(ps[0:SLOTS, 6 + h, :], hhT[:, c, 0:SLOTS], wdn[0][:, c, h * 512:(h + 1) * 512],
                                          start=c == 0, stop=c == 1)
                        last.then_inc(ovf_pe, 1)
                        pe.wait_ge(ovf_dve, tile * OVF_DVE + 6)
                        for part in range(2):
                            if part:
                                pe.wait_ge(ovf_dve, tile * OVF_DVE + 7)
                            for n in range(4 * part, 4 * part + 4):
                                w = Wq[0:SLOTS, (n // 2) * P:(n // 2 + 1) * P]
                                c = slice((n % 2) * 512, (n % 2 + 1) * 512)
                                mm(ps[:, n % 4, :], w, yhi[0:SLOTS, 0, c], start=True, stop=False)
                                last = mm(ps[:, n % 4, :], w, ylo[0:SLOTS, 1, c], start=False, stop=True)
                            last.then_inc(ovf_pe, 1)
            assert opened == dense.order, "the plan's order is the program's"


_INS = ["x", "mem", "positions", "norm_mix", "w_in", "mla_g_cq", "mla_w_uq", "mla_g_ckv", "mla_w_ukv",
        "mla_g_q", "mla_g_k", "pool_w", "pool_scale", "swa_g_q", "swa_g_k", "swa_sinks", "conv_w", "conv_b",
        "mix_out_norm", "w_mix_out", "norm_xa", "norm_mem", "xa_w_q", "xa_w_kv", "xa_g_q", "xa_g_k", "xa_w_o",
        "norm_ffn", "w_group", "b_group", "w_expert", "b_expert", "w_gate", "w_up", "w_down"]


def kernel(**inputs):
    import numpy as _np
    import concourse.bacc as _bacc
    from concourse import mybir as _mybir
    from concourse.bass_utils import run_bass_kernel_spmd as _run

    nc = _bacc.Bacc("TRN2", target_bir_lowering=False, num_devices=1)
    arrays, views = {}, {}
    for name in _INS:
        arr = _np.ascontiguousarray(inputs[name])
        arrays[f"in_{name}"] = arr
        views[name] = nc.dram_tensor(f"in_{name}", arr.shape, _mybir.dt.from_np(arr.dtype), kind="ExternalInput").ap()
    out = nc.dram_tensor("out_0", (1, SEQ, D), F32, kind="ExternalOutput").ap()
    build(nc, views, out)
    r = _run(nc, [arrays], core_ids=[0])
    return r.results[0]["out_0"]
```

```python
from contextlib import ExitStack

import concourse.bass as bass
from concourse import mybir
import math
import numpy as np

ALU = mybir.AluOpType
ACT = mybir.ActivationFunctionType
F32 = mybir.dt.float32
F32R = mybir.dt.float32r
BF16 = mybir.dt.bfloat16
I32 = mybir.dt.int32
AX_X = mybir.AxisListType.X

P = 128
SEQ = 512
D = 1024
DEPTH = 2
KD = D // P
NT = SEQ // P
MEM = 256
NM = MEM // P
EPS = 1e-6
GW = 256
HD = 64
QK = 96
ROPE = 32
NOPE = 64
QR = 256
KVR = 128
THETA = 10000.0
WINDOWS = (2, 4, 8, 16)
C_B = QR + KVR + ROPE
C_C = C_B + GW
C_D = C_C + 2 * GW
NG = 4
MIX_ORDER = (0, 1, 3, 2)
NE = 32
EPG = NE // NG
FF = 256
SLOTS = 64
PAIRS = NE // 2
OVF = 16
NEG = -1e30
BIG = 1e30

HALF = P // 2
TWO_PI = 2.0 * math.pi
PI_A = 6.28125
PI_B = float(np.float32(np.round((TWO_PI - PI_A) * 2 ** 21) / 2 ** 21))
PI_C = TWO_PI - PI_A - PI_B
PI_MAX = float(np.nextafter(np.float32(math.pi), np.float32(0)))
ROUND = 12582912.0
RSQRT_MAGIC = float(0x5F3759DF)


class Banks:

    def __init__(self):
        self.full = [0] * 8
        self.free = [0] * 8
        self.job = {}
        self.order = []

    def use(self, name, bank, frees=1):
        self.full[bank] += 1
        self.job[name] = (bank, self.full[bank], self.free[bank])
        self.free[bank] += frees
        self.order.append(name)


def attention_units():
    units = []
    for pair in range(2):
        for t in range(NT):
            units.append(("swa", pair, t, 1 if t == 0 else 2))
    for pair in range(2):
        for t in range(NT):
            units.append(("mla", pair, t, t + 1))
    return units


def cross_units():
    return [("xa", pair, t, NM) for pair in range(2) for t in range(NT)]


def dense_plan(units, cross):
    b = Banks()
    for i in range(NM):
        for h in range(2):
            b.use(("memT", i, h), 2 * i + h)
    for i in range(NM):
        b.use(("kvx", i), 4 + i, frees=2)
    for t in range(NT):
        for h in range(2):
            b.use(("xT", 0, t, h), 2 * (t % 2) + h)
    for t in range(NT):
        b.use(("uC", t, 0), 2 * (t % 2))
        b.use(("uC", t, 1), 2 * (t % 2) + 1)
    for i in range(NM):
        b.use(("kxT", i), 4 + i)
    for m in range(3):
        b.use(("A", m), 6 - m % 2, frees=2)
    b.use(("stA",), 7)
    for m in range(2):
        b.use(("B", m), m)
    for t in range(NT):
        b.use(("qA", t), 4 + 2 * (t % 2))
        b.use(("kvA", t), 5 + 2 * (t % 2))
    for t in range(NT):
        b.use(("cT", t), t, frees=2)
    b.use(("D", 0), 4)
    b.use(("pool", 0), 5, frees=2)
    b.use(("D", 1), 6)
    b.use(("pool", 1), 7, frees=2)
    b.use(("stY", 0), 0)
    b.use(("D", 2), 4)
    b.use(("stY", 1), 1)
    for t in range(2):
        b.use(("qAT", t), 2)
        b.use(("kAT", t), 3)
    b.use(("D", 3), 5)
    b.use(("D", 4), 6)
    for t in range(2, NT):
        b.use(("qAT", t), 2)
        b.use(("kAT", t), 3)
    b.use(("stY", 2), 0)
    b.use(("D", 5), 4)
    b.use(("stY", 3), 1)
    plan_units(b, units)
    for t in range(NT):
        for k, g in enumerate(MIX_ORDER):
            for h in range(2):
                b.use(("mix", t, g, h), (2 * k + h) % 6)
            if t == 0 and k == 1:
                b.use(("stY", 5), 6)
        if t > 0:
            for h in range(2):
                b.use(("xT", 1, t - 1, h), 6 + h)
    b.use(("qx", 0), 0)
    for h in range(2):
        b.use(("xT", 1, NT - 1, h), 6 + h)
    for t in range(1, NT):
        b.use(("qx", t), t)
    for t in range(NT):
        b.use(("qxT", t), 4 + t % 2)
    plan_units(b, cross)
    for t in range(NT):
        for h in range(2):
            b.use(("wo", t, h), 2 * (t % 2) + h)
        if t > 0:
            for h in range(2):
                b.use(("xT", 2, t - 1, h), 6 + h)
    b.use(("route",), 0)
    for h in range(2):
        b.use(("xT", 2, NT - 1, h), 6 + h)
    b.use(("rank",), 1)
    return b


def plan_units(b, units):
    for n in range(len(units) + 5):
        if n < len(units):
            for a in range(2):
                b.use(("S", units[n], a), 2 * (n % 2) + a)
        if 2 <= n <= len(units) + 1:
            for a in range(2):
                b.use(("T", units[n - 2], a), 4 + a)
        if 3 <= n <= len(units) + 2 and units[n - 3][2] == 0:
            kind, pair = units[n - 3][:2]
            b.use(("O", kind, pair), 6 + pair, frees=1 if kind == "xa" else 2)
        if pair_statistics(units, n - 5):
            b.use(("stY", stat_of(units[n - 5])), 4)


def pair_statistics(units, m):
    return 0 <= m < len(units) - 1 and units[m][2] == NT - 1 and units[m][0] != "xa"


def stat_of(unit):
    return {"mla": 4, "swa": 6}[unit[0]] + unit[1]


def moe_plans():
    head, step, tail = Banks(), Banks(), Banks()
    for h in range(2):
        head.use(("gather", "first", h), (3, 7)[h])
        head.use(("xgT", "first", h), 4 + h)
    head.use(("wslot", "first"), 6)
    head.use(("GT", "first"), 5)
    for b, ahead, back in ((head, True, False), (step, True, True), (tail, False, True)):
        b.use(("gu",), 4, frees=2)
        if ahead:
            b.use(("gather", "next", 0), 3)
        if back:
            for n in range(3):
                b.use(("comb", n), n % 3)
        b.use(("hhT",), 5, frees=2 if ahead else 1)
        if ahead:
            b.use(("gather", "next", 1), 3)
        if back:
            for n in (3, 4):
                b.use(("comb", n), n % 3)
        if ahead:
            b.use(("xgT", "next", 0), 3)
        for h in range(2):
            b.use(("down", h), 6 + h, frees=2)
        if ahead:
            b.use(("xgT", "next", 1), 3)
        if back:
            for n in range(5, 8):
                b.use(("comb", n), n % 3)
        if ahead:
            b.use(("GT", "next"), 5)
    for n in range(8):
        tail.use(("last comb", n), n % 3)
    return head, step, tail


LAYER_COUNTS = dict(
    mem_ssq=1, mem_rstd=1, hmT_ready=2 * NM, kx_squared=NM, kx_ready=NM,
    xa_kv_ready=2 * NM, x_ssq=3, x_rstd=3, xn_ready=NT, hT_ready=6 * NT,
    uC_copied=NT, uC_reduced=NT, qC_ready=NT, cT_ready=2 * NT, sqA_ready=3, cqT_ready=3,
    sA_ready=1, u_ready=2, u_free=2, pooled_ready=2, qkA_copied=NT, qkA_reduced=NT,
    qkA_ready=NT, qkAT_ready=2 * NT, c_ready=2, z_done=2, yD_ready=2, sqY_ready=8, yT_ready=8,
    max_ready=24, p_ready=24, pn_ready=24, x_updated=2 * NT, qx_copied=NT,
    qx_reduced=NT, qx_ready=NT, qxT_ready=NT, oTx_ready=2, xhi_ready=NT, xlo_ready=1,
    M_ready=1, W_ready=1, exp_arg=1, exp_done=1, route_ready=1, layer_done=1,
)
MOE_COUNTS = dict(
    G_ready=1, xg_ready=2, xgT_ready=2, ws_ready=1, Wt_ready=1, silu_ready=1, hh_ready=1,
    hhT_ready=1, yhi_ready=2, ylo_ready=2,
)


def build(nc, a, out):
    units = attention_units()
    cross = cross_units()
    dense = dense_plan(units, cross)
    head, step, tail = moe_plans()
    ctx = ExitStack()
    with ctx:
        base = 16512

        def at(name, shape, dt, offset):
            return nc.alloc_sbuf_tensor_at(name, shape, dt, offset=base + offset)

        E_BYTES = 3 * 8192
        wgu = [at(f"wgu{s}", [P, 2, KD, FF], F32, s * E_BYTES) for s in range(4)]
        wdn = [at(f"wdn{s}", [P, 2, D], F32, s * E_BYTES + 16384) for s in range(4)]

        memx = at("memx", [P, NM, D], F32, 0)
        hmT = at("hmT", [P, KD, MEM], F32, 8192)

        o = 2 * E_BYTES
        qTA = at("qTA", [P, 4, SEQ], F32, o)
        kTA = at("kTA", [P, 4, SEQ], F32, o + 8192)
        qkA = at("qkA", [P, NT, 8, QK], F32, o + 16384)
        sqO = at("sqO", [P, 2, SEQ], F32, o + 16384)
        o += 16384 + 10240
        vA = at("vA", [P, NT, GW], F32, o + 2048)
        qTC = at("qTC", [P, 2, SEQ], F32, o + 6144)
        kTC = at("kTC", [P, SEQ], F32, o + 10240)
        vC = at("vC", [P, NT, P], F32, o + 12288)
        w_uq = at("w_uq", [P, 2, 4 * QK], F32, o + 14336)
        w_ukv = at("w_ukv", [P, 512], F32, o + 17408)
        rope_q = at("rope_q", [P, NT, 2, ROPE], F32, o + 19456)
        rope_k = at("rope_k", [P, NT, 2, ROPE], F32, o + 20480)
        kr = at("kr", [P, NT, ROPE], F32, o + 21504)
        krot = at("krot", [P, NT, ROPE], F32, o + 22016)
        assert o + 22528 <= 4 * E_BYTES

        o = 4 * E_BYTES
        X = at("X", [P, NT, D], F32, o)
        o += 16384
        hT = at("hT", [P, KD, SEQ], F32, o)
        xgT = at("xgT", [P, KD, P], F32, o)
        Gx = at("Gx", [P, SEQ], F32, o + 8192)
        Pr = at("Pr", [P, 4, 2, SEQ], F32, o)
        o += 16384
        ring0 = at("ring0", [P, KD, 512], F32, o)
        xhi = at("xhi", [P, NT, D], F32R, o)
        o += 16384
        ring1 = at("ring1", [P, KD, 544], F32, o)
        xlo = at("xlo", [P, NT, D], F32R, o)
        M16 = at("M16", [P, NT, NE], BF16, o + 16384)
        o += 17408
        yT = at("yT", [P, 8, SEQ], F32, o)
        qkC = at("qkC", [P, NT, 384], F32, o + 8192)
        qx = at("qx", [P, NT, GW], F32, o)
        sqx = at("sqx", [P, 2, GW], F32, o + 4096)
        qTx = at("qTx", [P, 2, SEQ], F32, o + 6144)
        oTx = at("oTx", [P, 2, SEQ], F32, o + 10240)
        xs = at("xs", [P, NT, D], F32, o)
        yhi = at("yhi", [P, 2, D], F32R, o)
        ylo = at("ylo", [P, 2, D], F32R, o + 8192)
        o += 16384
        xn = at("xn", [P, 2, D], F32, o)
        cqT = at("cqT", [P, 3, SEQ], F32, o)
        w_qx = at("w_qx", [P, KD, GW], F32, o)
        sqC = at("sqC", [P, 2, 384], F32, o + 8192)
        knx = at("knx", [P, NM, GW], F32, o + 11264)
        sqA = at("sqA", [P, 3, SEQ], F32, o + 6144)
        U0 = at("U0", [P, 528], F32, o + 6144)
        U1 = at("U1", [P, 528], F32, o + 8256)
        U2 = at("U2", [P, 528], F32, o + 10368)
        sqY = at("sqY", [P, 640], F32, o + 12480)
        PT = at("PT", [P, 2, 2, SEQ], F32, o + 8192)
        rope0 = at("rope0", [P, 6, NT, 16], F32, o + 8192)
        pos_i = at("pos_i", [P, NT], I32, o + 10240)
        freqs = at("freqs", [P, 16], F32, o + 10304)
        rt = at("rt", [P, 16, NT * NE], F32, o + 8192)
        G = at("G", [P, NT, P], F32R, o)
        xg = at("xg", [P, D], F32, o + 2048)
        Wt = at("Wt", [P, 2, SEQ], F32R, o + 8192)
        silu = at("silu", [P, FF], F32, o + 12288)
        hh = at("hh", [P, FF], F32, o + 13312)
        hhT = at("hhT", [P, 2, P], F32, o + 14336)
        Gq = at("Gq", [P, NT, SLOTS], F32R, o)
        Gw = at("Gw", [P, NT, SLOTS], F32, o + 1024)
        xgq = at("xgq", [P, KD, SLOTS], F32, o + 2048)
        Wq = at("Wq", [P, SEQ], F32R, o + 8192)
        o += 16384

        def small(name, shape, dt=F32):
            nonlocal o
            n = int(np.prod(shape[1:])) * (2 if dt == BF16 else 4)
            got = at(name, shape, dt, o)
            o += -(-n // 32) * 32
            return got

        ident = small("ident", [P, P])
        ident16 = small("ident16", [P, P], BF16)
        causal16 = small("causal16", [P, P], BF16)
        before16 = small("before16", [P, P], BF16)
        earlier16 = small("earlier16", [P, P], BF16)
        ones16 = small("ones16", [P, P], BF16)
        iota = small("iota", [P, SEQ])
        ones = small("ones", [P, 2])
        cossin = small("cossin", [P, 2, NT, 16])
        inv_n = small("inv_n", [P, 2, 16])
        inv_w = small("inv_w", [P, 2])
        past = small("past", [P, 8])
        kTx = small("kTx", [P, 2, MEM])
        vX = small("vX", [P, NM, GW])
        gains = small("gains", [P, 4, KD])
        g_out = small("g_out", [P, KD])
        g_cq = small("g_cq", [P, 3])
        g_rope = small("g_rope", [P, 2, ROPE])
        g_qk = small("g_qk", [P, 6])
        pool_s = small("pool_s", [P, 4])
        pool_w = small("pool_w", [P, 2, P])
        conv_w = small("conv_w", [P, 3, 2])
        conv_b = small("conv_b", [P, 2])
        sinks = small("sinks", [P, 4])
        w_rt = small("w_rt", [P, KD, 36])
        b_rt = small("b_rt", [P, 36])
        stat = small("stat", [P, 32])
        rsq_h = small("rsq_h", [P, 32])
        rsq_t = small("rsq_t", [P, 32])
        ssq_x = small("ssq_x", [P, NT])
        rstd_x = small("rstd_x", [P, NT])
        ssq_kr = small("ssq_kr", [P, NT])
        sA = small("sA", [P, NT, 2])
        rC = small("rC", [P, NT, 8])
        ssqA = small("ssqA", [P, NT, 8])
        rope_t = small("rope_t", [P, 4, ROPE])
        stat6 = small("stat6", [P, 24])
        mem_s = small("mem_s", [P, 2, NM])
        ssqY = small("ssqY", [P, 8, NT])
        rstdY = small("rstdY", [P, NG, NT])
        neg_max = small("neg_max", [P, 4, 2])
        den = small("den", [P, 4, 2])
        sink_e = small("sink_e", [P, 4, 2])
        srel = small("srel", [P, 2, NT])
        wk = small("wk", [P, 2, NT])
        q_scale = small("q_scale", [P, NT, 4])
        W_te = small("W_te", [P, NT, NE])
        ws = small("ws", [P, 2])
        wsq = small("wsq", [P, 1])
        ovf = small("ovf", [P, 2 + OVF], I32)
        ovf_f = small("ovf_f", [P, 2 + OVF])
        assert base + o <= 229368, base + o

        ps = ctx.enter_context(nc.psum_tensor("ps", [P, 8, 512], F32))

        S = {n: ctx.enter_context(nc.semaphore(n)) for n in (*LAYER_COUNTS, *MOE_COUNTS, "gathered")}
        bank_full = [ctx.enter_context(nc.semaphore(f"bank_full{i}")) for i in range(8)]
        bank_free = [ctx.enter_context(nc.semaphore(f"bank_free{i}")) for i in range(8)]
        moe_full = [ctx.enter_context(nc.semaphore(f"moe_full{i}")) for i in range(8)]
        moe_free = [ctx.enter_context(nc.semaphore(f"moe_free{i}")) for i in range(8)]
        ring_in = [ctx.enter_context(nc.semaphore(f"ring_in{i}")) for i in range(2)]
        slot_in = [ctx.enter_context(nc.semaphore(f"slot_in{i}")) for i in range(4)]
        slots_read = [ctx.enter_context(nc.semaphore(f"slots_read{i}")) for i in range(2)]
        sem = lambda n: ctx.enter_context(nc.semaphore(n))
        x_in, mem_in, pos_in, gains_in, params_in, x_out = map(
            sem, ("x_in", "mem_in", "pos_in", "gains_in", "params_in", "x_out"))
        consts, init_pool, init_dve, sin_ready = map(sem, ("consts", "init_pool", "init_dve", "sin_ready"))
        rope_arg, waited, w_qx_in = map(sem, ("rope_arg", "waited", "w_qx_in"))
        ovf_w, ovf_pe, ovf_act, ovf_dve = map(sem, ("ovf_w", "ovf_pe", "ovf_act", "ovf_dve"))

        OVF_PE, OVF_ACT, OVF_DVE = 7, 2, 8

        def done(l, name, n):
            return l * LAYER_COUNTS[name] + n

        def mdone(l, p, name, n):
            return (l * PAIRS + p) * MOE_COUNTS[name] + n

        def mjob(l, p, name):
            first = isinstance(p, int) and p == 0
            last = isinstance(p, int) and p == PAIRS - 1
            plan = head if first else tail if last else step
            if name == ("GT", "before"):
                bank, n, before = step.job["hhT",][0], 0, 0
            else:
                bank, n, before = plan.job[name]

            def base(kind):
                h, s_, t = ((b.full if kind == "full" else b.free)[bank] for b in (head, step, tail))
                return l * (h + (PAIRS - 2) * s_ + t) + (0 if first else h + (p - 1) * s_)
            return bank, base("full") + n, base("free") + before

        def full(eng, l, name):
            bank, n, _ = dense.job[name]
            eng.wait_ge(bank_full[bank], l * dense.full[bank] + n)
            return ps[:, bank, :]

        def emptied(eng, l, name):
            bank, _, before = dense.job[name]
            eng.wait_ge(bank_free[bank], l * dense.free[bank] + before + 2)
            return ps[:, bank, :]

        def mfull(eng, l, p, name):
            bank, n, _ = mjob(l, p, name)
            eng.wait_ge(moe_full[bank], n)
            return ps[:, bank, :]

        def memptied(eng, l, p, name):
            bank, _, before = mjob(l, p, name)
            eng.wait_ge(moe_free[bank], before + 2)
            return ps[:, bank, :]

        def freed(name):
            return bank_free[dense.job[name][0]]

        def mfreed(name):
            return moe_free[(step if name in step.job else head if name in head.job else tail).job[name][0]]

        def wait_apart(eng, semaphore, value):
            eng.wait_ge(semaphore, value)
            eng.sem_inc(waited, 1)

        x_d = a["x"].rearrange("b (t p) d -> p (b t) d", p=P)
        out_d = out.rearrange("b (t p) d -> p (b t) d", p=P)
        mem_d = a["mem"].rearrange("b (t p) d -> p (b t) d", p=P)
        pos_d = a["positions"].rearrange("b (t p) -> p (b t)", p=P)

        def lay(name, l):
            return a[name][bass.ds(l, 1)]

        def cols(name, l, c0, c1):
            return lay(name, l).rearrange("l (p c) n -> p (l c) n", c=KD)[:, :, c0:c1]

        wg_d = a["w_gate"].rearrange("l e (p c) n -> (l e) p (c n)", c=KD)
        wu_d = a["w_up"].rearrange("l e (p c) n -> (l e) p (c n)", c=KD)
        wd_d = a["w_down"].rearrange("l e (p c) n -> (l e) p (c n)", c=2)

        def expert(w, e):
            return w[bass.ds(e, 1)].rearrange("e p n -> p (e n)")

        RING0_DMAS = 9
        RING1_DMAS = 11
        PARAM_DMAS = 35

        def ring0_wait(eng, l, n):
            eng.wait_ge(ring_in[0], (l * RING0_DMAS + n) * 16)

        def ring1_wait(eng, l, n):
            eng.wait_ge(ring_in[1], (l * RING1_DMAS + n) * 16)

        block = ctx.enter_context(nc.Block())

        @block.sync
        def _(sp):
            sp.dma_start(X[:], x_d).then_inc(x_in, 16)

            def read(l, name):
                bank, n, _ = dense.job[name]
                wait_apart(sp, bank_full[bank], l * dense.full[bank] + n)

            def load_mix(ring, q, l, n):
                w = lay("w_mix_out", l)[:, :, n * 512:(n + 1) * 512]

                def rows(r0, k):
                    return w[:, r0:r0 + k * P, :].rearrange("l (c p) n -> p (l c) n", p=P)
                sp.dma_start(ring[:, 0:2, 0:512], rows(GW, 2)).then_inc(ring_in[q], 16)
                sp.dma_start(ring[:, 2:4, 0:512], rows(3 * GW, 2)).then_inc(ring_in[q], 16)
                sp.dma_start(ring[:, 4:6, 0:512], rows(0, 2)).then_inc(ring_in[q], 16)
                for half in range(2):
                    src = w[:, 2 * GW + half * P:2 * GW + (half + 1) * P, :]
                    sp.dma_start(ring[half * HALF:(half + 1) * HALF, 6:8, 0:512],
                                 src.rearrange("l (c p) n -> p (l c) n", p=HALF)).then_inc(ring_in[q], 16)

            def load_pair(l, pair_of_layer, ps_):
                for j in range(2):
                    s = 2 * ps_ + j
                    e = l * NE + pair_of_layer * 2 + j
                    flat = wgu[s][:].rearrange("p u c n -> p u (c n)")
                    sp.dma_start(flat[:, 0, :], expert(wg_d, e)).then_inc(slot_in[s], 16)
                    sp.dma_start(flat[:, 1, :], expert(wu_d, e)).then_inc(slot_in[s], 16)
                    sp.dma_start(wdn[s][:].rearrange("p c n -> p (c n)"), expert(wd_d, e)).then_inc(slot_in[s], 16)

            with sp.Fori(0, DEPTH) as l:
                sp.wait_ge(slots_read[0], l * 8 + 1)
                sp.dma_start(memx[:], mem_d).then_inc(mem_in, 16)
                sp.wait_ge(S["gathered"], l + 1)
                sp.dma_start(ring0[:], cols("xa_w_kv", l, 0, 512)).then_inc(ring_in[0], 16)
                sp.dma_start(ring1[:, :, 0:ROPE], cols("w_in", l, C_B - ROPE, C_B)).then_inc(ring_in[1], 16)
                sp.dma_start(ring1[:, :, ROPE:544], cols("w_in", l, C_C, C_D)).then_inc(ring_in[1], 16)
                read(l, ("kvx", NM - 1))
                sp.dma_start(ring0[:, :, 0:384], cols("w_in", l, 0, 384)).then_inc(ring_in[0], 16)
                sp.wait_ge(S["mem_rstd"], done(l, "mem_rstd", 1))
                load_pair(l, 0, 0)
                read(l, ("uC", NT - 1, 1))
                sp.dma_start(ring1[:, :, 0:256], cols("w_in", l, C_B, C_C)).then_inc(ring_in[1], 16)
                sp.dma_start(ring1[:, :, 256:512], cols("w_in", l, C_D + 256, C_D + 512)).then_inc(ring_in[1], 16)
                read(l, ("A", 2))
                sp.dma_start(ring0[:, :, 0:256], cols("w_in", l, C_D + 512, C_D + 768)).then_inc(ring_in[0], 16)
                sp.dma_start(ring0[:, :, 256:512], cols("w_in", l, C_D, C_D + 256)).then_inc(ring_in[0], 16)
                read(l, ("D", 3))
                load_mix(ring1, 1, l, 0)
                read(l, ("D", 5))
                load_mix(ring0, 0, l, 1)
                wait_apart(sp, S["yT_ready"], done(l, "yT_ready", 4))
                read(l, ("stY", 3))
                sp.dma_start(w_qx[:], cols("xa_w_q", l, 0, GW)).then_inc(w_qx_in, 16)
                read(l, ("stY", 5))
                load_pair(l, 1, 1)
                read(l, ("mix", NT - 1, MIX_ORDER[-1], 1))
                for c in range(2):
                    src = lay("xa_w_o", l)[:, c * P:(c + 1) * P, :]
                    sp.dma_start(ring1[:, 4 * c:4 * c + 4, 272:528],
                                 src.rearrange("l p (q n) -> p (l q) n", n=256)).then_inc(ring_in[1], 16)
                with sp.Fori(1, PAIRS // 2) as i:
                    for parity in range(2):
                        sp.wait_ge(slots_read[parity], l * (PAIRS // 2) + i + 1)
                        load_pair(l, 2 * i + parity, parity)
                wait_apart(sp, S["route_ready"], l + 2)
                n_ovf = sp.value_load(ovf[0:1, 0:1], min_val=0, max_val=OVF - 1)
                before = sp.value_load(ovf[0:1, 1:2], min_val=0, max_val=DEPTH * OVF)
                with sp.If(n_ovf > 0):
                    wait_apart(sp, slots_read[0], l * 8 + 8 + 1)
                    with sp.Fori(0, n_ovf) as q:
                        e = sp.value_load(ovf[0:1, bass.ds(q + 2, 1)], min_val=0, max_val=NE - 1)
                        with sp.If(q > 0):
                            wait_apart(sp, ovf_pe, (before + q) * OVF_PE)
                        row = l * NE + e
                        flat = wgu[0][:].rearrange("p u c n -> p u (c n)")
                        sp.dma_start(flat[:, 0, :], expert(wg_d, row)).then_inc(ovf_w, 16)
                        sp.dma_start(flat[:, 1, :], expert(wu_d, row)).then_inc(ovf_w, 16)
                        sp.dma_start(wdn[0][:].rearrange("p c n -> p (c n)"), expert(wd_d, row)).then_inc(ovf_w, 16)
                    wait_apart(sp, ovf_pe, (before + n_ovf) * OVF_PE)
            sp.wait_ge(S["layer_done"], DEPTH + 1)
            sp.dma_start(out_d, X[:]).then_inc(x_out, 16)
            sp.wait_ge(x_out, 16)

        @block.gpsimd
        def _(pool):
            pool.dma_start(pos_i[:], pos_d, allow_slow_non_contiguous=True).then_inc(pos_in, 16)
            pool.memset(ident[:], 0.0)
            pool.memset(causal16[:], 0.0)
            pool.memset(before16[:], 0.0)
            pool.memset(earlier16[:], 1.0)
            pool.memset(ones16[:], 1.0)
            pool.memset(ones[:], 1.0)
            pool.memset(pool_w[:], 0.0)
            for j in range(16):
                freq = float(np.float32(THETA) ** (-np.float32(j) / np.float32(16)))
                pool.memset(freqs[:, j:j + 1], freq)
            pool.drain()
            for w in range(4):
                rows = slice((w % 2) * HALF, (w % 2 + 1) * HALF)
                pool.memset(inv_w[rows, w // 2:w // 2 + 1], 1.0 / WINDOWS[w])
                pool.memset(inv_n[rows, w // 2, :], float(WINDOWS[w]))
                pool.drain()
            pool.iota(iota[:], pattern=[[1, SEQ]], base=0, channel_multiplier=0, allow_small_or_imprecise_dtypes=True)
            pool.drain()
            pool.affine_select(out=ident[:], in_=ident[:], compare_op=ALU.not_equal, fill=1.0,
                               base=0, pattern=[[-1, P]], channel_multiplier=1)
            pool.affine_select(out=causal16[:], in_=causal16[:], compare_op=ALU.is_ge, fill=NEG,
                               base=0, pattern=[[-1, P]], channel_multiplier=1)
            pool.affine_select(out=before16[:], in_=before16[:], compare_op=ALU.is_gt, fill=NEG,
                               base=0, pattern=[[1, P]], channel_multiplier=-1)
            pool.affine_select(out=earlier16[:], in_=earlier16[:], compare_op=ALU.is_gt, fill=0.0,
                               base=0, pattern=[[1, P]], channel_multiplier=-1)
            pool.drain()
            pool.tensor_copy(ident16[:], ident[:])
            pool.drain()
            pool.nop().then_inc(init_pool, 1)

            n_dma = 0

            def load(dst, src):
                nonlocal n_dma
                n_dma += 1
                pool.dma_start(dst, src, allow_slow_non_contiguous=True).then_inc(params_in, 16)

            def across(src, n):
                return src.partition_broadcast(n)

            def load_gain(i, name, semaphore):
                pool.dma_start(gains[:, i, :], lay(name, l).rearrange("l (p c) -> p (l c)", c=KD),
                               allow_slow_non_contiguous=True).then_inc(semaphore, 16)

            with pool.Fori(0, DEPTH) as l:
                n_dma = 2
                wait_apart(pool, S["route_ready"], l + 1)
                load_gain(3, "norm_mem", gains_in)
                load_gain(0, "norm_mix", gains_in)
                load_gain(1, "norm_xa", params_in)
                load(g_cq[:, 0:2], lay("mla_g_cq", l).rearrange("l (c p) -> p (l c)", p=P))
                load(g_cq[:, 2:3], lay("mla_g_ckv", l).rearrange("l (c p) -> p (l c)", p=P))
                for i, name in enumerate(("mla_g_q", "mla_g_k")):
                    g = lay(name, l)
                    load(g_rope[:, i, :], g[0, NOPE:QK].partition_broadcast(P))
                    load(g_qk[0:NOPE, i:i + 1], g[:, 0:NOPE].rearrange("l p -> p l"))
                for i, name in enumerate(("swa_g_q", "swa_g_k", "xa_g_q", "xa_g_k")):
                    for half in range(2):
                        load(g_qk[half * HD:(half + 1) * HD, 2 + i:3 + i], lay(name, l).rearrange("l p -> p l"))
                load(pool_s[:, 0:2], lay("pool_scale", l).rearrange("l (c p) -> p (l c)", p=P))
                for g in range(4):
                    h = (g % 2) * HD
                    load(pool_w[h:h + HD, g // 2, h:h + HD], lay("pool_w", l)[:, g].rearrange("l c d -> c (l d)"))
                load(conv_w[:].rearrange("p k c -> p (k c)"), lay("conv_w", l).rearrange("l k (c p) -> p (l k c)", p=P))
                load(conv_b[:], lay("conv_b", l).rearrange("l (c p) -> p (l c)", p=P))
                load(sinks[:], lay("swa_sinks", l)[0].partition_broadcast(P))
                g = lay("mix_out_norm", l)
                load(g_out[:, 0:2], g[:, GW:2 * GW].rearrange("l (c p) -> p (l c)", p=P))
                load(g_out[:, 2:4], g[:, 3 * GW:].rearrange("l (c p) -> p (l c)", p=P))
                load(g_out[:, 4:6], g[:, 0:GW].rearrange("l (c p) -> p (l c)", p=P))
                for half in range(2):
                    load(g_out[half * HALF:(half + 1) * HALF, 6:8],
                         g[:, 2 * GW + half * P:2 * GW + (half + 1) * P].rearrange("l (c p) -> p (l c)", p=HALF))
                load(w_rt[:, :, 0:NG], cols("w_group", l, 0, NG))
                load(w_rt[:, :, NG:NG + NE], cols("w_expert", l, 0, NE))
                load(b_rt[:, 0:NG], lay("b_group", l)[0].partition_broadcast(P))
                load(b_rt[:, NG:NG + NE], lay("b_expert", l)[0].partition_broadcast(P))
                wait_apart(pool, S["layer_done"], l + 1)
                load_gain(2, "norm_ffn", params_in)
                load(w_uq[:], lay("mla_w_uq", l).rearrange("l (c p) n -> p (l c) n", p=P))
                load(w_ukv[:], lay("mla_w_ukv", l).rearrange("l p n -> p (l n)"))
                for t in range(NT):
                    wait_apart(pool, S["xhi_ready"], done(l, "xhi_ready", t + 1))
                    pool.tensor_tensor(xlo[:, t], xs[:, t], xhi[:, t].bitcast(F32), ALU.subtract)
                pool.drain()
                pool.nop().then_inc(S["xlo_ready"], 1)
            assert n_dma == PARAM_DMAS, n_dma

        @block.scalar
        def _(act):
            def copy(dst, src, scale=1.0):
                return nc.scalar.activation(dst, src, ACT.Copy, scale=scale)

            def square(dst, src, **kw):
                return nc.scalar.activation(dst, src, ACT.Square, **kw)

            act.wait_ge(rope_arg, 1)
            nc.scalar.activation(cossin[:], rope0[:, 4:6], ACT.Sin).then_inc(sin_ready, 1)

            def normalise(l, t):
                act.wait_ge(S["x_rstd"], done(l, "x_rstd", 1))
                if t >= 2:
                    full(act, l, ("xT", 0, t - 2, 1))
                copy(xn[:, t % 2], X[:, t], scale=rstd_x[:, t:t + 1]).then_inc(S["xn_ready"], 1)

            def sum_squares(l, s, t):
                act.wait_ge(S["x_updated"], done(l, "x_updated", NT * (s - 1) + t + 1))
                square(PT[:, t % 2].rearrange("p h n -> p (h n)"), X[:, t], accum_out=ssq_x[:, t:t + 1])
                act.drain()
                if t == NT - 1:
                    act.nop().then_inc(S["x_ssq"], 1)

            def attend(l, list_, first):
                for n in range(len(list_) + 5):
                    if n < len(list_):
                        kind, pair, t, nk = list_[n]
                        u = first + n
                        L = nk * P
                        act.wait_ge(S["max_ready"], done(l, "max_ready", u + 1))
                        if n >= 4:
                            full(act, l, ("T", list_[n - 4], 1))
                        for h in range(2):
                            bank = full(act, l, ("S", list_[n], h))
                            nc.scalar.activation(Pr[:, n % 4, h, 0:L], bank[:, 0:L], ACT.Exp,
                                                 bias=neg_max[:, n % 4, h:h + 1],
                                                 scale=q_scale[:, t, 2 * pair + h:2 * pair + h + 1]
                                                 if kind == "xa" else 1.0,
                                                 accum_out=den[:, n % 4, h:h + 1]
                                                 ).then_inc(freed(("S", list_[n], h)), 1)
                        if kind == "swa":
                            nc.scalar.activation(sink_e[:, n % 4], sink_e[:, n % 4], ACT.Exp)
                        act.drain()
                        act.nop().then_inc(S["p_ready"], 1)
                    if 2 <= n <= len(list_) + 1:
                        nk = list_[n - 2][3]
                        bank = full(act, l, ("T", list_[n - 2], 0))
                        copy(PT[:, n % 2, 0, 0:nk * P], bank[:, 0:nk * P]
                             ).then_inc(freed(("T", list_[n - 2], 0)), 1)
                    if 3 <= n <= len(list_) + 2 and list_[n - 3][2] == NT - 1:
                        kind, pair = list_[n - 3][:2]
                        bank = full(act, l, ("O", kind, pair))
                        if kind == "xa":
                            copy(oTx[:, pair], bank).then_inc(freed(("O", kind, pair)), 1)
                            act.drain()
                            act.nop().then_inc(S["oTx_ready"], 1)
                        else:
                            if kind == "mla":
                                full(act, l, ("stY", stat_of(("swa", pair))))
                            square(sqO[:, pair], bank).then_inc(freed(("O", kind, pair)), 1)
                            act.drain()
                            act.nop().then_inc(S["sqY_ready"], 1)

            with act.Fori(0, DEPTH) as l:
                act.wait_ge(S["layer_done"], l + 1)
                act.wait_ge(x_in, 16)
                for t in range(NT):
                    square(xn[:, t % 2], X[:, t], accum_out=ssq_x[:, t:t + 1])
                    act.drain()
                act.nop().then_inc(S["x_ssq"], 1)
                act.wait_ge(mem_in, (l + 1) * 16)
                for i in range(NM):
                    square(xn[:, i], memx[:, i], accum_out=mem_s[:, 0, i:i + 1])
                    act.drain()
                act.nop().then_inc(S["mem_ssq"], 1)
                normalise(l, 0)
                normalise(l, 1)
                act.wait_ge(S["mem_rstd"], done(l, "mem_rstd", 1))
                for i in range(NM):
                    bank = full(act, l, ("kvx", i))
                    copy(vX[:, i], bank[:, GW:], scale=mem_s[:, 1, i:i + 1]).then_inc(S["xa_kv_ready"], 1)
                    square(sqC[:, i, 0:GW], bank[:, 0:GW], scale=mem_s[:, 1, i:i + 1]).then_inc(freed(("kvx", i)), 1)
                    act.drain()
                    act.nop().then_inc(S["kx_squared"], 1)
                normalise(l, 2)
                normalise(l, 3)
                act.wait_ge(S["kx_ready"], done(l, "kx_ready", NM))
                for t in range(NT):
                    if t >= 2:
                        act.wait_ge(S["uC_reduced"], done(l, "uC_reduced", t - 1))
                    bank = full(act, l, ("uC", t, 0))
                    copy(kr[:, t], bank[:, 0:ROPE])
                    square(sqC[:, t % 2, 0:ROPE], bank[:, 0:ROPE], accum_out=ssq_kr[:, t:t + 1])
                    act.drain()
                    copy(qkC[:, t, 0:GW].rearrange("p (g k d) -> p k g d", g=2, k=2),
                         bank[:, ROPE:ROPE + GW].rearrange("p (k g d) -> p k g d", g=2, k=2)
                         ).then_inc(freed(("uC", t, 0)), 1)
                    bank = full(act, l, ("uC", t, 1))
                    copy(vC[:, t], bank[:, P:2 * P])
                    copy(qkC[:, t, GW:], bank[:, 0:P]).then_inc(freed(("uC", t, 1)), 1)
                    act.drain()
                    square(sqC[:, t % 2], qkC[:, t])
                    act.drain()
                    act.nop().then_inc(S["uC_copied"], 1)
                act.wait_ge(params_in, (l + 1) * PARAM_DMAS * 16)
                for i in range(NM):
                    bank = full(act, l, ("kxT", i))
                    copy(kTx[:, :, i * P:(i + 1) * P], bank[:, 0:2 * P].rearrange("p (c m) -> p c m", c=2),
                         scale=g_qk[:, 5:6]).then_inc(freed(("kxT", i)), 1)
                    act.drain()
                    act.nop().then_inc(S["xa_kv_ready"], 1)
                act.wait_ge(S["uC_reduced"], done(l, "uC_reduced", NT))
                for m in range(3):
                    bank = full(act, l, ("A", m))
                    square(sqA[:, m], bank).then_inc(freed(("A", m)), 1)
                    act.drain()
                    act.nop().then_inc(S["sqA_ready"], 1)
                full(act, l, ("stA",))
                for m in range(2):
                    bank = full(act, l, ("B", m))
                    if m > 0:
                        act.wait_ge(S["u_free"], done(l, "u_free", m))
                    nc.scalar.activation(U0[:, 0:16], bank[:, 0:16], ACT.Copy, scale=0.0)
                    copy(U0[:, 16:528], bank).then_inc(freed(("B", m)), 1)
                    act.drain()
                    act.nop().then_inc(S["u_ready"], 1)
                act.wait_ge(S["sA_ready"], done(l, "sA_ready", 1))
                for t in range(NT):
                    bank = full(act, l, ("qA", t))
                    if t > 0:
                        act.wait_ge(S["qkA_reduced"], done(l, "qkA_reduced", t))
                    copy(qkA[:, t, 0:4], bank[:, 0:384].rearrange("p (h d) -> p h d", h=4), scale=sA[:, t, 0:1]).then_inc(freed(("qA", t)), 1)
                    bank = full(act, l, ("kvA", t))
                    kv = bank.rearrange("p (h u d) -> p h u d", h=4, u=2)
                    copy(qkA[:, t, 4:8, 0:NOPE], kv[:, :, 0, :], scale=sA[:, t, 1:2])
                    copy(vA[:, t].rearrange("p (h d) -> p h d", h=4), kv[:, :, 1, :],
                         scale=sA[:, t, 1:2]).then_inc(freed(("kvA", t)), 1)
                    act.drain()
                    square(sqY[:, 0:384].rearrange("p (h d) -> p h d", h=4), qkA[:, t, 0:4])
                    square(sqY[:, 384:640].rearrange("p (h d) -> p h d", h=4), qkA[:, t, 4:8, 0:NOPE])
                    act.drain()
                    act.nop().then_inc(S["qkA_copied"], 1)
                for t in range(NT):
                    bank = full(act, l, ("cT", t))
                    copy(qTC[:, :, t * P:(t + 1) * P], bank[:, 0:2 * P].rearrange("p (c m) -> p c m", c=2),
                         scale=g_qk[:, 2:3]).then_inc(freed(("cT", t)), 1)
                    act.drain()
                    act.nop().then_inc(S["cT_ready"], 1)

                def gate_copy(i, name):
                    bank = full(act, l, name)
                    if i > 0:
                        act.wait_ge(S["z_done"], done(l, "z_done", i))
                    copy(U0[:, 0:SEQ], bank).then_inc(freed(name), 1)
                    act.drain()
                    act.nop().then_inc(S["c_ready"], 1)

                def pool_square(m):
                    bank = full(act, l, ("pool", m))
                    if m > 0:
                        full(act, l, ("stY", m - 1))
                    square(sqY[:, 0:SEQ], bank, scale=pool_s[:, m:m + 1]).then_inc(freed(("pool", m)), 1)
                    act.drain()
                    act.nop().then_inc(S["sqY_ready"], 1)

                def conv_square(m):
                    full(act, l, ("stY", 1 + m))
                    act.wait_ge(S["yD_ready"], done(l, "yD_ready", m + 1))
                    square(sqY[:, 0:SEQ], U2[:, 0:SEQ])
                    act.drain()
                    act.nop().then_inc(S["sqY_ready"], 1)

                def query_transposed(t):
                    bank = full(act, l, ("qAT", t))
                    copy(qTA[0:QK, :, t * P:(t + 1) * P], bank[0:QK].rearrange("p (h m) -> p h m", h=4),
                         scale=g_qk[0:QK, 0:1]).then_inc(freed(("qAT", t)), 1)
                    act.drain()
                    act.nop().then_inc(S["qkAT_ready"], 1)

                act.wait_ge(S["u_free"], done(l, "u_free", 2))
                gate_copy(0, ("D", 0))
                act.wait_ge(S["qkA_reduced"], done(l, "qkA_reduced", NT))
                pool_square(0)
                pool_square(1)
                query_transposed(0)
                query_transposed(1)
                gate_copy(1, ("D", 3))
                query_transposed(2)
                query_transposed(3)
                conv_square(0)
                conv_square(1)
                attend(l, units, 0)
                for t in range(NT):
                    sum_squares(l, 1, t)
                def query_copy(t):
                    bank = full(act, l, ("qx", t))
                    copy(qx[:, t], bank[:, 0:GW])
                    act.drain()
                    act.nop().then_inc(S["qx_ready"], 1)

                query_copy(0)
                query_copy(1)
                act.wait_ge(S["x_rstd"], done(l, "x_rstd", 2))
                for t in range(NT):
                    bank = full(act, l, ("qx", t))
                    if t >= 2:
                        act.wait_ge(S["qx_reduced"], done(l, "qx_reduced", t - 1))
                    square(sqx[:, t % 2], bank[:, 0:GW], scale=rstd_x[:, t:t + 1]).then_inc(freed(("qx", t)), 1)
                    act.drain()
                    act.nop().then_inc(S["qx_copied"], 1)
                    if t < 2:
                        query_copy(t + 2)
                for t in range(NT):
                    bank = full(act, l, ("qxT", t))
                    copy(qTx[:, :, t * P:(t + 1) * P], bank[:, 0:2 * P].rearrange("p (c m) -> p c m", c=2),
                         scale=g_qk[:, 4:5]).then_inc(freed(("qxT", t)), 1)
                    act.drain()
                    act.nop().then_inc(S["qxT_ready"], 1)
                attend(l, cross, len(units))
                for t in range(NT):
                    sum_squares(l, 2, t)
                act.wait_ge(S["x_rstd"], done(l, "x_rstd", 3))
                full(act, l, ("wo", NT - 1, 1))
                for t in range(NT):
                    copy(xs[:, t], X[:, t], scale=rstd_x[:, t:t + 1])
                    copy(xhi[:, t], X[:, t], scale=rstd_x[:, t:t + 1]).then_inc(S["xhi_ready"], 1)

                act.wait_ge(S["exp_arg"], done(l, "exp_arg", 1))
                nc.scalar.activation(rt[:, 10, 0:NT * NG], rt[:, 10, 0:NT * NG], ACT.Exp)
                nc.scalar.activation(rt[:, 11, 0:NT], rt[:, 11, 0:NT], ACT.Exp)
                act.drain()
                act.nop().then_inc(S["exp_done"], 1)

                def gathered_copy(p, who, h):
                    bank = mfull(act, l, p, ("gather", who, h))
                    copy(xg[:, h * 512:(h + 1) * 512], bank).then_inc(mfreed(("gather", who, h)), 1)
                    act.drain()
                    act.nop().then_inc(S["xg_ready"], 1)

                def one_hot_copy(p, who, parity):
                    bank = mfull(act, l, p, ("GT", who))
                    copy(Wt[:, parity], bank).then_inc(mfreed(("GT", who)), 1)
                    act.drain()
                    act.nop().then_inc(S["Wt_ready"], 1)

                def step_(p, parity, ahead):
                    bank = mfull(act, l, p, ("gu",))
                    nc.scalar.activation(silu[:], bank[:, 0:FF], ACT.Silu).then_inc(mfreed(("gu",)), 1)
                    act.drain()
                    act.nop().then_inc(S["silu_ready"], 1)
                    if ahead:
                        gathered_copy(p, "next", 0)
                    bank = mfull(act, l, p, ("hhT",))
                    copy(hhT[:], bank[:, 0:2 * P].rearrange("p (c m) -> p c m", c=2)).then_inc(mfreed(("hhT",)), 1)
                    act.drain()
                    act.nop().then_inc(S["hhT_ready"], 1)
                    if ahead:
                        gathered_copy(p, "next", 1)
                    act.wait_ge(S["ws_ready"], mdone(l, p, "ws_ready", 1))
                    for h in range(2):
                        bank = mfull(act, l, p, ("down", h))
                        copy(yhi[:, parity, h * 512:(h + 1) * 512], bank, scale=ws[:, parity:parity + 1]
                             ).then_inc(mfreed(("down", h)), 1)
                        act.drain()
                        act.nop().then_inc(S["yhi_ready"], 1)
                    if ahead:
                        one_hot_copy(p, "next", 1 - parity)

                for h in range(2):
                    gathered_copy(0, "first", h)
                one_hot_copy(0, "first", 0)
                step_(0, 0, True)
                with act.Fori(0, PAIRS // 2 - 1) as i:
                    step_(2 * i + 1, 1, True)
                    step_(2 * i + 2, 0, True)
                step_(PAIRS - 1, 1, False)

                wait_apart(act, S["route_ready"], l + 2)
                n_ovf = act.value_load(ovf[0:1, 0:1], min_val=0, max_val=OVF - 1)
                before = act.value_load(ovf[0:1, 1:2], min_val=0, max_val=DEPTH * OVF)
                with act.If(n_ovf > 0):
                    with act.Fori(0, n_ovf) as q:
                        tile = before + q
                        act.wait_ge(ovf_pe, tile * OVF_PE + 3)
                        nc.scalar.activation(silu[0:SLOTS], ps[0:SLOTS, 4, 0:FF], ACT.Silu).then_inc(ovf_act, 1)
                        act.wait_ge(ovf_pe, tile * OVF_PE + 5)
                        act.wait_ge(ovf_dve, tile * OVF_DVE + 3)
                        copy(yhi[0:SLOTS, 0].rearrange("p (h n) -> p h n", h=2), ps[0:SLOTS, 6:8, :],
                             scale=wsq[0:SLOTS]).then_inc(ovf_act, 1)

        @block.vector
        def _(dve):
            tt, ts, stt = nc.vector.tensor_tensor, nc.vector.tensor_scalar, nc.vector.scalar_tensor_tensor

            def signal(name):
                dve.drain()
                dve.nop().then_inc(S[name], 1)

            def mean_eps(dst, src, n):
                ts(dst, src, 1.0 / n, EPS, ALU.mult, ALU.add)

            def rsqrt(dst, v, n):
                h, w = rsq_h[:, 0:n], rsq_t[:, 0:n]
                dve.drain()
                ts(h, v, -0.5, None, ALU.mult)
                ts(dst.bitcast(I32), v.bitcast(I32), 1, None, ALU.logical_shift_right)
                dve.drain()
                ts(dst.bitcast(I32), dst.bitcast(I32), -1.0, RSQRT_MAGIC, ALU.mult, ALU.add)
                for _ in range(3):
                    dve.drain()
                    tt(w, dst, dst, ALU.mult)
                    dve.drain()
                    tt(w, w, h, ALU.mult)
                    dve.drain()
                    stt(dst, w, 1.5, dst, ALU.add, ALU.mult)
                dve.drain()

            def flat(tile):
                pattern = {2: "p a -> p a", 3: "p a b -> p (a b)", 4: "p a b c -> p (a b c)"}[len(tile.shape)]
                return tile[:].rearrange(pattern)

            def transposed(l, s, t, gain):
                for h in range(2):
                    bank = full(dve, l, ("xT", s, t, h))
                    g = gains[:, gain, 4 * h:4 * h + 4].unsqueeze(2).to_broadcast([P, 4, P])
                    tt(hT[:, 4 * h:4 * h + 4, t * P:(t + 1) * P], bank.rearrange("p (c m) -> p c m", c=4), g,
                       ALU.mult).then_inc(freed(("xT", s, t, h)), 1)
                    signal("hT_ready")

            def stream_rstd(l, s):
                dve.wait_ge(S["x_ssq"], done(l, "x_ssq", s + 1))
                mean_eps(stat[:, 0:NT], ssq_x[:], D)
                rsqrt(rstd_x[:], stat[:, 0:NT], NT)
                signal("x_rstd")

            def attend(l, list_, first):
                for n in range(len(list_) + 5):
                    if n < len(list_):
                        kind, pair, t, nk = list_[n]
                        L = nk * P
                        full(dve, l, ("S", list_[n], 0))
                        full(dve, l, ("S", list_[n], 1))
                        u = n % 4
                        m = neg_max[:, u]
                        nc.vector.tensor_reduce(m, ps[:, 2 * (n % 2):2 * (n % 2) + 2, 0:L], AX_X, ALU.max)
                        dve.drain()
                        if kind == "swa":
                            sink = sinks[:, pair::2]
                            tt(m, m, sink, ALU.max)
                            dve.drain()
                            tt(sink_e[:, u], sink, m, ALU.subtract)
                        if kind == "xa":
                            stt(m, m, -1.0, q_scale[:, t, 2 * pair:2 * pair + 2], ALU.mult, ALU.mult)
                        else:
                            ts(m, m, -1.0, None, ALU.mult)
                        signal("max_ready")
                    if 1 <= n <= len(list_):
                        kind, _, _, nk = list_[n - 1]
                        u = (n - 1) % 4
                        dve.wait_ge(S["p_ready"], done(l, "p_ready", first + n))
                        if kind == "swa":
                            tt(den[:, u], den[:, u], sink_e[:, u], ALU.add)
                            dve.drain()
                        nc.vector.reciprocal(den[:, u], den[:, u])
                        dve.drain()
                        for h in range(2):
                            ts(Pr[:, u, h, 0:nk * P], Pr[:, u, h, 0:nk * P], den[:, u, h:h + 1], None, ALU.mult)
                        signal("pn_ready")
                    if 2 <= n <= len(list_) + 1:
                        nk = list_[n - 2][3]
                        bank = full(dve, l, ("T", list_[n - 2], 1))
                        nc.vector.tensor_copy(PT[:, n % 2, 1, 0:nk * P], bank[:, 0:nk * P]
                                              ).then_inc(freed(("T", list_[n - 2], 1)), 1)
                    if 4 <= n <= len(list_) + 3 and list_[n - 4][2] == NT - 1 and list_[n - 4][0] != "xa":
                        kind2, pair2 = list_[n - 4][:2]
                        bank = emptied(dve, l, ("O", kind2, pair2))
                        c = stat_of(list_[n - 4])
                        ts(yT[:, c], bank, g_out[:, c:c + 1], None, ALU.mult).then_inc(freed(("O", kind2, pair2)), 1)
                        signal("yT_ready")
                    if pair_statistics(list_, n - 5):
                        evacuate_stat(l, stat_of(list_[n - 5]))

            def evacuate_stat(l, c):
                bank = full(dve, l, ("stY", c))
                nc.vector.tensor_copy(ssqY[:, c], bank[:, 0:NT]).then_inc(freed(("stY", c)), 1)

            def argmax_first(vals, n, m, oh, tmp):
                mb = m.to_broadcast([P, NT, n])
                tt(tmp, vals, mb, ALU.is_lt)
                dve.drain()
                io = iota[:, 0:n].unsqueeze(1).to_broadcast([P, NT, n])
                stt(tmp, tmp, float(SEQ), io, ALU.mult, ALU.add)
                dve.drain()
                nc.vector.tensor_reduce(rt[:, 15, 0:NT].unsqueeze(2), tmp, AX_X, ALU.min)
                dve.drain()
                tt(oh, io, rt[:, 15, 0:NT].unsqueeze(2).to_broadcast([P, NT, n]), ALU.is_equal)
                dve.drain()

            for bank in range(8):
                dve.sem_inc(bank_free[bank], 1)
                dve.sem_inc(moe_free[bank], 1)
            for s_ in (*slots_read, S["layer_done"], S["gathered"], S["route_ready"]):
                dve.sem_inc(s_, 1)
            dve.wait_ge(init_pool, 1)
            dve.wait_ge(pos_in, 16)
            posf = rope0[:, 3, 0, 0:NT]
            nc.vector.tensor_copy(posf, pos_i[:])
            dve.drain()
            tt(rope0[:, 0], posf.unsqueeze(2).to_broadcast([P, NT, 16]),
               freqs[:].unsqueeze(1).to_broadcast([P, NT, 16]), ALU.mult)
            dve.drain()
            ts(rope0[:, 1], rope0[:, 0], 1.0 / TWO_PI, ROUND, ALU.mult, ALU.add)
            dve.drain()
            ts(rope0[:, 1], rope0[:, 1], -ROUND, None, ALU.add)
            dve.drain()
            stt(rope0[:, 2], rope0[:, 1], -PI_A, rope0[:, 0], ALU.mult, ALU.add)
            dve.drain()
            stt(rope0[:, 0], rope0[:, 1], -PI_B, rope0[:, 2], ALU.mult, ALU.add)
            dve.drain()
            stt(rope0[:, 2], rope0[:, 1], -PI_C, rope0[:, 0], ALU.mult, ALU.add)
            dve.drain()
            ts(rope0[:, 0], rope0[:, 2], math.pi / 2, None, ALU.add)
            ts(rope0[:, 5], rope0[:, 2], PI_MAX, -PI_MAX, ALU.min, ALU.max)
            dve.drain()
            ts(rope0[:, 1], rope0[:, 0], math.pi, -TWO_PI, ALU.is_gt, ALU.mult)
            dve.drain()
            tt(rope0[:, 0], rope0[:, 0], rope0[:, 1], ALU.add)
            dve.drain()
            ts(rope0[:, 4], rope0[:, 0], PI_MAX, -PI_MAX, ALU.min, ALU.max)
            dve.drain()
            dve.nop().then_inc(rope_arg, 1)
            for c in range(2):
                stt(inv_n[:, c], iota[:, 0:16], 1.0, inv_n[:, c], ALU.add, ALU.min)
            dve.drain()
            nc.vector.reciprocal(inv_n[:], inv_n[:])
            ts(past[:, 0:7], iota[:, 1:8], float(SLOTS), None, ALU.mult)
            nc.vector.memset(ovf_f[:], 0.0)
            dve.drain()
            dve.nop().then_inc(init_dve, 1)
            dve.wait_ge(sin_ready, 1)

            with dve.Fori(0, DEPTH) as l:
                dve.wait_ge(gains_in, (l + 1) * 2 * 16)
                for i in range(NM):
                    for h in range(2):
                        bank = full(dve, l, ("memT", i, h))
                        g = gains[:, 3, 4 * h:4 * h + 4].unsqueeze(2).to_broadcast([P, 4, P])
                        tt(hmT[:, 4 * h:4 * h + 4, i * P:(i + 1) * P], bank.rearrange("p (c m) -> p c m", c=4), g,
                           ALU.mult).then_inc(freed(("memT", i, h)), 1)
                        signal("hmT_ready")
                stream_rstd(l, 0)
                dve.wait_ge(S["mem_ssq"], done(l, "mem_ssq", 1))
                mean_eps(stat[:, 0:NM], mem_s[:, 0], D)
                rsqrt(mem_s[:, 1], stat[:, 0:NM], NM)
                signal("mem_rstd")
                for t in range(NT):
                    transposed(l, 0, t, 0)
                dve.wait_ge(S["kx_squared"], done(l, "kx_squared", NM))
                for i in range(NM):
                    nc.vector.tensor_reduce(stat[:, 8 + 4 * i:12 + 4 * i].unsqueeze(2),
                                            sqC[:, i, 0:GW].rearrange("p (h d) -> p h d", h=4), AX_X, ALU.add)
                dve.drain()
                mean_eps(stat[:, 0:8], stat[:, 8:16], HD)
                rsqrt(stat[:, 16:24], stat[:, 0:8], 8)
                for i in range(NM):
                    ts(stat[:, 16 + 4 * i:20 + 4 * i], stat[:, 16 + 4 * i:20 + 4 * i], mem_s[:, 1, i:i + 1], None,
                       ALU.mult)
                dve.drain()
                for i in range(NM):
                    bank = full(dve, l, ("kvx", i))
                    r = stat[:, 16 + 4 * i:20 + 4 * i].unsqueeze(2).to_broadcast([P, 4, HD])
                    tt(knx[:, i].rearrange("p (h d) -> p h d", h=4), bank[:, 0:GW].rearrange("p (h d) -> p h d", h=4),
                       r, ALU.mult).then_inc(freed(("kvx", i)), 1)
                    signal("kx_ready")
                for t in range(NT):
                    dve.wait_ge(S["uC_copied"], done(l, "uC_copied", t + 1))
                    nc.vector.tensor_reduce(rC[:, t, 0:6].unsqueeze(2),
                                            sqC[:, t % 2].rearrange("p (h d) -> p h d", h=6), AX_X, ALU.add)
                    signal("uC_reduced")
                mean_eps(stat[:, 0:24].rearrange("p (t h) -> p t h", t=NT), rC[:, :, 0:6], HD)
                rsqrt(stat6[:], stat[:, 0:24], 24)
                s6 = stat6[:].rearrange("p (t h) -> p t h", t=NT)
                ts(s6[:, :, 0:4], s6[:, :, 0:4], HD ** -0.5, None, ALU.mult)
                dve.drain()
                for t in range(NT):
                    r = s6[:, t].unsqueeze(2).to_broadcast([P, 6, HD])
                    v = qkC[:, t].rearrange("p (h d) -> p h d", h=6)
                    tt(v, v, r, ALU.mult)
                    signal("qC_ready")
                dve.wait_ge(params_in, (l + 1) * PARAM_DMAS * 16)
                tt(pool_s[:, 2:4], pool_s[:, 0:2], g_out[:, 0:2], ALU.mult)
                nc.vector.memset(g_qk[HD:QK, 0:2], 1.0)
                for table, i in ((rope_q, 0), (rope_k, 1)):
                    g1 = g_rope[:, i, 0:16].unsqueeze(1).to_broadcast([P, NT, 16])
                    g2 = g_rope[:, i, 16:32].unsqueeze(1).to_broadcast([P, NT, 16])
                    tt(table[:, :, 0, 0:16], cossin[:, 0], g1, ALU.mult)
                    tt(table[:, :, 0, 16:32], cossin[:, 0], g2, ALU.mult)
                    stt(table[:, :, 1, 0:16], cossin[:, 1], -1.0, g2, ALU.mult, ALU.mult)
                    tt(table[:, :, 1, 16:32], cossin[:, 1], g1, ALU.mult)
                dve.drain()
                def rotate(dst, src, table, heads, tmp):
                    shape = [P, heads, ROPE]
                    c = table[:, 0].unsqueeze(1).to_broadcast(shape)
                    s1 = table[:, 1, 0:16].unsqueeze(1).to_broadcast([P, heads, 16])
                    s2 = table[:, 1, 16:32].unsqueeze(1).to_broadcast([P, heads, 16])
                    tt(tmp[:, :, 0:16], src[:, :, 16:32], s1, ALU.mult)
                    tt(tmp[:, :, 16:32], src[:, :, 0:16], s2, ALU.mult)
                    dve.drain()
                    tt(dst, src, c, ALU.mult)
                    dve.drain()
                    tt(dst, dst, tmp, ALU.add)
                tt(krot[:, :, 0:16], kr[:, :, 16:32], rope_k[:, :, 1, 0:16], ALU.mult)
                tt(krot[:, :, 16:32], kr[:, :, 0:16], rope_k[:, :, 1, 16:32], ALU.mult)
                dve.drain()
                tt(kr[:], kr[:], rope_k[:, :, 0], ALU.mult)
                dve.drain()
                tt(krot[:], krot[:], kr[:], ALU.add)
                for m in range(3):
                    bank = emptied(dve, l, ("A", m))
                    ts(cqT[:, m], bank, g_cq[:, m:m + 1], None, ALU.mult).then_inc(freed(("A", m)), 1)
                    signal("cqT_ready")
                bank = full(dve, l, ("stA",))
                v = bank[:, 0:2 * NT].rearrange("p (t j) -> p t j", j=2)
                st = stat[:, 0:8].rearrange("p (t j) -> p t j", j=2)
                mean_eps(st[:, :, 0], v[:, :, 0], QR)
                ts(st[:, :, 1], v[:, :, 1], 1.0 / KVR, EPS, ALU.mult, ALU.add).then_inc(freed(("stA",)), 1)
                rsqrt(flat(sA), stat[:, 0:8], 8)
                signal("sA_ready")
                for m in range(2):
                    dve.wait_ge(S["u_ready"], done(l, "u_ready", m + 1))
                    src, spare, width = U0, [U1, U2], 1
                    wins = []
                    for k in range(2 * m + 2):
                        dst = spare[k % 2]
                        rows = slice(0, P) if k < 2 * m + 1 else slice(HALF, P)
                        lo = 2 * width - 1
                        tt(dst[rows, lo:528], src[rows, lo:528], src[rows, lo - width:528 - width], ALU.add)
                        dve.drain()
                        wins.append(dst)
                        src, width = dst, 2 * width
                    for rows, win in ((slice(0, HALF), wins[-2]), (slice(HALF, P), wins[-1])):
                        stt(yT[rows, 2 + m, 16:SEQ], win[rows, 32:528], inv_w[rows, m:m + 1], U0[rows, 32:528],
                            ALU.mult, ALU.subtract)
                        tt(yT[rows, 2 + m, 0:16], win[rows, 16:32], inv_n[rows, m], ALU.mult)
                    dve.drain()
                    tt(yT[:, 2 + m, 0:16], yT[:, 2 + m, 0:16], U0[:, 16:32], ALU.subtract)
                    dve.drain()
                    dve.nop().then_inc(S["u_free"], 1)
                    dve.nop().then_inc(S["pooled_ready"], 1)
                for t in range(NT):
                    dve.wait_ge(S["qkA_copied"], done(l, "qkA_copied", t + 1))
                    nc.vector.tensor_reduce(ssqA[:, t, 0:4].unsqueeze(2),
                                            sqY[:, 0:384].rearrange("p (h d) -> p h d", h=4), AX_X, ALU.add)
                    nc.vector.tensor_reduce(ssqA[:, t, 4:8].unsqueeze(2),
                                            sqY[:, 384:640].rearrange("p (h d) -> p h d", h=4), AX_X, ALU.add)
                    signal("qkA_reduced")
                for t in range(NT):
                    bank = emptied(dve, l, ("cT", t))
                    ts(kTC[:, t * P:(t + 1) * P], bank[:, 2 * P:3 * P], g_qk[:, 3:4], None,
                       ALU.mult).then_inc(freed(("cT", t)), 1)
                    signal("cT_ready")
                for t in range(NT):
                    ts(ssqA[:, t, 4:8], ssqA[:, t, 4:8], ssq_kr[:, t:t + 1], None, ALU.add)
                dve.drain()
                mean_eps(stat[:, 0:32], flat(ssqA), QK)
                rsqrt(flat(ssqA), stat[:, 0:32], 32)
                ts(ssqA[:, :, 0:4], ssqA[:, :, 0:4], QK ** -0.5, None, ALU.mult)
                dve.drain()
                for t in range(NT):
                    q, k, kr_ = qkA[:, t, 0:4], qkA[:, t, 4:8, 0:NOPE], qkA[:, t, 4:8, NOPE:QK]
                    tt(q, q, ssqA[:, t, 0:4].unsqueeze(2).to_broadcast([P, 4, QK]), ALU.mult)
                    tt(k, k, ssqA[:, t, 4:8].unsqueeze(2).to_broadcast([P, 4, NOPE]), ALU.mult)
                    tt(kr_, krot[:, t].unsqueeze(1).to_broadcast([P, 4, ROPE]),
                       ssqA[:, t, 4:8].unsqueeze(2).to_broadcast([P, 4, ROPE]), ALU.mult)
                    dve.drain()
                    rotate(q[:, :, NOPE:QK], q[:, :, NOPE:QK], rope_q[:, t], 4, rope_t[:])
                    signal("qkA_ready")

                def conv_in(i, name):
                    dve.wait_ge(S["c_ready"], done(l, "c_ready", i + 1))
                    bank = full(dve, l, name)
                    nc.vector.memset(U1[:, 0:2], 0.0)
                    tt(U1[:, 2:514], bank, U0[:, 0:SEQ], ALU.mult).then_inc(freed(name), 1)
                    signal("z_done")
                    if i > 0:
                        dve.wait_ge(S["sqY_ready"], done(l, "sqY_ready", 2 + i))
                    ts(U2[:, 0:SEQ], U1[:, 0:SEQ], conv_w[:, 0, i:i + 1], conv_b[:, i:i + 1], ALU.mult, ALU.add)
                    for k in (1, 2):
                        dve.drain()
                        stt(U2[:, 0:SEQ], U1[:, k:k + SEQ], conv_w[:, k, i:i + 1], U2[:, 0:SEQ], ALU.mult, ALU.add)
                    dve.drain()

                def conv_gate(i, name):
                    bank = full(dve, l, name)
                    tt(U2[:, 0:SEQ], bank, U2[:, 0:SEQ], ALU.mult).then_inc(freed(name), 1)
                    signal("yD_ready")
                    ts(yT[:, 2 + i], U2[:, 0:SEQ], g_out[:, 2 + i:3 + i], None, ALU.mult)
                    signal("yT_ready")

                def pool_out(m):
                    bank = emptied(dve, l, ("pool", m))
                    ts(yT[:, m], bank, pool_s[:, 2 + m:3 + m], None, ALU.mult).then_inc(freed(("pool", m)), 1)
                    signal("yT_ready")

                def key_transposed(t):
                    bank = full(dve, l, ("kAT", t))
                    ts(kTA[0:QK, :, t * P:(t + 1) * P], bank[0:QK].rearrange("p (h m) -> p h m", h=4),
                       g_qk[0:QK, 1:2], None, ALU.mult).then_inc(freed(("kAT", t)), 1)
                    signal("qkAT_ready")

                conv_in(0, ("D", 1))
                pool_out(0)
                pool_out(1)
                evacuate_stat(l, 0)
                evacuate_stat(l, 1)
                conv_gate(0, ("D", 2))
                key_transposed(0)
                key_transposed(1)
                key_transposed(2)
                key_transposed(3)
                conv_in(1, ("D", 4))
                evacuate_stat(l, 2)
                conv_gate(1, ("D", 5))
                evacuate_stat(l, 3)
                attend(l, units, 0)

                evacuate_stat(l, 5)
                dve.drain()
                v = ssqY[:].rearrange("p (g m) t -> p g m t", m=2)
                tt(v[:, :, 0], v[:, :, 0], v[:, :, 1], ALU.add)
                dve.drain()
                mean_eps(stat[:, 0:16].rearrange("p (g t) -> p g t", g=NG), v[:, :, 0], GW)
                rsqrt(flat(rstdY), stat[:, 0:16], 16)
                for t in range(NT):
                    for g in MIX_ORDER:
                        for h in range(2):
                            bank = full(dve, l, ("mix", t, g, h))
                            xh = X[:, t, h * 512:(h + 1) * 512]
                            stt(xh, bank, rstdY[:, g, t:t + 1], xh, ALU.mult, ALU.add
                                ).then_inc(freed(("mix", t, g, h)), 1)
                        dve.drain()
                    dve.nop().then_inc(S["x_updated"], 1)
                    if t > 0:
                        transposed(l, 1, t - 1, 1)
                transposed(l, 1, NT - 1, 1)
                stream_rstd(l, 1)

                for t in range(NT):
                    dve.wait_ge(S["qx_copied"], done(l, "qx_copied", t + 1))
                    nc.vector.tensor_reduce(rC[:, t, 0:4].unsqueeze(2),
                                            sqx[:, t % 2].rearrange("p (h d) -> p h d", h=4), AX_X, ALU.add)
                    signal("qx_reduced")
                mean_eps(stat[:, 0:16].rearrange("p (t h) -> p t h", t=NT), rC[:, :, 0:4], HD)
                rsqrt(stat[:, 16:32], stat[:, 0:16], 16)
                ts(stat[:, 16:32], stat[:, 16:32], HD ** -0.5, None, ALU.mult)
                dve.drain()
                tt(q_scale[:], stat[:, 16:32].rearrange("p (t h) -> p t h", t=NT),
                   rstd_x[:].unsqueeze(2).to_broadcast([P, NT, 4]), ALU.mult)
                dve.drain()
                attend(l, cross, len(units))
                for t in range(NT):
                    for h in range(2):
                        bank = full(dve, l, ("wo", t, h))
                        xh = X[:, t, h * 512:(h + 1) * 512]
                        tt(xh, bank, xh, ALU.add).then_inc(freed(("wo", t, h)), 1)
                    signal("x_updated")
                    if t > 0:
                        transposed(l, 2, t - 1, 2)
                transposed(l, 2, NT - 1, 2)
                stream_rstd(l, 2)
                def r32(i):
                    return rt[:, i].rearrange("p (t e) -> p t e", t=NT)

                def r4(i):
                    return rt[:, i, 0:16].rearrange("p (t e) -> p t e", t=NT)

                def r1(i):
                    return rt[:, i, 0:NT].unsqueeze(2)
                bank = full(dve, l, ("route",))
                lg = bank[:, 0:36 * NT].rearrange("p (t e) -> p t e", t=NT)
                tt(r4(0), lg[:, :, 0:NG], rstd_x[:].unsqueeze(2).to_broadcast([P, NT, NG]), ALU.mult)
                tt(r32(1), lg[:, :, NG:36], rstd_x[:].unsqueeze(2).to_broadcast([P, NT, NE]), ALU.mult
                   ).then_inc(freed(("route",)), 1)
                dve.drain()
                tt(r4(0), r4(0), b_rt[:, 0:NG].unsqueeze(1).to_broadcast([P, NT, NG]), ALU.add)
                tt(r32(1), r32(1), b_rt[:, NG:36].unsqueeze(1).to_broadcast([P, NT, NE]), ALU.add)
                dve.drain()
                nc.vector.tensor_reduce(r1(2), r4(0), AX_X, ALU.max)
                dve.drain()
                argmax_first(r4(0), NG, r1(2), r4(3), r4(4))
                ts(r4(5), r4(3), -1.0, BIG, ALU.add, ALU.mult)
                dve.drain()
                tt(r32(1).rearrange("p t (g e) -> p t g e", g=NG), r32(1).rearrange("p t (g e) -> p t g e", g=NG),
                   r4(5).unsqueeze(3).to_broadcast([P, NT, NG, EPG]), ALU.add)
                dve.drain()
                nc.vector.tensor_reduce(r1(6), r32(1), AX_X, ALU.max)
                dve.drain()
                argmax_first(r32(1), NE, r1(6), r32(7), r32(10))
                stt(r32(1), r32(7), -2.0 * BIG, r32(1), ALU.mult, ALU.add)
                dve.drain()
                nc.vector.tensor_reduce(r1(9), r32(1), AX_X, ALU.max)
                dve.drain()
                argmax_first(r32(1), NE, r1(9), r32(8), r32(10))
                tt(M16[:], r32(7), r32(8), ALU.add)
                signal("M_ready")
                tt(rt[:, 11, 0:NT], rt[:, 9, 0:NT], rt[:, 6, 0:NT], ALU.subtract)
                tt(r4(10), r4(0), r1(2).to_broadcast([P, NT, NG]), ALU.subtract)
                signal("exp_arg")
                bank = full(dve, l, ("rank",))
                counts = bank[:, NT * NE:NT * NE + NE]
                over = Gx[:, 0:NE * 7].rearrange("p (e k) -> p e k", k=7)
                tt(over, counts.unsqueeze(2).to_broadcast([P, NE, 7]),
                   past[:, 0:7].unsqueeze(1).to_broadcast([P, NE, 7]), ALU.is_gt)
                dve.drain()
                nc.vector.tensor_reduce(rt[:, 0, 0:NE].unsqueeze(2), over, AX_X, ALU.add)
                nc.vector.memset(rt[:, 2, 0:NE], 0.0)
                dve.drain()
                nc.vector.tensor_tensor_scan(rt[:, 3, 0:NE], rt[:, 0, 0:NE], rt[:, 2, 0:NE], 0.0, ALU.add, ALU.add)
                dve.drain()
                tt(rt[:, 2, 0:NE], rt[:, 3, 0:NE], rt[:, 0, 0:NE], ALU.subtract)
                rank = bank[:, 0:NT * NE].rearrange("p (t e) -> p t e", t=NT)
                past_e = rt[:, 4, 0:NE]
                dve.drain()
                stt(past_e, rt[:, 2, 0:NE], float(NE - 1), iota[:, 0:NE], ALU.add, ALU.subtract)
                ts(r32(9), rank, float(SLOTS), None, ALU.is_ge)
                dve.drain()
                tt(r32(9), r32(9), past_e.unsqueeze(1).to_broadcast([P, NT, NE]), ALU.mult)
                dve.drain()
                tt(r32(9), r32(9), iota[:, 0:NE].unsqueeze(1).to_broadcast([P, NT, NE]), ALU.add)
                dve.drain()
                stt(r32(9), r32(9), float(SLOTS), rank, ALU.mult, ALU.add)
                dve.drain()
                both = rt[:, 13:15].rearrange("p k (t e) -> p k t e", t=NT)
                tt(both, rt[:, 7:9].rearrange("p k (t e) -> p k t e", t=NT),
                   r32(9).unsqueeze(1).to_broadcast([P, 2, NT, NE]), ALU.mult)
                dve.drain()
                nc.vector.tensor_reduce(srel[:].unsqueeze(3), both, AX_X, ALU.add)
                dve.drain()
                dve.nop().then_inc(freed(("rank",)), 1)

                def overflow_tiles():
                    tt(ovf_f[:, 1:2], ovf_f[:, 1:2], ovf_f[:, 0:1], ALU.add)
                    over = Gx[:, 0:NE * OVF].rearrange("p (q e) -> p q e", q=OVF)
                    dve.drain()
                    tt(over, rt[:, 3, 0:NE].unsqueeze(1).to_broadcast([P, OVF, NE]),
                       iota[:, 0:OVF].unsqueeze(2).to_broadcast([P, OVF, NE]), ALU.is_le)
                    nc.vector.tensor_copy(ovf_f[:, 0:1], rt[:, 3, NE - 1:NE])
                    dve.drain()
                    nc.vector.tensor_reduce(ovf_f[:, 2:2 + OVF].unsqueeze(2), over, AX_X, ALU.add)
                    dve.drain()
                    ts(ovf_f[:, 2:2 + OVF], ovf_f[:, 2:2 + OVF], float(NE - 1), None, ALU.min)
                    dve.drain()
                    nc.vector.tensor_copy(ovf[:], ovf_f[:])
                    signal("route_ready")

                def token_weights():
                    dve.wait_ge(S["exp_done"], done(l, "exp_done", 1))
                    nc.vector.tensor_reduce(r1(12), rt[:, 10, 0:NT * NG].rearrange("p (t g) -> p t g", t=NT),
                                            AX_X, ALU.add)
                    ts(rt[:, 13, 0:NT], rt[:, 11, 0:NT], 1.0, None, ALU.add)
                    dve.drain()
                    tt(rt[:, 12, 0:NT], rt[:, 12, 0:NT], rt[:, 13, 0:NT], ALU.mult)
                    dve.drain()
                    nc.vector.reciprocal(wk[:, 0], rt[:, 12, 0:NT])
                    dve.drain()
                    tt(wk[:, 1], wk[:, 0], rt[:, 11, 0:NT], ALU.mult)
                    dve.drain()
                    tt(W_te[:], r32(7), wk[:, 0].unsqueeze(2).to_broadcast([P, NT, NE]), ALU.mult)
                    tt(r32(13), r32(8), wk[:, 1].unsqueeze(2).to_broadcast([P, NT, NE]), ALU.mult)
                    dve.drain()
                    tt(W_te[:], W_te[:], r32(13), ALU.add)
                    signal("W_ready")

                def one_hot(p, who):
                    if who == "next":
                        mfull(dve, l, *p)
                    for t in range(NT):
                        ts(Gx[:, t * P:(t + 1) * P], iota[:, 0:P], srel[:, 0, t:t + 1], None, ALU.is_equal)
                    dve.drain()
                    for t in range(NT):
                        stt(G[:, t], iota[:, 0:P], srel[:, 1, t:t + 1], Gx[:, t * P:(t + 1) * P],
                            ALU.is_equal, ALU.add)
                    dve.drain()
                    ts(srel[:], srel[:], -float(P), None, ALU.add)
                    signal("G_ready")

                def gathered_gain(p, who, h):
                    bank = mfull(dve, l, p, ("xgT", who, h))
                    g = gains[:, 2, 4 * h:4 * h + 4].unsqueeze(2).to_broadcast([P, 4, P])
                    tt(xgT[:, 4 * h:4 * h + 4], bank.rearrange("p (c m) -> p c m", c=4), g,
                       ALU.mult).then_inc(mfreed(("xgT", who, h)), 1)
                    signal("xgT_ready")

                def slot_weights(bank, column, parity, free):
                    nc.vector.tensor_copy(ws[0:HALF, parity:parity + 1], bank[0:HALF, column:column + 1])
                    nc.vector.tensor_copy(ws[HALF:P, parity:parity + 1], bank[HALF:P, column + 1:column + 2]
                                          ).then_inc(free, 1)
                    signal("ws_ready")

                def bring_back(p, what, which):
                    for n in which:
                        bank = mfull(dve, l, p, (what, n))
                        xh = X[:, n // 2, (n % 2) * 512:(n % 2 + 1) * 512]
                        tt(xh, bank, xh, ALU.add).then_inc(mfreed((what, n)), 1)

                def step_(p, parity, ahead, back, before=None):
                    if ahead:
                        one_hot(before, "next")
                    dve.wait_ge(S["silu_ready"], mdone(l, p, "silu_ready", 1))
                    bank = ps[:, step.job[("gu",)][0], :]
                    tt(hh[:], bank[:, FF:2 * FF], silu[:], ALU.mult).then_inc(mfreed(("gu",)), 1)
                    signal("hh_ready")
                    if back:
                        bring_back(p, "comb", range(3))
                    if ahead:
                        bank = memptied(dve, l, p, ("hhT",))
                        slot_weights(bank, 2 * P, 1 - parity, mfreed(("hhT",)))
                    if back:
                        bring_back(p, "comb", (3, 4))
                    if ahead:
                        gathered_gain(p, "next", 0)
                        gathered_gain(p, "next", 1)
                    if back:
                        bring_back(p, "comb", range(5, 8))
                    for h in range(2):
                        dve.wait_ge(S["yhi_ready"], mdone(l, p, "yhi_ready", h + 1))
                        bank = ps[:, step.job["down", h][0], :]
                        c = slice(h * 512, (h + 1) * 512)
                        stt(ylo[:, parity, c], bank, ws[:, parity:parity + 1], yhi[:, parity, c].bitcast(F32),
                            ALU.mult, ALU.subtract).then_inc(mfreed(("down", h)), 1)
                        signal("ylo_ready")

                one_hot(None, "first")
                overflow_tiles()
                token_weights()
                for h in range(2):
                    gathered_gain(0, "first", h)
                slot_weights(mfull(dve, l, 0, ("wslot", "first")), 0, 0, mfreed(("wslot", "first")))
                step_(0, 0, True, False, (0, ("GT", "first")))
                with dve.Fori(0, PAIRS // 2 - 1) as i:
                    for k in range(2):
                        step_(2 * i + 1 + k, 1 - k, True, True, (2 * i + 1 + k, ("GT", "before")))
                step_(PAIRS - 1, 1, False, True)
                dve.drain()
                bring_back(PAIRS - 1, "last comb", range(8))

                n_ovf = dve.value_load(ovf[0:1, 0:1], min_val=0, max_val=OVF - 1)
                before = dve.value_load(ovf[0:1, 1:2], min_val=0, max_val=DEPTH * OVF)
                with dve.If(n_ovf > 0):
                    with dve.Fori(0, n_ovf) as q:
                        tile = before + q

                        def tile_step():
                            dve.drain()
                            dve.nop().then_inc(ovf_dve, 1)
                        dve.drain()
                        for t in range(NT):
                            io = iota[:, 0:SLOTS]
                            ts(Gx[:, 0:SLOTS], io, srel[:, 0, t:t + 1], None, ALU.is_equal)
                            ts(Gx[:, SLOTS:2 * SLOTS], io, srel[:, 1, t:t + 1], None, ALU.is_equal)
                            dve.drain()
                            tt(Gq[:, t], Gx[:, 0:SLOTS], Gx[:, SLOTS:2 * SLOTS], ALU.add)
                            ts(Gx[:, 2 * SLOTS:3 * SLOTS], Gx[:, 0:SLOTS], wk[:, 0, t:t + 1], None, ALU.mult)
                            dve.drain()
                            stt(Gw[:, t], Gx[:, SLOTS:2 * SLOTS], wk[:, 1, t:t + 1], Gx[:, 2 * SLOTS:3 * SLOTS],
                                ALU.mult, ALU.add)
                            dve.drain()
                        ts(srel[:], srel[:], -float(SLOTS), None, ALU.add)
                        tile_step()
                        dve.wait_ge(ovf_pe, tile * OVF_PE + 1)
                        g = gains[:, 2].unsqueeze(2).to_broadcast([P, KD, SLOTS])
                        tt(xgq[:], ps[:, 0, :].rearrange("p (c s) -> p c s", c=KD), g, ALU.mult)
                        dve.wait_ge(ovf_pe, tile * OVF_PE + 2)
                        nc.vector.tensor_copy(Wq[0:SLOTS], ps[0:SLOTS, 1, :])
                        tile_step()
                        nc.vector.tensor_copy(wsq[0:SLOTS], ps[0:SLOTS, 2, 0:1])
                        tile_step()
                        dve.wait_ge(ovf_act, tile * OVF_ACT + 1)
                        tt(hh[0:SLOTS], ps[0:SLOTS, 4, FF:2 * FF], silu[0:SLOTS], ALU.mult)
                        tile_step()
                        dve.wait_ge(ovf_pe, tile * OVF_PE + 4)
                        nc.vector.tensor_copy(hhT[:, :, 0:SLOTS], ps[:, 5, 0:2 * SLOTS].rearrange("p (c s) -> p c s", c=2))
                        tile_step()
                        dve.wait_ge(ovf_act, tile * OVF_ACT + 2)
                        for h in range(2):
                            c = slice(h * 512, (h + 1) * 512)
                            stt(ylo[0:SLOTS, 1, c], ps[0:SLOTS, 6 + h, :], wsq[0:SLOTS], yhi[0:SLOTS, 0, c].bitcast(F32),
                                ALU.mult, ALU.subtract)
                        tile_step()
                        for part in range(2):
                            dve.wait_ge(ovf_pe, tile * OVF_PE + 6 + part)
                            for n in range(4 * part, 4 * part + 4):
                                xh = X[:, n // 2, (n % 2) * 512:(n % 2 + 1) * 512]
                                tt(xh, ps[:, n % 4, :], xh, ALU.add)
                            tile_step()
                signal("layer_done")

        @block.tensor
        def _(pe):
            mm = nc.tensor.matmul
            opened = []

            def bank_of(l, name):
                opened.append(name)
                bank, _, before = dense.job[name]
                pe.wait_ge(bank_free[bank], l * dense.free[bank] + before + 1)
                return ps[:, bank, :]

            def filled(name):
                return bank_full[dense.job[name][0]]

            def mbank_of(l, p, name):
                bank, _, before = mjob(l, p, name)
                pe.wait_ge(moe_free[bank], before + 1)
                return ps[:, bank, :]

            def mfilled(name):
                return moe_full[(step if name in step.job else head if name in head.job else tail).job[name][0]]

            def flip(out_, in_):
                k = in_.shape[0]
                return nc.tensor.transpose(out_, in_, ident[0:k, 0:k])

            def transpose_tile(l, s, t):
                if s == 0:
                    pe.wait_ge(S["xn_ready"], done(l, "xn_ready", t + 1))
                    tile = xn[:, t % 2]
                else:
                    pe.wait_ge(S["x_updated"], done(l, "x_updated", NT * (s - 1) + t + 1))
                    tile = X[:, t]
                for h in range(2):
                    bank = bank_of(l, ("xT", s, t, h))
                    for c in range(4):
                        last = flip(bank[:, c * P:(c + 1) * P], tile[:, 4 * h + c::KD])
                    last.then_inc(filled(("xT", s, t, h)), 1)

            def tokens(l, name, lhs, t, w, c0, c1, n=0):
                bank = bank_of(l, name)
                for c in range(KD):
                    last = mm(bank[:, n:n + c1 - c0], lhs[:, c, t * P:(t + 1) * P], w[:, c, c0:c1],
                              start=c == 0, stop=c == KD - 1)
                last.then_inc(filled(name), 1)

            def channels(l, name, w, c0):
                bank = bank_of(l, name)
                for c in range(KD):
                    last = mm(bank, w[:, c, c0:c0 + P], hT[:, c, :], start=c == 0, stop=c == KD - 1)
                last.then_inc(filled(name), 1)

            def attend(l, list_, first):
                obank = {}
                for n in range(len(list_) + 5):
                    if n < len(list_):
                        kind, pair, t, nk = list_[n]
                        L = nk * P
                        q = slice(t * P, (t + 1) * P)
                        for h in range(2):
                            bank = bank_of(l, ("S", list_[n], h))
                            if kind == "mla":
                                head = 2 * pair + h
                                lhs, rhs = qTA[0:QK, head, q], kTA[0:QK, head, 0:L]
                            elif kind == "swa":
                                rows = slice(h * HD, (h + 1) * HD)
                                lhs, rhs = qTC[rows, pair, q], kTC[rows, (t + 1) * P - L:(t + 1) * P]
                            else:
                                rows = slice(h * HD, (h + 1) * HD)
                                lhs, rhs = qTx[rows, pair, q], kTx[rows, pair, 0:L]
                            last = mm(bank[:, 0:L], lhs, rhs, start=True, stop=kind == "xa")
                            if kind == "swa" and nk == 2:
                                mm(bank[:, 0:P], ident16[:], before16[:], start=False, stop=False)
                            if kind != "xa":
                                last = mm(bank[:, L - P:L], ident16[:], causal16[:], start=False, stop=True)
                            last.then_inc(filled(("S", list_[n], h)), 1)
                    if 2 <= n <= len(list_) + 1:
                        nk = list_[n - 2][3]
                        pe.wait_ge(S["pn_ready"], done(l, "pn_ready", first + n - 1))
                        for h in range(2):
                            bank = bank_of(l, ("T", list_[n - 2], h))
                            for j in range(nk):
                                last = flip(bank[:, j * P:(j + 1) * P], Pr[:, (n - 2) % 4, h, j * P:(j + 1) * P])
                            last.then_inc(filled(("T", list_[n - 2], h)), 1)
                    if 3 <= n <= len(list_) + 2:
                        kind, pair, t, nk = list_[n - 3]
                        for h in range(2):
                            emptied(pe, l, ("T", list_[n - 3], h))
                        if t == 0:
                            obank = bank_of(l, ("O", kind, pair))
                        for h in range(2):
                            for j in range(nk):
                                if kind == "mla":
                                    head = 2 * pair + h
                                    v = vA[:, j, head * HD:(head + 1) * HD]
                                elif kind == "swa":
                                    v = vC[:, t + 1 - nk + j, h * HD:(h + 1) * HD]
                                else:
                                    head = 2 * pair + h
                                    v = vX[:, j, head * HD:(head + 1) * HD]
                                last = mm(obank[h * HD:(h + 1) * HD, t * P:(t + 1) * P], v,
                                          PT[:, (n - 1) % 2, h, j * P:(j + 1) * P], start=j == 0, stop=j == nk - 1)
                        if t == NT - 1:
                            last.then_inc(filled(("O", kind, pair)), 1)
                    if pair_statistics(list_, n - 5):
                        c = stat_of(list_[n - 5])
                        sum_channels(l, c, {6: 5, 7: 6, 4: 7}[c], sqO[:, list_[n - 5][1]])

            def sum_channels(l, c, n, sq):
                pe.wait_ge(S["sqY_ready"], done(l, "sqY_ready", n))
                bank = bank_of(l, ("stY", c))
                for t in range(NT):
                    last = mm(bank[:, t:t + 1], sq[:, t * P:(t + 1) * P], ones[:, 0:1], start=True, stop=True)
                last.then_inc(filled(("stY", c)), 1)

            pe.wait_ge(init_pool, 1)
            with pe.Fori(0, DEPTH) as l:
                pe.wait_ge(S["layer_done"], l + 1)
                for i in range(NM):
                    pe.wait_ge(mem_in, (l + 1) * 16)
                    for h in range(2):
                        bank = bank_of(l, ("memT", i, h))
                        for c in range(4):
                            last = flip(bank[:, c * P:(c + 1) * P], memx[:, i, 4 * h + c::KD])
                        last.then_inc(filled(("memT", i, h)), 1)
                ring0_wait(pe, l, 1)
                for i in range(NM):
                    pe.wait_ge(S["hmT_ready"], done(l, "hmT_ready", 2 * i + 2))
                    tokens(l, ("kvx", i), hmT, i, ring0, 0, 512)
                for t in range(NT):
                    transpose_tile(l, 0, t)
                ring1_wait(pe, l, 2)
                for t in range(NT):
                    pe.wait_ge(S["hT_ready"], done(l, "hT_ready", 2 * t + 2))
                    tokens(l, ("uC", t, 0), hT, t, ring1, 0, ROPE + GW)
                    tokens(l, ("uC", t, 1), hT, t, ring1, ROPE + GW, 544)
                for i in range(NM):
                    pe.wait_ge(S["kx_ready"], done(l, "kx_ready", i + 1))
                    bank = bank_of(l, ("kxT", i))
                    for c in range(2):
                        last = flip(bank[:, c * P:(c + 1) * P], knx[:, i, c * P:(c + 1) * P])
                    last.then_inc(filled(("kxT", i)), 1)
                ring0_wait(pe, l, 2)
                for m in range(3):
                    channels(l, ("A", m), ring0, m * P)
                pe.wait_ge(S["sqA_ready"], done(l, "sqA_ready", 3))
                bank = bank_of(l, ("stA",))
                for t in range(NT):
                    q = slice(t * P, (t + 1) * P)
                    mm(bank[:, 2 * t:2 * t + 1], sqA[:, 0, q], ones[:, 0:1], start=True, stop=False)
                    mm(bank[:, 2 * t:2 * t + 1], sqA[:, 1, q], ones[:, 0:1], start=False, stop=True)
                    last = mm(bank[:, 2 * t + 1:2 * t + 2], sqA[:, 2, q], ones[:, 0:1], start=True, stop=True)
                last.then_inc(filled(("stA",)), 1)
                ring1_wait(pe, l, 4)
                for m in range(2):
                    channels(l, ("B", m), ring1, m * P)
                pe.wait_ge(S["cqT_ready"], done(l, "cqT_ready", 3))
                pe.wait_ge(params_in, (l + 1) * PARAM_DMAS * 16)
                for t in range(NT):
                    q = slice(t * P, (t + 1) * P)
                    bank = bank_of(l, ("qA", t))
                    mm(bank[:, 0:384], cqT[:, 0, q], w_uq[:, 0, :], start=True, stop=False)
                    mm(bank[:, 0:384], cqT[:, 1, q], w_uq[:, 1, :], start=False, stop=True
                       ).then_inc(filled(("qA", t)), 1)
                    bank = bank_of(l, ("kvA", t))
                    mm(bank, cqT[:, 2, q], w_ukv[:], start=True, stop=True).then_inc(filled(("kvA", t)), 1)
                for t in range(NT):
                    pe.wait_ge(S["qC_ready"], done(l, "qC_ready", t + 1))
                    bank = bank_of(l, ("cT", t))
                    for c in range(3):
                        last = flip(bank[:, c * P:(c + 1) * P], qkC[:, t, c * P:(c + 1) * P])
                    last.then_inc(filled(("cT", t)), 1)

                def pool_map(m):
                    pe.wait_ge(S["pooled_ready"], done(l, "pooled_ready", m + 1))
                    bank = bank_of(l, ("pool", m))
                    mm(bank, pool_w[:, m, :], yT[:, 2 + m, :], start=True, stop=True
                       ).then_inc(filled(("pool", m)), 1)

                def heads_transposed(t):
                    pe.wait_ge(S["qkA_ready"], done(l, "qkA_ready", t + 1))
                    bank = bank_of(l, ("qAT", t))
                    for h in range(4):
                        last = flip(bank[0:QK, h * P:(h + 1) * P], qkA[:, t, h])
                    last.then_inc(filled(("qAT", t)), 1)
                    bank = bank_of(l, ("kAT", t))
                    for h in range(4):
                        last = flip(bank[0:QK, h * P:(h + 1) * P], qkA[:, t, 4 + h])
                    last.then_inc(filled(("kAT", t)), 1)

                channels(l, ("D", 0), ring1, GW)
                pool_map(0)
                ring0_wait(pe, l, 4)
                channels(l, ("D", 1), ring0, 0)
                pool_map(1)
                sum_channels(l, 0, 1, sqY)
                channels(l, ("D", 2), ring0, GW)
                sum_channels(l, 1, 2, sqY)
                heads_transposed(0)
                heads_transposed(1)
                channels(l, ("D", 3), ring1, GW + P)
                channels(l, ("D", 4), ring0, P)
                heads_transposed(2)
                heads_transposed(3)
                sum_channels(l, 2, 3, sqY)
                channels(l, ("D", 5), ring0, GW + P)
                sum_channels(l, 3, 4, sqY)
                pe.wait_ge(S["cT_ready"], done(l, "cT_ready", 2 * NT))
                pe.wait_ge(S["qkAT_ready"], done(l, "qkAT_ready", 2 * NT))
                attend(l, units, 0)

                ring0_wait(pe, l, 9)
                ring1_wait(pe, l, 9)
                for t in range(NT):
                    for k, g in enumerate(MIX_ORDER):
                        if t == 0:
                            pe.wait_ge(S["yT_ready"], done(l, "yT_ready", 2 * k + 2))
                        for h in range(2):
                            bank = bank_of(l, ("mix", t, g, h))
                            w = (ring1, ring0)[h]
                            for j in range(2):
                                c = 2 * g + j
                                last = mm(bank, yT[:, c, t * P:(t + 1) * P], w[:, c, 0:512], start=j == 0, stop=j == 1)
                            last.then_inc(filled(("mix", t, g, h)), 1)
                        if t == 0 and k == 1:
                            sum_channels(l, 5, 8, sqO[:, 1])
                    if t > 0:
                        transpose_tile(l, 1, t - 1)
                pe.wait_ge(w_qx_in, (l + 1) * 16)
                for t in range(NT):
                    if t == 1:
                        transpose_tile(l, 1, NT - 1)
                    pe.wait_ge(S["hT_ready"], done(l, "hT_ready", 2 * NT + 2 * t + 2))
                    tokens(l, ("qx", t), hT, t, w_qx, 0, GW)
                for t in range(NT):
                    pe.wait_ge(S["qx_ready"], done(l, "qx_ready", t + 1))
                    bank = bank_of(l, ("qxT", t))
                    for c in range(2):
                        last = flip(bank[:, c * P:(c + 1) * P], qx[:, t, c * P:(c + 1) * P])
                    last.then_inc(filled(("qxT", t)), 1)
                pe.wait_ge(S["xa_kv_ready"], done(l, "xa_kv_ready", 2 * NM))
                pe.wait_ge(S["qxT_ready"], done(l, "qxT_ready", NT))
                attend(l, cross, len(units))
                pe.wait_ge(S["oTx_ready"], done(l, "oTx_ready", 2))
                ring1_wait(pe, l, 11)
                for t in range(NT):
                    for h in range(2):
                        bank = bank_of(l, ("wo", t, h))
                        for c in range(2):
                            r = 4 * c + 2 * h
                            last = mm(bank, oTx[:, c, t * P:(t + 1) * P], ring1[:, r:r + 2, 272:528],
                                      start=c == 0, stop=c == 1)
                        last.then_inc(filled(("wo", t, h)), 1)
                    if t > 0:
                        transpose_tile(l, 2, t - 1)

                bank = bank_of(l, ("route",))
                for t in range(NT):
                    if t == 2:
                        transpose_tile(l, 2, NT - 1)
                    pe.wait_ge(S["hT_ready"], done(l, "hT_ready", 4 * NT + 2 * t + 2))
                    for c in range(KD):
                        last = mm(bank[:, 36 * t:36 * (t + 1)], hT[:, c, t * P:(t + 1) * P], w_rt[:, c, :],
                                  start=c == 0, stop=c == KD - 1)
                last.then_inc(filled(("route",)), 1)
                pe.wait_ge(S["M_ready"], done(l, "M_ready", 1))
                bank = bank_of(l, ("rank",))
                for t in range(NT):
                    for j in range(t + 1):
                        mm(bank[:, t * NE:(t + 1) * NE], (earlier16 if j == t else ones16)[:], M16[:, j, :],
                           start=j == 0, stop=j == t)
                for j in range(NT):
                    last = mm(bank[:, NT * NE:(NT + 1) * NE], ones16[:], M16[:, j, :], start=j == 0, stop=j == NT - 1)
                last.then_inc(filled(("rank",)), 1)
                wait_apart(pe, S["xhi_ready"], done(l, "xhi_ready", NT))
                wait_apart(pe, S["xlo_ready"], done(l, "xlo_ready", 1))

                def gather(p, who, h):
                    bank = mbank_of(l, p, ("gather", who, h))
                    for t in range(NT):
                        for part in (xhi, xlo):
                            rhs = part[:, t].rearrange("p (j c) -> p c j", c=KD)[:, 4 * h:4 * h + 4, :]
                            last = mm(bank, G[:, t], rhs, start=t == 0 and part is xhi,
                                      stop=t == NT - 1 and part is xlo)
                    last.then_inc(mfilled(("gather", who, h)), 1)

                def gathered_transposed(p, who, h, pair, read=None):
                    pe.wait_ge(S["xg_ready"], mdone(l, pair, "xg_ready", h + 1))
                    bank = mbank_of(l, p, ("xgT", who, h))
                    for c in range(4):
                        last = flip(bank[:, c * P:(c + 1) * P], xg[:, (4 * h + c) * P:(4 * h + c + 1) * P])
                        if c == 0 and read is not None:
                            last.then_inc(read, 1)
                    last.then_inc(mfilled(("xgT", who, h)), 1)

                def slot_weights(bank, column, pair):
                    for t in range(NT):
                        last = mm(bank[:, column:column + 2], G[:, t].bitcast(F32),
                                  W_te[:, t, bass.ds(2 * pair, 2)], start=t == 0, stop=t == NT - 1)
                    return last

                def one_hot_transposed(p, who):
                    bank = mbank_of(l, p, ("GT", who))
                    for t in range(NT):
                        last = flip(bank[:, t * P:(t + 1) * P], G[:, t].bitcast(F32))
                    last.then_inc(mfilled(("GT", who)), 1)

                def bring_back(p, what, which, parity):
                    for n in which:
                        bank = mbank_of(l, p, (what, n))
                        w = Wt[:, parity, (n // 2) * P:(n // 2 + 1) * P]
                        c = slice((n % 2) * 512, (n % 2 + 1) * 512)
                        mm(bank, w, yhi[:, parity, c], start=True, stop=False)
                        mm(bank, w, ylo[:, parity, c], start=False, stop=True).then_inc(mfilled((what, n)), 1)

                def step_(p, parity, ahead, back):
                    pe.wait_ge(S["xgT_ready"], mdone(l, p, "xgT_ready", 2))
                    bank = mbank_of(l, p, ("gu",))
                    for j in range(2):
                        pe.wait_ge(slot_in[2 * parity + j], uses_before(l, p, parity) * 48 + 48)
                    for c in range(KD):
                        for j in range(2):
                            r = slice(j * SLOTS, (j + 1) * SLOTS)
                            last = mm(bank[r], xgT[:, c, r], wgu[2 * parity + j][:, :, c, :],
                                      start=c == 0, stop=c == KD - 1)
                    last.then_inc(mfilled(("gu",)), 1)
                    if ahead:
                        pe.wait_ge(S["G_ready"], mdone(l, p, "G_ready", 2))
                        gather(p, "next", 0)
                    if back:
                        pe.wait_ge(S["ylo_ready"], mdone(l, p, "ylo_ready", 0))
                        pe.wait_ge(S["Wt_ready"], mdone(l, p, "Wt_ready", 0))
                        bring_back(p, "comb", range(3), 1 - parity)
                    pe.wait_ge(S["hh_ready"], mdone(l, p, "hh_ready", 1))
                    bank = mbank_of(l, p, ("hhT",))
                    for c in range(2):
                        last = flip(bank[:, c * P:(c + 1) * P], hh[:, c::2])
                    if ahead:
                        last = slot_weights(bank, 2 * P, p + 1)
                    last.then_inc(mfilled(("hhT",)), 1)
                    if ahead:
                        gather(p, "next", 1)
                    if back:
                        bring_back(p, "comb", (3, 4), 1 - parity)
                    if ahead:
                        gathered_transposed(p, "next", 0, p + 1)
                    pe.wait_ge(S["hhT_ready"], mdone(l, p, "hhT_ready", 1))
                    for h in range(2):
                        bank = mbank_of(l, p, ("down", h))
                        for c in range(2):
                            for j in range(2):
                                r = slice(j * SLOTS, (j + 1) * SLOTS)
                                last = mm(bank[r], hhT[:, c, r], wdn[2 * parity + j][:, c, h * 512:(h + 1) * 512],
                                          start=c == 0, stop=c == 1)
                        last.then_inc(mfilled(("down", h)), 1)
                    if ahead:
                        gathered_transposed(p, "next", 1, p + 1, slots_read[parity])
                    if back:
                        bring_back(p, "comb", range(5, 8), 1 - parity)
                    if ahead:
                        one_hot_transposed(p, "next")

                def uses_before(l, p, parity):
                    return l * (PAIRS // 2) + (p // 2 if isinstance(p, int) else i + (1 if parity == 0 else 0))

                pe.wait_ge(S["G_ready"], mdone(l, 0, "G_ready", 1))
                gather(0, "first", 0)
                gather(0, "first", 1)
                gathered_transposed(0, "first", 0, 0)
                gathered_transposed(0, "first", 1, 0)
                pe.wait_ge(S["route_ready"], l + 2)
                one_hot_transposed(0, "first")
                pe.wait_ge(S["W_ready"], done(l, "W_ready", 1))
                bank = mbank_of(l, 0, ("wslot", "first"))
                slot_weights(bank, 0, 0).then_inc(mfilled(("wslot", "first")), 1)
                step_(0, 0, True, False)
                with pe.Fori(0, PAIRS // 2 - 1) as i:
                    step_(2 * i + 1, 1, True, True)
                    step_(2 * i + 2, 0, True, True)
                pe.drain()
                pe.nop().then_inc(S["gathered"], 1)
                step_(PAIRS - 1, 1, False, True)
                pe.drain()
                pe.nop().then_inc(slots_read[1], 1)
                pe.wait_ge(S["ylo_ready"], mdone(l, PAIRS, "ylo_ready", 0))
                pe.wait_ge(S["Wt_ready"], mdone(l, PAIRS, "Wt_ready", 0))
                bring_back(PAIRS - 1, "last comb", range(8), 1)

                wait_apart(pe, S["route_ready"], l + 2)
                n_ovf = pe.value_load(ovf[0:1, 0:1], min_val=0, max_val=OVF - 1)
                before = pe.value_load(ovf[0:1, 1:2], min_val=0, max_val=DEPTH * OVF)
                with pe.If(n_ovf > 0):
                    with pe.Fori(0, n_ovf) as q:
                        tile = before + q
                        pe.wait_ge(ovf_dve, tile * OVF_DVE + 1)
                        for c in range(KD):
                            for t in range(NT):
                                o_ = ps[:, 0, c * SLOTS:(c + 1) * SLOTS]
                                mm(o_, xhi[:, t, c::KD], Gq[:, t], start=t == 0, stop=False)
                                last = mm(o_, xlo[:, t, c::KD], Gq[:, t], start=False, stop=t == NT - 1)
                        last.then_inc(ovf_pe, 1)
                        for t in range(NT):
                            flip(ps[0:SLOTS, 1, t * P:(t + 1) * P], Gq[:, t].bitcast(F32))
                        for t in range(NT):
                            last = mm(ps[0:SLOTS, 2, 0:1], Gw[:, t], ones[:, 0:1], start=t == 0, stop=t == NT - 1)
                        last.then_inc(ovf_pe, 1)
                        pe.wait_ge(ovf_dve, tile * OVF_DVE + 2)
                        pe.wait_ge(ovf_w, (tile + 1) * 48)
                        for c in range(KD):
                            last = mm(ps[0:SLOTS, 4, :], xgq[:, c, :], wgu[0][:, :, c, :], start=c == 0, stop=c == KD - 1)
                        last.then_inc(ovf_pe, 1)
                        wait_apart(pe, ovf_dve, tile * OVF_DVE + 4)
                        for c in range(2):
                            last = flip(ps[:, 5, c * SLOTS:(c + 1) * SLOTS], hh[0:SLOTS, c::2])
                        last.then_inc(ovf_pe, 1)
                        pe.wait_ge(ovf_dve, tile * OVF_DVE + 5)
                        for h in range(2):
                            for c in range(2):
                                last = mm(ps[0:SLOTS, 6 + h, :], hhT[:, c, 0:SLOTS], wdn[0][:, c, h * 512:(h + 1) * 512],
                                          start=c == 0, stop=c == 1)
                        last.then_inc(ovf_pe, 1)
                        pe.wait_ge(ovf_dve, tile * OVF_DVE + 6)
                        for part in range(2):
                            if part:
                                pe.wait_ge(ovf_dve, tile * OVF_DVE + 7)
                            for n in range(4 * part, 4 * part + 4):
                                w = Wq[0:SLOTS, (n // 2) * P:(n // 2 + 1) * P]
                                c = slice((n % 2) * 512, (n % 2 + 1) * 512)
                                mm(ps[:, n % 4, :], w, yhi[0:SLOTS, 0, c], start=True, stop=False)
                                last = mm(ps[:, n % 4, :], w, ylo[0:SLOTS, 1, c], start=False, stop=True)
                            last.then_inc(ovf_pe, 1)
            assert opened == dense.order, "the plan's order is the program's"


_INS = ["x", "mem", "positions", "norm_mix", "w_in", "mla_g_cq", "mla_w_uq", "mla_g_ckv", "mla_w_ukv",
        "mla_g_q", "mla_g_k", "pool_w", "pool_scale", "swa_g_q", "swa_g_k", "swa_sinks", "conv_w", "conv_b",
        "mix_out_norm", "w_mix_out", "norm_xa", "norm_mem", "xa_w_q", "xa_w_kv", "xa_g_q", "xa_g_k", "xa_w_o",
        "norm_ffn", "w_group", "b_group", "w_expert", "b_expert", "w_gate", "w_up", "w_down"]


def kernel(**inputs):
    import numpy as _np
    import concourse.bacc as _bacc
    from concourse import mybir as _mybir
    from concourse.bass_utils import run_bass_kernel_spmd as _run

    nc = _bacc.Bacc("TRN2", target_bir_lowering=False, num_devices=1)
    arrays, views = {}, {}
    for name in _INS:
        arr = _np.ascontiguousarray(inputs[name])
        arrays[f"in_{name}"] = arr
        views[name] = nc.dram_tensor(f"in_{name}", arr.shape, _mybir.dt.from_np(arr.dtype), kind="ExternalInput").ap()
    out = nc.dram_tensor("out_0", (1, SEQ, D), F32, kind="ExternalOutput").ap()
    build(nc, views, out)
    r = _run(nc, [arrays], core_ids=[0])
    return r.results[0]["out_0"]
```
